# Optimizing a Trainium2 kernel written in Bass

```python
import jax, jax.numpy as jnp
from jax import lax
import numpy as np

D_MODEL = 1024
BATCH = 1
SEQ = 256
DEPTH = 2
DEC_BATCH = 8
DEC_SEQ = 1
PAST_LEN = 2048
PAGE_SIZE = 128

HG_HEADS = 8
HG_DK = 128
HG_DV = D_MODEL // HG_HEADS
HG_QK = HG_HEADS * HG_DK
HG_V = HG_HEADS * HG_DV
CHUNK = 64
CONV_DIM = D_MODEL
CONV_W = 31
D_FF = 2816
N_EXPERTS = 8
TOP_K = 2
D_FF_EXPERT = 2816
N_DENSE = (DEPTH + 1) // 2
N_MOE = DEPTH // 2
EPS = 1e-6
IN_COLS = 2 * HG_QK + 2 * HG_V + 2 * CONV_DIM + 2 * D_MODEL
IN_SPLITS = (HG_QK, 2 * HG_QK, 2 * HG_QK + HG_V, 2 * HG_QK + 2 * HG_V,
             2 * HG_QK + 2 * HG_V + CONV_DIM, 2 * HG_QK + 2 * HG_V + 2 * CONV_DIM,
             2 * HG_QK + 2 * HG_V + 2 * CONV_DIM + D_MODEL)

kernel_name = 'hgrn2_conformer_gated_hybrid_step'

def rmsnorm(x, g):
    xf = x.astype(jnp.float32)
    y = xf * lax.rsqrt(jnp.mean(xf * xf, axis=-1, keepdims=True) + EPS)
    return (y * g.astype(jnp.float32)).astype(x.dtype)

def layernorm(x, g, b):
    xf = x.astype(jnp.float32)
    mu = jnp.mean(xf, axis=-1, keepdims=True)
    xc = xf - mu
    y = xc * lax.rsqrt(jnp.mean(xc * xc, axis=-1, keepdims=True) + EPS)
    return (y * g.astype(jnp.float32) + b.astype(jnp.float32)).astype(x.dtype)

def lower_bounds(lb_logits):
    p = jax.nn.softmax(lb_logits.astype(jnp.float32), axis=0)
    return jnp.cumsum(p, axis=0) - p[0:1]

def gla_chunked(q, k, v, logf, s0):
    B, T, H, DK = q.shape
    DV = v.shape[-1]
    C = min(CHUNK, T)
    n = -(-T // C)
    pad = n * C - T
    padw = ((0, 0), (0, pad), (0, 0), (0, 0))
    q, k, v, logf = (jnp.pad(a, padw) for a in (q, k, v, logf))
    to_chunks = lambda a: a.reshape(B, n, C, H, a.shape[-1]).transpose(1, 0, 3, 2, 4)
    qc, kc, vc, lc = to_chunks(q), to_chunks(k), to_chunks(v), to_chunks(logf)
    causal = jnp.tril(jnp.ones((C, C), dtype=bool))[:, :, None]

    def step(S, inp):
        qb, kb, vb, lb = inp
        b = jnp.cumsum(lb, axis=2)
        o_inter = jnp.einsum('bhtk,bhkv->bhtv', qb * jnp.exp(b), S)
        diff = b[:, :, :, None, :] - b[:, :, None, :, :]
        decay = jnp.where(causal, jnp.exp(jnp.where(causal, diff, 0.0)), 0.0)
        att = jnp.einsum('bhtk,bhsk,bhtsk->bhts', qb, kb, decay)
        o_intra = jnp.einsum('bhts,bhsv->bhtv', att, vb)
        b_last = b[:, :, -1]
        S_new = jnp.exp(b_last)[..., None] * S + jnp.einsum(
            'bhsk,bhsv->bhkv', kb * jnp.exp(b_last[:, :, None, :] - b), vb)
        return S_new, o_inter + o_intra

    S_fin, o = lax.scan(step, s0, (qc, kc, vc, lc))
    o = o.transpose(1, 0, 3, 2, 4).reshape(B, n * C, H, DV)[:, :T]
    return o, S_fin

def causal_depthwise_conv(u, buf, w, bias):
    full = jnp.concatenate([buf.astype(u.dtype), u], axis=1)
    y = lax.conv_general_dilated(full, w.astype(u.dtype)[:, None, :], window_strides=(1,),
                                 padding='VALID', dimension_numbers=('NWC', 'WIO', 'NWC'),
                                 feature_group_count=u.shape[-1])
    return y + bias.astype(u.dtype), full[:, -(CONV_W - 1):]

def swiglu(h, wg, wu, wd):
    return (jax.nn.silu(h @ wg) * (h @ wu)) @ wd

def moe_swiglu(h, router_w, wg, wu, wd):
    B, T, D = h.shape
    t = h.reshape(B * T, D)
    logits = (t @ router_w).astype(jnp.float32)
    top_v, top_i = lax.top_k(logits, TOP_K)
    top_w = jax.nn.softmax(top_v, axis=-1)
    combine = jnp.sum(jax.nn.one_hot(top_i, N_EXPERTS, dtype=jnp.float32) * top_w[..., None], axis=1)
    out = jnp.zeros_like(t)
    for e in range(N_EXPERTS):
        out = out + combine[:, e:e + 1].astype(t.dtype) * swiglu(t, wg[e], wu[e], wd[e])
    return out.reshape(B, T, D)

def trunk(x, c, s_hgrn, s_conv, P):
    B, T, _ = x.shape
    f32 = jnp.float32
    lb_all = lower_bounds(P['lb_logits'])
    c_act = jax.nn.silu(c)
    new_h, new_c = [], []
    for l in range(DEPTH):
        mod = (c_act @ P['ada_w'][l] + P['ada_b'][l])[:, None, :]
        sh1, sc1, g1, sh2, sc2, g2 = jnp.split(mod, 6, axis=-1)
        h = rmsnorm(x, P['norm1_g'][l]) * (1 + sc1) + sh1
        z = h @ P['w_in'][l]
        zq, zf, zi, zg, za, zb, gate_a, gate_b = jnp.split(z, IN_SPLITS, axis=-1)
        lb = lb_all[l]
        ff = zf.astype(f32)
        k = (1 - lb) * jax.nn.sigmoid(-ff)
        logf = jnp.log(lb + (1 - lb) * jax.nn.sigmoid(ff))
        q = jax.nn.silu(zq.astype(f32))
        heads = lambda a, d: a.reshape(B, T, HG_HEADS, d)
        o, s_out = gla_chunked(heads(q, HG_DK), heads(k, HG_DK), heads(zi.astype(f32), HG_DV),
                               heads(logf, HG_DK), s_hgrn[l].astype(f32))
        o = o * lax.rsqrt(jnp.mean(o * o, axis=-1, keepdims=True) + EPS)
        o = o.reshape(B, T, HG_V) * P['hg_norm_g'][l].astype(f32)
        o = o.astype(x.dtype) * jax.nn.silu(zg)
        y_a = o @ P['w_hg_out'][l]
        u = za * jax.nn.sigmoid(zb)
        v, buf = causal_depthwise_conv(u, s_conv[l], P['conv_w'][l], P['conv_b'][l])
        v = jax.nn.silu(layernorm(v, P['conv_ln_g'][l], P['conv_ln_b'][l]))
        y_b = v @ P['w_conv_out'][l]
        mixed = jax.nn.sigmoid(gate_a) * y_a + jax.nn.sigmoid(gate_b) * y_b
        x = x + g1 * (mixed @ P['w_o'][l])
        h2 = rmsnorm(x, P['norm2_g'][l]) * (1 + sc2) + sh2
        j = l // 2
        if l % 2 == 0:
            f_out = swiglu(h2, P['ffn_w_gate'][j], P['ffn_w_up'][j], P['ffn_w_down'][j])
        else:
            f_out = moe_swiglu(h2, P['router_w'][j], P['moe_w_gate'][j], P['moe_w_up'][j],
                               P['moe_w_down'][j])
        x = x + g2 * f_out
        new_h.append(s_out)
        new_c.append(buf)
    return rmsnorm(x, P['final_norm_g']), jnp.stack(new_h), jnp.stack(new_c)

def setup_inputs(seed: int = 0) -> dict:
    key = jax.random.key(seed)
    ks = iter(jax.random.split(key, 40))
    nrm = lambda shape, s: jax.random.normal(next(ks), shape, jnp.float32) * s
    D = D_MODEL
    return {
        'x_prompt': nrm((BATCH, SEQ, D), 1.0),
        'x_sample': nrm((DEC_BATCH, DEC_SEQ, D), 1.0),
        'state_hgrn': nrm((DEPTH, DEC_BATCH, HG_HEADS, HG_DK, HG_DV), 0.2),
        'state_conv': nrm((DEPTH, DEC_BATCH, CONV_W - 1, CONV_DIM), 0.5),
        'c_prompt': nrm((BATCH, D), 1.0),
        'c_sample': nrm((DEC_BATCH, D), 1.0),
        'ada_w': nrm((DEPTH, D, 6 * D), 0.5 * D ** -0.5),
        'ada_b': nrm((DEPTH, 6 * D), 0.02),
        'norm1_g': 1.0 + nrm((DEPTH, D), 0.02),
        'norm2_g': 1.0 + nrm((DEPTH, D), 0.02),
        'w_in': nrm((DEPTH, D, IN_COLS), D ** -0.5),
        'lb_logits': nrm((DEPTH, HG_QK), 0.5),
        'hg_norm_g': 1.0 + nrm((DEPTH, HG_V), 0.02),
        'w_hg_out': nrm((DEPTH, HG_V, D), HG_V ** -0.5),
        'conv_w': nrm((DEPTH, CONV_W, CONV_DIM), CONV_W ** -0.5),
        'conv_b': nrm((DEPTH, CONV_DIM), 0.02),
        'conv_ln_g': 1.0 + nrm((DEPTH, CONV_DIM), 0.02),
        'conv_ln_b': nrm((DEPTH, CONV_DIM), 0.02),
        'w_conv_out': nrm((DEPTH, CONV_DIM, D), CONV_DIM ** -0.5),
        'w_o': nrm((DEPTH, D, D), D ** -0.5),
        'ffn_w_gate': nrm((N_DENSE, D, D_FF), D ** -0.5),
        'ffn_w_up': nrm((N_DENSE, D, D_FF), D ** -0.5),
        'ffn_w_down': nrm((N_DENSE, D_FF, D), D_FF ** -0.5),
        'router_w': nrm((N_MOE, D, N_EXPERTS), D ** -0.5),
        'moe_w_gate': nrm((N_MOE, N_EXPERTS, D, D_FF_EXPERT), D ** -0.5),
        'moe_w_up': nrm((N_MOE, N_EXPERTS, D, D_FF_EXPERT), D ** -0.5),
        'moe_w_down': nrm((N_MOE, N_EXPERTS, D_FF_EXPERT, D), D_FF_EXPERT ** -0.5),
        'final_norm_g': 1.0 + nrm((D,), 0.02),
    }

def reference(x_prompt, x_sample, state_hgrn, state_conv, c_prompt, c_sample,
              ada_w, ada_b, norm1_g, norm2_g, w_in, lb_logits, hg_norm_g, w_hg_out,
              conv_w, conv_b, conv_ln_g, conv_ln_b, w_conv_out, w_o,
              ffn_w_gate, ffn_w_up, ffn_w_down, router_w, moe_w_gate, moe_w_up, moe_w_down,
              final_norm_g):
    P = {'ada_w': ada_w, 'ada_b': ada_b, 'norm1_g': norm1_g, 'norm2_g': norm2_g,
         'w_in': w_in, 'lb_logits': lb_logits, 'hg_norm_g': hg_norm_g, 'w_hg_out': w_hg_out,
         'conv_w': conv_w, 'conv_b': conv_b, 'conv_ln_g': conv_ln_g, 'conv_ln_b': conv_ln_b,
         'w_conv_out': w_conv_out, 'w_o': w_o, 'ffn_w_gate': ffn_w_gate, 'ffn_w_up': ffn_w_up,
         'ffn_w_down': ffn_w_down, 'router_w': router_w, 'moe_w_gate': moe_w_gate,
         'moe_w_up': moe_w_up, 'moe_w_down': moe_w_down, 'final_norm_g': final_norm_g}
    bp = x_prompt.shape[0]
    h0 = jnp.zeros((DEPTH, bp, HG_HEADS, HG_DK, HG_DV), jnp.float32)
    c0 = jnp.zeros((DEPTH, bp, CONV_W - 1, CONV_DIM), x_prompt.dtype)
    y_prompt, hgrn_prompt, conv_prompt = trunk(x_prompt, c_prompt, h0, c0, P)
    y_sample, hgrn_sample, conv_sample = trunk(x_sample, c_sample, state_hgrn, state_conv, P)
    return (y_prompt, y_sample, hgrn_prompt, conv_prompt, hgrn_sample, conv_sample)


_drawn_inputs = setup_inputs


def setup_inputs(seed=0):
    import zlib

    import numpy as np

    out = dict(_drawn_inputs(seed))
    spreads = {}
    factors = {'norm1_g': 2.722,
     'norm2_g': 3.441,
     'hg_norm_g': 7.69,
     'conv_b': 5.978,
     'conv_ln_g': 19.937,
     'conv_ln_b': 44.301,
     'final_norm_g': 29.056}
    for name, (base, spread) in spreads.items():
        noise = np.random.default_rng([zlib.crc32(name.encode()), seed]).standard_normal(out[name].shape)
        drawn = base * np.exp(spread * noise) if base else spread * noise
        out[name] = __import__('jax').numpy.asarray(drawn.astype(out[name].dtype))
    for name, factor in factors.items():
        out[name] = (out[name] * factor).astype(out[name].dtype)
    return out
```

```python
import concourse.bass as bass
from concourse import mybir
from contextlib import ExitStack

P = 128
D = 1024
KT = D // P
TP = 256
TS = 8
T = TP + TS
NC_TOK = 1 + TS
LAYERS = 2
HEADS = 8
CH = 128
NCH = TP // CH
HC = HEADS * NCH
CW = 31
PAST = CW - 1
FF = 2816
FT = FF // P
NE = 8
SLOT_BLOCKS = 16
SLOT_W = SLOT_BLOCKS * P
RING = 6
BANKS = 8
EPS = 1e-6
SPANS = [64, 32, 16, 8, 4, 2, 1]
REST = [(g, t) for g in ("zb", "za", "g", "ga", "gb") for t in range(KT)]
LEVEL_AFTER = {5 * n + 4: n for n in range(8)}
CAP = 128
TT = [(0, P), (P, P), (TP, TS)]
POOL_CONV = (6, 7)
DVE_CONV = tuple(t for t in range(KT) if t not in POOL_CONV)

_at = 0
PAR = {}
for _name, _n in (("ada_b", LAYERS * 48), ("n1", LAYERS * KT), ("n2", LAYERS * KT), ("lb", LAYERS * KT),
                  ("hgn", LAYERS * KT), ("cb", LAYERS * KT), ("lng", LAYERS * KT), ("lnb", LAYERS * KT),
                  ("cw", LAYERS * KT * CW), ("fin", KT), ("rw", KT * NE)):
    PAR[_name] = (_at, _n)
    _at += _n
NPAR = _at


def psum_order():
    out = [("mod", 0, 0)]
    for l in range(LAYERS):
        out.append(("n1", l))
        out += [(g, l, t) for g in ("f", "q", "i") for t in range(KT)]
        for r, (g, t) in enumerate(REST):
            out.append((g, l, t))
            if r in LEVEL_AFTER:
                out += [("att", l, LEVEL_AFTER[r], b) for b in range(4)]
        if l == 0:
            out.append(("mod", 0, 1))
        out += [("vt", l, b) for b in range(4)] + [("kt", l, b) for b in range(4)]
        out += [("s0", l, b) for b in range(2)] + [("o", l, b) for b in range(4)] + [("s1", l, b) for b in range(2)]
        out += [("ks", l, b) for b in range(2)] + [("vs", l, b) for b in range(2)]
        for h in range(HEADS + 1):
            if h < HEADS:
                out += [("kv", l, h, 0), ("kv", l, h, 1)]
            if h >= 1:
                out.append(("os", l, h - 1))
        if l == 0:
            out.append(("mod", 0, 2))
        out.append(("mu", l))
        out += [("hn", l, h) for h in range(HEADS)]
        out.append(("var", l))
        out += [(g, l, t) for g in ("ya", "yb", "wo") for t in range(KT)]
        if l == 0:
            out.append(("mod", 1, 0))
        out.append(("n2", l))
        if l == 0:
            out.append(("mod", 1, 1))
            for j in range(FT):
                out += [("fg", j), ("fu", j)]
            out += [("fd", t) for t in range(KT)]
            out.append(("mod", 1, 2))
    out += [("tok", b) for b in range(6)] + [("lg",), ("pos",)]
    return out


USE = {name: n for n, name in enumerate(psum_order())}
MOE_USE0 = len(USE)
MOE_USES = 24
STREAM_SLOTS = (LAYERS * (48 + 64 + 24) * KT + 3 * FT * KT) // SLOT_BLOCKS
MOE_SLOTS = 3 * FT * KT // SLOT_BLOCKS
DVE_STEPS = 8


def trunk_kernel(nc, x_in, c_in, par_in, stream_in, moe_in, sh_in, sc_in,
                 y_out, hp_out, cp_out, hs_out, cs_out):
    fp32, u8, u32, i32 = mybir.dt.float32, mybir.dt.uint8, mybir.dt.uint32, mybir.dt.int32
    ALU = mybir.AluOpType
    ACT = mybir.ActivationFunctionType
    AX = mybir.AxisListType.X
    ctx = ExitStack()
    with ctx:
        def sb(name, shape, dt=fp32):
            return ctx.enter_context(nc.sbuf_tensor(name, shape, dt))

        def sem(name):
            return ctx.enter_context(nc.semaphore(name))

        ring = sb("ring", [P, RING, SLOT_W])
        x = sb("x", [P, KT, T])
        h = sb("h", [P, KT, T])
        qkv = sb("qkv", [P, 3, KT, T])
        big = sb("big", [P, 6, KT, T])
        tmp = sb("tmp", [P, 3, KT * T])
        attb = sb("attb", [P, HC, P])
        s0b = sb("s0b", [P, HEADS, P])
        ubuf = sb("ubuf", [P, KT, PAST + TP])
        sconv = sb("sconv", [P, KT, TS, PAST])
        par = sb("par", [P, NPAR])
        modt = sb("modt", [P, LAYERS, 48, NC_TOK])
        sc1g = sb("sc1g", [P, KT, NC_TOK])
        cT = sb("cT", [P, KT, NC_TOK])
        ident = sb("ident", [P, P])
        ones = sb("ones", [P, P])
        masks = sb("masks", [P, 8, P], u8)
        eps_col = sb("eps_col", [P, 1])
        lbt = sb("lbt", [P, 2, LAYERS, KT])
        lsm = sb("lsm", [P, 4, KT])
        fs = sb("fs", [P, HEADS, TS])
        us = sb("us", [P, KT, TS])
        ebl = sb("ebl", [P, HEADS, NCH])
        row = sb("row", [P, 2, T])
        small = sb("small", [P, KT * TS])
        rt = sb("rt", [P, 3, 80])
        scratch = sb("scratch", [P, 1])
        small_conv = [sb(f"pool_product{n}", [P, TP])[:, :] for n in range(2)]
        flag = sb("flag", [1, 2], i32)

        Q, K, V = (qkv[:, n] for n in range(3))
        F, SBZ, SG, GA, GB, B = (big[:, n] for n in range(6))
        DEC, X0, X1 = (tmp[:, n, :] for n in range(3))
        Xb = [X0, X1]
        KTOK, VTOK = DEC, X1
        KS, VS = X0[0:TS, 0:D], X0[0:TS, D:2 * D]
        VD = [DEC[0:TS, n * 1024:(n + 1) * 1024] for n in range(2)]
        Bf = B.rearrange("p k t -> p (k t)")
        STB = [Bf[:, 0:1024], Bf[:, 1024:2048]]
        SNEW = F.rearrange("p k t -> p (k t)")[:, 0:KT * TS * PAST]
        qkv_f = qkv[:, :, :, :].rearrange("p a k t -> p (a k t)")
        HID = qkv_f[:, 0:FT * T].rearrange("p (j t) -> p j t", t=T)
        SILU = [GA.rearrange("p k t -> p (k t)")[:, n * 512:n * 512 + T] for n in range(2)]
        MHID = qkv_f[:, 0:FT * CAP].rearrange("p (j t) -> p j t", t=CAP)
        H2G = [V.rearrange("p k t -> p (k t)")[:, n * 1024:(n + 1) * 1024] for n in range(2)]
        tmp_f = tmp[:, :, :].rearrange("p a n -> p (a n)")
        H2TOK = tmp_f[:, 0:3 * D].rearrange("p (a n) -> p a n", a=3)
        SEL = [tmp_f[:, 3 * D + n * 384:3 * D + (n + 1) * 384].rearrange("p (a n) -> p a n", a=3) for n in range(2)]
        SELC = [tmp_f[:, 4 * D + n * 384:4 * D + (n + 1) * 384].rearrange("p (a n) -> p a n", a=3) for n in range(2)]
        YE = F.rearrange("p k t -> p (k t)")[:, 0:D]
        MSILU = [SBZ.rearrange("p k t -> p (k t)")[:, n * 256:(n + 1) * 256] for n in range(2)]
        SCT = [SG.rearrange("p k t -> p (k t)")[:, n * T:(n + 1) * T] for n in range(2)]
        FACC = GA
        TRI = attb[:, 0, :]
        IOTA = attb[:, 1, :]
        PSEL = sb("psel", [P, 2, NE, 3])
        CUR = sb("cur", [P, 2, 2, 3])

        banks = [ctx.enter_context(nc.psum_tensor(f"bank{n}", [P, 512], fp32)) for n in range(BANKS)]
        psum_full = sem("psum_full")
        psum_read = [sem(f"psum_read{n}") for n in range(BANKS)]
        landed = [sem(f"weights_landed{n}") for n in range(RING)]
        started = sem("slot_started")
        s_in = sem("inputs_landed")
        s_state = [sem(f"state_landed{n}") for n in range(2)]
        s_sconv = sem("sconv_landed")
        s_const = sem("constants_ready")
        s_pool = sem("pool_step")
        s_dve = sem("dve_step")
        s_act = sem("act_step")
        s_sq = sem("squares_ready")
        s_rstd = sem("roots_ready")
        s_mod = sem("modulation_ready")
        s_cact = sem("c_act_ready")
        s_lbx = sem("lb_max_ready")
        s_lbe = sem("lb_exp_ready")
        s_h = sem("h_ready")
        s_fg = sem("forget_ready")
        s_ln = sem("logf_ready")
        s_scan = sem("cumsum_ready")
        s_qv = sem("qv_ready")
        s_zb = sem("sigmoid_zb_ready")
        s_glu = sem("glu_ready")
        s_dif = sem("decay_exponent_ready")
        s_exp = sem("decay_ready")
        s_xl = sem("level_operand_ready")
        s_kq = sem("decayed_kq_ready")
        s_eb = sem("chunk_decay_ready")
        s_vt = sem("vtok_ready")
        s_kt = sem("ktok_ready")
        s_att0 = sem("att_cleared")
        s_att = sem("att_ready")
        s_s0 = sem("s0_ready")
        s_s1 = sem("s1_ready")
        s_s1out = sem("s1_stored")
        s_kvs = sem("sample_kv_ready")
        s_vd = sem("vdiag_ready")
        s_sn = sem("sample_state_ready")
        s_ssout = [sem(f"sample_state_stored{n}") for n in range(2)]
        s_o = sem("heads_out_ready")
        s_osq = sem("heads_squares_ready")
        s_hn = sem("heads_roots_ready")
        s_on = sem("gated_heads_ready")
        s_conv = sem("conv_tap")
        s_pconv = sem("pool_conv_tap")
        s_cs = sem("sample_products_ready")
        s_snew = sem("sample_conv_state_ready")
        s_csout = sem("conv_states_stored")
        s_cv = sem("conv_ready")
        s_mu = sem("mean_ready")
        s_xc = sem("centred_ready")
        s_lnn = sem("layernorm_ready")
        s_yb = sem("branch_b_ready")
        s_sgr = sem("gates_ready")
        s_mix = sem("mixed_ready")
        s_x = sem("x_ready")
        s_gsilu = sem("ffn_silu_ready")
        s_hid = sem("hidden_ready")
        s_tok = sem("h2_token_major_ready")
        s_lg = sem("logits_ready")
        s_rex = sem("router_exp_ready")
        s_sel = sem("assignment_ready")
        s_flag = sem("flag_ready")
        m_sel = sem("moe_selection_ready")
        m_h2g = sem("moe_gathered_ready")
        m_silu = sem("moe_silu_ready")
        m_hid = sem("moe_hidden_ready")
        m_sct = sem("moe_scatter_ready")
        m_y = sem("moe_y_ready")
        m_acc = sem("moe_accumulated")
        m_dve = sem("moe_dve_step")
        f_x = sem("final_x_ready")
        f_sq = sem("final_squares_ready")
        f_st = sem("final_sum_ready")
        f_rt = sem("final_root_ready")
        f_dve = sem("final_dve_step")
        f_y = sem("y_ready")
        s_done = sem("outputs_stored")

        def par_of(name, l=None):
            at, n = PAR[name]
            if l is None:
                return par[:, at:at + n]
            n //= LAYERS
            return par[:, at + l * n:at + (l + 1) * n]

        def bank(name):
            return banks[USE[name] % BANKS]

        def await_use(eng, name):
            eng.wait_ge(psum_full, USE[name] + 1)
            return bank(name)

        def freed(ins, name):
            ins.then_inc(psum_read[USE[name] % BANKS], 1)

        def levels_view(buf, m):
            v = buf[:, :, 0:TP].rearrange("p h (n a m) -> p h n a m", a=2, m=m)
            return v[:, :, :, 0, :], v[:, :, :, 1, :]

        def as_kt(flat):
            return flat.rearrange("p (k t) -> p k t", t=T)

        def bc(ap, axis, shape):
            return ap.unsqueeze(axis).broadcast_to(shape)

        block = ctx.enter_context(nc.Block())

        @block.sync
        def _(sp):
            sp.dma_start(cT[:, :, :], c_in).then_inc(s_in, 16)
            sp.dma_start(par[:, :], par_in).then_inc(s_in, 16)
            for n in range(STREAM_SLOTS):
                if n >= RING:
                    sp.wait_ge(started, n - RING + 2)
                sp.dma_start(ring[:, n % RING, :], stream_in[n]).then_inc(landed[n % RING], 16)
                if n == 0:
                    sp.dma_start(x[:, :, :], x_in).then_inc(s_in, 16)

            def expert_pair(pair, turn):
                for n in range(2 * MOE_SLOTS):
                    at = STREAM_SLOTS + n
                    sp.wait_ge(started, turn * (2 * MOE_SLOTS) + at - RING + 2)
                    sp.dma_start(ring[:, at % RING, :], moe_in[bass.ds(pair, 1), n]).then_inc(landed[at % RING], 16)

            with sp.Fori(0, NE // 2) as pair:
                expert_pair(pair, pair)
            sp.wait_ge(s_flag, 2)
            more = sp.value_load(flag[0:1, 0:1], min_val=0, max_val=1)
            with sp.If(more > 0):
                with sp.Fori(1, 3) as rnd:
                    with sp.Fori(0, NE // 2) as pair:
                        expert_pair(pair, rnd * (NE // 2) + pair)
            sp.wait_ge(f_y, 1)
            sp.dma_start(y_out, as_kt(X0)).then_inc(s_done, 16)
            sp.wait_ge(s_done, 16)
            sp.wait_ge(s_csout, 32 * LAYERS)
            sp.wait_ge(s_s1out, 16 * LAYERS)
            for n in range(2):
                sp.wait_ge(s_ssout[n], 64 * LAYERS)

        @block.tensor
        def _(pe):
            order = psum_order()
            at = {"use": 0, "block": 0}

            def mm(out, lhsT, rhs, start=True, stop=True):
                return nc.tensor.matmul(out, lhsT, rhs, start=start, stop=stop)

            def open_use(name):
                n = at["use"]
                assert order[n] == name, (order[n], name)
                at["use"] += 1
                if n >= BANKS:
                    pe.wait_ge(psum_read[n % BANKS], n // BANKS)
                return banks[n % BANKS]

            def weight_mm(out, rhs, start, stop):
                b = at["block"]
                n, w = b // SLOT_BLOCKS, b % SLOT_BLOCKS
                at["block"] += 1
                if w == 0:
                    pe.wait_ge(landed[n % RING], 16 * (n // RING + 1))
                ins = mm(out, ring[:, n % RING, w * P:(w + 1) * P], rhs, start, stop)
                if w == 0:
                    ins.then_inc(started, 1)
                return ins

            def project(name, src):
                ps = open_use(name)
                for k in range(KT):
                    ins = weight_mm(ps[:, 0:T], src[:, k, :], k == 0, k == KT - 1)
                ins.then_inc(psum_full, 1)

            def modulation(l, pair):
                ps = open_use(("mod", l, pair))
                for t in range(16):
                    for k in range(KT):
                        ins = weight_mm(ps[:, t * NC_TOK:(t + 1) * NC_TOK], cT[:, k, :], k == 0, k == KT - 1)
                ins.then_inc(psum_full, 1)

            def feature_sum(name, src):
                ps = open_use(name)
                for k in range(KT):
                    ins = mm(ps[:, 0:T], ones[:, :], src[:, k, :], k == 0, k == KT - 1)
                ins.then_inc(psum_full, 1)

            pe.wait_ge(s_const, 1)
            pe.wait_ge(s_cact, 1)
            modulation(0, 0)
            for l in range(LAYERS):
                pe.wait_ge(s_sq, 4 * l + 1)
                feature_sum(("n1", l), as_kt(X1))
                pe.wait_ge(s_h, 2 * l + 1)
                for g in ("f", "q", "i"):
                    for t in range(KT):
                        project((g, l, t), h)
                for r, (g, t) in enumerate(REST):
                    project((g, l, t), h)
                    if r not in LEVEL_AFTER:
                        continue
                    n = LEVEL_AFTER[r]
                    if n == 0:
                        pe.wait_ge(s_fg, l + 1)
                        pe.wait_ge(s_qv, l + 1)
                    else:
                        pe.wait_ge(s_xl, 7 * l + n)
                    for b in range(4):
                        ps = open_use(("att", l, n, b))
                        for s in range(4):
                            hd, c = divmod(4 * b + s, NCH)
                            tok = slice(c * CH, (c + 1) * CH)
                            a, w = (K, Q) if n == 0 else (as_kt(Xb[n % 2]), as_kt(Xb[n % 2]))
                            ins = mm(ps[:, s * P:(s + 1) * P], a[:, hd, tok], w[:, hd, tok])
                        ins.then_inc(psum_full, 1)
                if l == 0:
                    modulation(0, 1)
                for b in range(4):
                    ps = open_use(("vt", l, b))
                    for s in range(4):
                        hd, c = divmod(4 * b + s, NCH)
                        ins = nc.tensor.transpose(ps[:, s * P:(s + 1) * P], V[:, hd, c * CH:(c + 1) * CH], ident[:, :])
                    ins.then_inc(psum_full, 1)
                pe.wait_ge(s_kq, 2 * l + 1)
                for b in range(4):
                    ps = open_use(("kt", l, b))
                    for s in range(4):
                        hd, c = divmod(4 * b + s, NCH)
                        ins = nc.tensor.transpose(ps[:, s * P:(s + 1) * P], as_kt(X0)[:, hd, c * CH:(c + 1) * CH], ident[:, :])
                    ins.then_inc(psum_full, 1)
                pe.wait_ge(s_vt, l + 1)
                pe.wait_ge(s_kt, l + 1)
                for b in range(2):
                    ps = open_use(("s0", l, b))
                    for s in range(4):
                        hc = (4 * b + s) * NCH
                        ins = mm(ps[:, s * P:(s + 1) * P], KTOK[:, hc * P:(hc + 1) * P], VTOK[:, hc * P:(hc + 1) * P])
                    ins.then_inc(psum_full, 1)
                pe.wait_ge(s_att, l + 1)
                pe.wait_ge(s_s0, l + 1)
                pe.wait_ge(s_kq, 2 * l + 2)
                for b in range(4):
                    ps = open_use(("o", l, b))
                    for s in range(2):
                        hd = 2 * b + s
                        hc = hd * NCH
                        mm(ps[:, s * TP:s * TP + CH], VTOK[:, hc * P:(hc + 1) * P], attb[:, hc, :])
                        out = ps[:, s * TP + CH:(s + 1) * TP]
                        mm(out, VTOK[:, (hc + 1) * P:(hc + 2) * P], attb[:, hc + 1, :], True, False)
                        ins = mm(out, s0b[:, hd, :], Q[:, hd, CH:TP], False, True)
                    ins.then_inc(psum_full, 1)
                for b in range(2):
                    ps = open_use(("s1", l, b))
                    for s in range(4):
                        hc = (4 * b + s) * NCH + 1
                        ins = mm(ps[:, s * P:(s + 1) * P], KTOK[:, hc * P:(hc + 1) * P], VTOK[:, hc * P:(hc + 1) * P])
                    ins.then_inc(psum_full, 1)
                for name, src in (("ks", K), ("vs", V)):
                    for b in range(2):
                        ps = open_use((name, l, b))
                        for s in range(4):
                            ins = mm(ps[0:TS, s * P:(s + 1) * P], src[:, 4 * b + s, TP:T], ident[:, :])
                        ins.then_inc(psum_full, 1)
                pe.wait_ge(s_kvs, l + 1)
                for hd in range(HEADS + 1):
                    if hd < HEADS:
                        pe.wait_ge(s_vd, HEADS * l + hd + 1)
                        for half in range(2):
                            ps = open_use(("kv", l, hd, half))
                            mm(ps[:, :], KS[:, hd * P:(hd + 1) * P], VD[hd % 2][:, half * 512:(half + 1) * 512])\
                                .then_inc(psum_full, 1)
                    if hd >= 1:
                        g = hd - 1
                        ps = open_use(("os", l, g))
                        pe.wait_ge(s_sn, HEADS * l + g + 1)
                        for b in range(TS):
                            ins = mm(ps[:, b:b + 1], STB[g % 2][:, b * P:(b + 1) * P], Q[:, g, TP + b:TP + b + 1])
                        ins.then_inc(psum_full, 1)
                if l == 0:
                    modulation(0, 2)
                pe.wait_ge(s_cv, l + 1)
                feature_sum(("mu", l), SBZ)
                pe.wait_ge(s_osq, l + 1)
                for hd in range(HEADS):
                    ps = open_use(("hn", l, hd))
                    mm(ps[:, 0:T], ones[:, :], as_kt(X1)[:, hd, :]).then_inc(psum_full, 1)
                pe.wait_ge(s_sq, 4 * l + 2)
                feature_sum(("var", l), as_kt(DEC))
                pe.wait_ge(s_on, l + 1)
                for t in range(KT):
                    project(("ya", l, t), h)
                pe.wait_ge(s_yb, l + 1)
                for t in range(KT):
                    project(("yb", l, t), SBZ)
                pe.wait_ge(s_mix, l + 1)
                for t in range(KT):
                    project(("wo", l, t), GA)
                if l == 0:
                    modulation(1, 0)
                pe.wait_ge(s_sq, 4 * l + 3)
                feature_sum(("n2", l), as_kt(X1))
                if l == 0:
                    modulation(1, 1)
                pe.wait_ge(s_h, 2 * l + 2)
                if l == 0:
                    for j in range(FT):
                        project(("fg", j), h)
                        project(("fu", j), h)
                    pe.wait_ge(s_hid, FT)
                    for t in range(KT):
                        ps = open_use(("fd", t))
                        for k in range(FT):
                            ins = weight_mm(ps[:, 0:T], HID[:, k, :], k == 0, k == FT - 1)
                        ins.then_inc(psum_full, 1)
                    modulation(1, 2)
            assert at["block"] == STREAM_SLOTS * SLOT_BLOCKS

            for b in range(6):
                tt, half = divmod(b, 2)
                t0, tn = TT[tt]
                ps = open_use(("tok", b))
                for s in range(4):
                    ins = mm(ps[0:tn, s * P:(s + 1) * P], h[:, 4 * half + s, t0:t0 + tn], ident[:, :])
                ins.then_inc(psum_full, 1)
            rw = par_of("rw").rearrange("p (k e) -> p k e", e=NE)
            ps = open_use(("lg",))
            for tt, (t0, tn) in enumerate(TT):
                for k in range(KT):
                    ins = mm(ps[0:tn, tt * NE:(tt + 1) * NE], h[:, k, t0:t0 + tn], rw[:, k, :], k == 0, k == KT - 1)
            ins.then_inc(psum_full, 1)
            pe.wait_ge(s_sel, 1)
            ps = open_use(("pos",))
            for tt, (_, tn) in enumerate(TT):
                for u in range(tt + 1):
                    un = TT[u][1]
                    lhsT = TRI[0:un, 0:tn] if u == tt else ones[0:un, 0:tn]
                    mm(ps[0:tn, tt * NE:(tt + 1) * NE], lhsT, rt[0:un, u, 8:16], u == 0, u == tt)
            for u, (_, un) in enumerate(TT):
                ins = mm(ps[:, 3 * NE:4 * NE], ones[0:un, :], rt[0:un, u, 8:16], u == 0, u == 2)
            ins.then_inc(psum_full, 1)
            assert at["use"] == MOE_USE0

            def expert(turn, s):
                use, blk = [s * MOE_USES], [s * MOE_SLOTS * SLOT_BLOCKS]

                def open_moe():
                    n = MOE_USE0 + use[0]
                    use[0] += 1
                    pe.wait_ge(psum_read[n % BANKS], turn * (2 * MOE_USES // BANKS) + n // BANKS)
                    return banks[n % BANKS]

                def slot_ap(width):
                    n, w = divmod(blk[0], SLOT_BLOCKS)
                    n += STREAM_SLOTS
                    if w == 0:
                        pe.wait_ge(landed[n % RING], turn * (16 * 2 * MOE_SLOTS // RING) + 16 * (n // RING + 1))
                    ap = ring[:, n % RING, w * P:(w + width) * P]
                    blk[0] += width
                    return ap, w == 0

                pe.wait_ge(m_sel, 2 * turn + s + 1)
                for half in range(2):
                    ps = open_moe()
                    for g in range(4):
                        k = 4 * half + g
                        for tt, (_, tn) in enumerate(TT):
                            ins = mm(ps[:, g * P:(g + 1) * P], H2TOK[0:tn, tt, k * P:(k + 1) * P],
                                     SEL[s][0:tn, tt, :], tt == 0, tt == 2)
                    ins.then_inc(psum_full, 1)
                ps = open_moe()
                for tt, (t0, tn) in enumerate(TT):
                    ins = mm(ps[:, t0:t0 + tn], SELC[s][0:tn, tt, :], ident[0:tn, 0:tn])
                ins.then_inc(psum_full, 1)
                pe.wait_ge(m_h2g, 2 * turn + s + 1)
                for j in range(FT // 2):
                    ps = open_moe()
                    for piece in range(4):
                        for k in range(KT):
                            w, first = slot_ap(1)
                            ins = mm(ps[:, piece * P:(piece + 1) * P], w, H2G[s][:, k * P:(k + 1) * P], k == 0, k == KT - 1)
                            if first:
                                ins.then_inc(started, 1)
                    ins.then_inc(psum_full, 1)
                halves = [open_moe(), open_moe()]
                for k in range(FT):
                    if k % 2 == 0:
                        pe.wait_ge(m_hid, (2 * turn + s) * (FT // 2) + k // 2 + 1)
                    for half in range(2):
                        w, first = slot_ap(4)
                        ins = mm(halves[half][:, :], MHID[:, k, :], w, k == 0, k == FT - 1)
                        if first:
                            ins.then_inc(started, 1)
                        if k == FT - 1:
                            ins.then_inc(psum_full, 1)
                pe.wait_ge(m_sct, 2 * turn + s + 1)
                for t in range(KT):
                    if t % 4 == 0:
                        pe.wait_ge(m_y, 2 * (2 * turn + s) + t // 4 + 1)
                    ps = open_moe()
                    mm(ps[:, 0:T], YE[:, t * P:(t + 1) * P], SCT[s]).then_inc(psum_full, 1)
                assert use[0] == (s + 1) * MOE_USES

            with pe.Fori(0, NE // 2) as pair:
                for s in range(2):
                    expert(pair, s)
            pe.wait_ge(s_flag, 2)
            more = pe.value_load(flag[0:1, 0:1], min_val=0, max_val=1)
            with pe.If(more > 0):
                with pe.Fori(1, 3) as rnd:
                    with pe.Fori(0, NE // 2) as pair:
                        for s in range(2):
                            expert(rnd * (NE // 2) + pair, s)
            pe.wait_ge(f_sq, 1)
            for k in range(KT):
                ins = mm(banks[0][:, 0:T], ones[:, :], as_kt(X1)[:, k, :], k == 0, k == KT - 1)
            ins.then_inc(f_st, 1)

        @block.scalar
        def _(act):
            steps = [0]

            def link(ins):
                steps[0] += 1
                ins.then_inc(s_act, 1)
                act.wait_ge(s_act, steps[0])

            def root(name, out, scale):
                ps = await_use(act, name)
                freed(act.activation(out, ps[:, 0:T], ACT.Sqrt, bias=eps_col[:, 0:1], scale=scale), name)

            act.wait_ge(s_in, 48)
            act.activation(cT[:, :, :], cT[:, :, :], ACT.Silu).then_inc(s_cact, 1)
            act.activation(as_kt(X1), x[:, :, :], ACT.Square).then_inc(s_sq, 1)
            act.wait_ge(s_lbx, 1)
            act.activation(lsm[:, 1:3, :], lsm[:, 1:3, :], ACT.Exp).then_inc(s_lbe, 1)
            act.wait_ge(s_const, 1)
            for l in range(LAYERS):
                if l > 0:
                    act.wait_ge(s_x, 2 * l)
                    act.activation(as_kt(X1), x[:, :, :], ACT.Square).then_inc(s_sq, 1)
                root(("n1", l), row[:, 0, :], 1.0 / D)
                act.wait_ge(psum_read[USE[("n1", l)] % BANKS], USE[("n1", l)] // BANKS + 1)
                act.sem_inc(s_rstd, 1)
                if l > 0:
                    act.wait_ge(s_csout, 32 * l)
                    for n in range(2):
                        act.wait_ge(s_ssout[n], 64 * l)
                for t in range(KT):
                    ps = await_use(act, ("f", l, t))
                    act.activation(F[:, t, :], ps[:, 0:T], ACT.Sigmoid).then_inc(s_act, 1)
                    steps[0] += 1
                    freed(act.activation(K[:, t, :], ps[:, 0:T], ACT.Sigmoid, scale=-1.0), ("f", l, t))
                act.wait_ge(s_fg, l + 1)
                act.activation(B[:, :, 0:TP], F[:, :, 0:TP], ACT.Ln).then_inc(s_ln, 1)
                for t in range(KT):
                    ps = await_use(act, ("q", l, t))
                    freed(act.activation(Q[:, t, :], ps[:, 0:T], ACT.Silu), ("q", l, t))
                for t in range(KT):
                    ps = await_use(act, ("i", l, t))
                    freed(act.activation(V[:, t, :], ps[:, 0:T], ACT.Copy), ("i", l, t))
                act.wait_ge(psum_read[USE[("i", l, KT - 1)] % BANKS], USE[("i", l, KT - 1)] // BANKS + 1)
                act.sem_inc(s_qv, 1)
                if l > 0:
                    act.wait_ge(s_x, 2 * l)

                def level_exp(n):
                    act.wait_ge(s_dif, 8 * l + n)
                    act.activation(as_kt(DEC)[:, :, 0:TP], as_kt(DEC)[:, :, 0:TP], ACT.Exp).then_inc(s_exp, 1)

                level_exp(1)
                for r, (g, t) in enumerate(REST):
                    name = (g, l, t)
                    if g != "za":
                        dst, func = {"zb": (SBZ, ACT.Sigmoid), "g": (SG, ACT.Silu), "ga": (GA, ACT.Sigmoid),
                                     "gb": (GB, ACT.Sigmoid)}[g]
                        ps = await_use(act, name)
                        ins = act.activation(dst[:, t, :], ps[:, 0:T], func)
                        freed(ins, name)
                        if g == "zb":
                            act.wait_ge(psum_read[USE[name] % BANKS], USE[name] // BANKS + 1)
                            act.sem_inc(s_zb, 1)
                    if r in LEVEL_AFTER and 1 <= LEVEL_AFTER[r] < 7:
                        level_exp(LEVEL_AFTER[r] + 1)
                name = ("gb", l, KT - 1)
                act.wait_ge(psum_read[USE[name] % BANKS], USE[name] // BANKS + 1)
                act.sem_inc(s_sgr, 1)
                level_exp(8)
                act.activation(ebl[:, :, :], B[:, :, CH - 1:TP:CH], ACT.Exp).then_inc(s_act, 1)
                steps[0] += 1
                act.wait_ge(s_act, steps[0])
                act.activation(B[:, :, CH:TP], B[:, :, CH:TP], ACT.Exp).then_inc(s_eb, 1)
                for b in range(4):
                    if b == 0:
                        act.wait_ge(s_att, l + 1)
                    ps = await_use(act, ("vt", l, b))
                    ins = act.activation(VTOK[:, b * 512:(b + 1) * 512], ps[:, :], ACT.Copy)
                    freed(ins, ("vt", l, b))
                for b in range(4):
                    if b == 0:
                        act.wait_ge(s_kq, 2 * l + 1)
                    ps = await_use(act, ("kt", l, b))
                    ins = act.activation(KTOK[:, b * 512:(b + 1) * 512], ps[:, :], ACT.Copy)
                    freed(ins, ("kt", l, b))
                name = ("kt", l, 3)
                act.wait_ge(psum_read[USE[name] % BANKS], USE[name] // BANKS + 1)
                act.sem_inc(s_vt, 1)
                act.sem_inc(s_kt, 1)
                for b in range(2):
                    if b == 0 and l > 0:
                        act.wait_ge(s_s1out, 16 * l)
                    ps = await_use(act, ("s0", l, b))
                    ins = act.activation(s0b[:, 4 * b:4 * b + 4, :], ps[:, :].rearrange("p (a n) -> p a n", a=4), ACT.Copy)
                    freed(ins, ("s0", l, b))
                name = ("s0", l, 1)
                act.wait_ge(psum_read[USE[name] % BANKS], USE[name] // BANKS + 1)
                act.sem_inc(s_s0, 1)
                act.wait_ge(s_kq, 2 * l + 2)
                for hd in range(2):
                    act.dma_start(STB[hd], sh_in[l, hd].rearrange("p b n -> p (b n)")).then_inc(s_state[hd], 16)
                for b in range(4):
                    ps = await_use(act, ("o", l, b))
                    ins = act.activation(h[:, 2 * b:2 * b + 2, 0:TP], ps[:, :].rearrange("p (a n) -> p a n", a=2), ACT.Copy)
                    freed(ins, ("o", l, b))
                for name, dst in (("ks", KS), ("vs", VS)):
                    for b in range(2):
                        ps = await_use(act, (name, l, b))
                        ins = act.activation(dst[:, b * 512:(b + 1) * 512], ps[0:TS, :], ACT.Copy)
                        freed(ins, (name, l, b))
                name = ("vs", l, 1)
                act.wait_ge(psum_read[USE[name] % BANKS], USE[name] // BANKS + 1)
                act.sem_inc(s_kvs, 1)
                act.wait_ge(s_s1, l + 1)
                act.dma_start(hp_out[l], s0b[:, :, :]).then_inc(s_s1out, 16)
                for hd in range(HEADS):
                    act.wait_ge(s_sn, HEADS * l + hd + 1)
                    st = hd % 2
                    act.dma_start(hs_out[l, hd].rearrange("p b n -> p (b n)"), STB[st]).then_inc(s_ssout[st], 16)
                    ps = await_use(act, ("os", l, hd))
                    ins = act.activation(h[:, hd, TP:T], ps[:, 0:TS], ACT.Copy)
                    freed(ins, ("os", l, hd))
                    if hd + 2 < HEADS:
                        act.wait_ge(s_ssout[st], 16 * ((HEADS * l + hd) // 2 + 1))
                        act.dma_start(STB[st], sh_in[l, hd + 2].rearrange("p b n -> p (b n)")).then_inc(s_state[st], 16)
                name = ("os", l, HEADS - 1)
                act.wait_ge(psum_read[USE[name] % BANKS], USE[name] // BANKS + 1)
                act.activation(as_kt(X1), h[:, :, :], ACT.Square).then_inc(s_osq, 1)
                ps = await_use(act, ("mu", l))
                freed(act.activation(row[:, 0, :], ps[:, 0:T], ACT.Copy, scale=1.0 / D), ("mu", l))
                act.wait_ge(psum_read[USE[("mu", l)] % BANKS], USE[("mu", l)] // BANKS + 1)
                act.sem_inc(s_mu, 1)
                for hd in range(HEADS):
                    root(("hn", l, hd), as_kt(X0)[:, hd, :], 1.0 / P)
                name = ("hn", l, HEADS - 1)
                act.wait_ge(psum_read[USE[name] % BANKS], USE[name] // BANKS + 1)
                act.sem_inc(s_hn, 1)
                act.wait_ge(s_xc, l + 1)
                act.activation(as_kt(DEC), SBZ, ACT.Square).then_inc(s_sq, 1)
                root(("var", l), row[:, 1, :], 1.0 / D)
                act.wait_ge(psum_read[USE[("var", l)] % BANKS], USE[("var", l)] // BANKS + 1)
                act.sem_inc(s_rstd, 1)
                act.wait_ge(s_lnn, l + 1)
                for t in range(KT):
                    ins = act.activation(SBZ[:, t, :], SBZ[:, t, :], ACT.Silu, bias=par_of("lnb", l)[:, t:t + 1],
                                         scale=par_of("lng", l)[:, t:t + 1])
                ins.then_inc(s_yb, 1)
                act.wait_ge(s_x, 2 * l + 1)
                act.activation(as_kt(X1), x[:, :, :], ACT.Square).then_inc(s_sq, 1)
                root(("n2", l), row[:, 0, :], 1.0 / D)
                act.wait_ge(psum_read[USE[("n2", l)] % BANKS], USE[("n2", l)] // BANKS + 1)
                act.sem_inc(s_rstd, 1)
                act.sem_inc(s_sq, 1)
                if l == 0:
                    for j in range(FT):
                        if j >= 2:
                            act.wait_ge(s_hid, j - 1)
                        ps = await_use(act, ("fg", j))
                        ins = act.activation(SILU[j % 2], ps[:, 0:T], ACT.Silu)
                        freed(ins, ("fg", j))
                        act.wait_ge(psum_read[USE[("fg", j)] % BANKS], USE[("fg", j)] // BANKS + 1)
                        act.sem_inc(s_gsilu, 1)
            for b in range(6):
                tt, half = divmod(b, 2)
                tn = TT[tt][1]
                ps = await_use(act, ("tok", b))
                ins = act.activation(H2TOK[0:tn, tt, half * 512:(half + 1) * 512], ps[0:tn, :], ACT.Copy)
                freed(ins, ("tok", b))
            name = ("tok", 5)
            act.wait_ge(psum_read[USE[name] % BANKS], USE[name] // BANKS + 1)
            act.sem_inc(s_tok, 1)
            act.wait_ge(s_lg, 1)
            act.activation(rt[:, :, 36:37], rt[:, :, 36:37], ACT.Exp).then_inc(s_rex, 1)

            def expert(turn, s):
                base = MOE_USE0 + s * MOE_USES

                def full(n):
                    act.wait_ge(psum_full, turn * (2 * MOE_USES) + base + n + 1)
                    return banks[(base + n) % BANKS]

                for half in range(2):
                    ps = full(half)
                    act.activation(H2G[s][:, half * 512:(half + 1) * 512], ps[:, :], ACT.Copy)\
                        .then_inc(psum_read[(base + half) % BANKS], 1)
                ps = full(2)
                act.activation(SCT[s], ps[:, 0:T], ACT.Copy).then_inc(psum_read[(base + 2) % BANKS], 1)
                act.wait_ge(psum_read[(base + 2) % BANKS],
                            turn * (2 * MOE_USES // BANKS) + (base + 2) // BANKS + 1)
                act.sem_inc(m_h2g, 1)
                act.sem_inc(m_sct, 1)
                for j in range(FT // 2):
                    ps = full(3 + j)
                    if s > 0 or j >= 2:
                        act.wait_ge(m_hid, (2 * turn + s) * (FT // 2) + j - 1)
                    gates = ps[:, :].rearrange("p (a b n) -> p a b n", a=2, b=2)[:, :, 0, :]
                    act.activation(MSILU[j % 2].rearrange("p (a n) -> p a n", a=2), gates, ACT.Silu).then_inc(m_silu, 1)
                for half in range(2):
                    n = 3 + FT // 2 + half
                    ps = full(n)
                    act.activation(YE[:, half * 512:(half + 1) * 512], ps[:, :], ACT.Copy)\
                        .then_inc(psum_read[(base + n) % BANKS], 1)
                    act.wait_ge(psum_read[(base + n) % BANKS],
                                turn * (2 * MOE_USES // BANKS) + (base + n) // BANKS + 1)
                    act.sem_inc(m_y, 1)

            act.wait_ge(s_csout, 32 * LAYERS)
            with act.Fori(0, NE // 2) as pair:
                for s in range(2):
                    expert(pair, s)
            act.wait_ge(s_flag, 2)
            more = act.value_load(flag[0:1, 0:1], min_val=0, max_val=1)
            with act.If(more > 0):
                with act.Fori(1, 3) as rnd:
                    with act.Fori(0, NE // 2) as pair:
                        for s in range(2):
                            expert(rnd * (NE // 2) + pair, s)
            act.wait_ge(f_x, 1)
            act.activation(as_kt(X1), x[:, :, :], ACT.Square).then_inc(f_sq, 1)
            act.wait_ge(f_st, 1)
            act.activation(row[:, 0, :], banks[0][:, 0:T], ACT.Sqrt, bias=eps_col[:, 0:1], scale=1.0 / D).then_inc(f_rt, 1)

        @block.gpsimd
        def _(pool):
            steps = [0]

            def link(ins):
                steps[0] += 1
                ins.then_inc(s_pool, 1)
                pool.wait_ge(s_pool, steps[0])

            pool.memset(eps_col[:, :], EPS)
            pool.memset(ones[:, :], 1.0)
            link(pool.memset(ident[:, :], 0.0))
            link(pool.affine_select(out=ident[:, :], in_=ident[:, :], compare_op=ALU.not_equal, fill=1.0,
                                    base=0, pattern=[[-1, P]], channel_multiplier=1))
            mf = as_kt(X0)[:, :, 0:P]
            link(pool.memset(mf, 0.0))
            link(pool.tensor_copy(mf[:, 0, :], ident[:, :]))
            for n, m in enumerate(SPANS):
                second = mf[:, n + 1, :].rearrange("p (n a m) -> p n a m", a=2, m=m)[:, :, 1, :]
                link(pool.memset(second, 1.0))
                blocks = P // (2 * m)
                link(pool.affine_select(out=second, in_=second, compare_op=ALU.is_ge, fill=0.0, base=0,
                                        pattern=[[-2 * m, blocks], [0, m]], channel_multiplier=1))
                link(pool.affine_select(out=second, in_=second, compare_op=ALU.is_ge, fill=0.0, base=m - 1,
                                        pattern=[[2 * m, blocks], [0, m]], channel_multiplier=-1))
            link(pool.tensor_copy(masks[:, :, :], mf))
            link(pool.memset(ubuf[:, :, 0:PAST], 0.0))
            pool.memset(ubuf[:, 0, 0:1], 0.0).then_inc(s_const, 1)
            taps = [0]
            for l in range(LAYERS):
                if l > 0:
                    pool.wait_ge(s_csout, 32 * l)
                    pool.wait_ge(s_cv, l)
                pool.dma_start(sconv[:, :, :, :], sc_in[l]).then_inc(s_sconv, 16)
                if l > 0:
                    pool.wait_ge(s_on, l)
                pool.memset(attb[:, :, :], 0.0).then_inc(s_att0, 1)
                pool.wait_ge(s_glu, l + 1)
                cw = par_of("cw", l).rearrange("p (k j) -> p k j", j=CW)
                pool.dma_start(cp_out[l], ubuf[:, :, TP:TP + PAST]).then_inc(s_csout, 16)
                pool.wait_ge(s_sconv, 16 * (l + 1))
                snew = SNEW.rearrange("p (k b j) -> p k b j", b=TS, j=PAST)
                sv = sconv[:, :, :, :].rearrange("p k b j -> p (k b) j")
                snv = SNEW.rearrange("p (n j) -> p n j", j=PAST)
                pool.tensor_copy(snv[:, :, 0:PAST - 1], sv[:, :, 1:PAST])
                link(pool.tensor_copy(snew[:, :, :, PAST - 1], us[:, :, :]))
                pool.dma_start(cs_out[l], SNEW).then_inc(s_csout, 16)
                pool.tensor_tensor(sconv[:, :, :, :], sconv[:, :, :, :],
                                   bc(cw[:, :, 0:PAST], 2, [P, KT, TS, PAST]), ALU.mult).then_inc(s_cs, 1)
                for j in range(CW):
                    for n, t in enumerate(POOL_CONV):
                        win = ubuf[:, t, j:j + TP]
                        acc = SBZ[:, t, 0:TP]
                        if j == 0:
                            pool.tensor_scalar(acc, win, cw[:, t, 0:1], par_of("cb", l)[:, t:t + 1], ALU.mult, ALU.add)\
                                .then_inc(s_pconv, 1)
                            taps[0] += 1
                            continue
                        prod = small_conv[n]
                        if taps[0] > 0:
                            pool.wait_ge(s_pconv, taps[0] - 1)
                        link(pool.tensor_scalar(prod, win, cw[:, t, j:j + 1], None, ALU.mult))
                        pool.tensor_tensor(acc, acc, prod, ALU.add).then_inc(s_pconv, 1)
                        taps[0] += 1
                diag = bc(ident[0:TS, 0:TS], 2, [TS, TS, P])
                pool.wait_ge(s_kvs, l + 1)
                pool.wait_ge(s_s1, l + 1)
                for hd in range(HEADS):
                    if hd >= 2:
                        pool.wait_ge(psum_full, USE[("kv", l, hd - 2, 1)] + 1)
                    vd = VD[hd % 2].rearrange("p (b n) -> p b n", b=TS)
                    pool.tensor_tensor(vd, diag, bc(VS[:, hd * P:(hd + 1) * P], 1, [TS, TS, P]), ALU.mult)\
                        .then_inc(s_vd, 1)
                if l == LAYERS - 1:
                    pool.wait_ge(s_on, LAYERS)
                    link(pool.memset(TRI, 1.0))
                    link(pool.affine_select(out=TRI, in_=TRI, compare_op=ALU.is_gt, fill=0.0, base=0,
                                            pattern=[[1, P]], channel_multiplier=-1))
                    pool.iota(IOTA, pattern=[[1, P]], base=0, channel_multiplier=0,
                              allow_small_or_imprecise_dtypes=True).then_inc(s_const, 1)

        @block.vector
        def _(dve):
            steps = [0]

            def link(ins):
                steps[0] += 1
                ins.then_inc(s_dve, 1)
                dve.wait_ge(s_dve, steps[0])

            def done(signal):
                link(dve.memset(scratch[:, :], 0.0))
                dve.sem_inc(signal, 1)

            dve.wait_ge(s_in, 48)
            lb0, lb1 = par_of("lb", 0), par_of("lb", 1)
            link(dve.tensor_tensor(lsm[:, 0, :], lb0, lb1, ALU.max))
            dve.tensor_tensor(lsm[:, 1, :], lb0, lsm[:, 0, :], ALU.subtract)
            dve.tensor_tensor(lsm[:, 2, :], lb1, lsm[:, 0, :], ALU.subtract).then_inc(s_lbx, 1)
            dve.wait_ge(s_lbe, 1)
            link(dve.tensor_tensor(lsm[:, 3, :], lsm[:, 1, :], lsm[:, 2, :], ALU.add))
            link(dve.reciprocal(lsm[:, 3, :], lsm[:, 3, :]))
            dve.tensor_tensor(lsm[:, 1, :], lsm[:, 1, :], lsm[:, 3, :], ALU.mult)
            link(dve.tensor_tensor(lsm[:, 2, :], lsm[:, 2, :], lsm[:, 3, :], ALU.mult))
            dve.tensor_tensor(lbt[:, 0, 0, :], lsm[:, 1, :], lsm[:, 1, :], ALU.subtract)
            link(dve.tensor_tensor(lsm[:, 3, :], lsm[:, 1, :], lsm[:, 2, :], ALU.add))
            link(dve.tensor_tensor(lbt[:, 0, 1, :], lsm[:, 3, :], lsm[:, 1, :], ALU.subtract))
            link(dve.tensor_scalar(lbt[:, 1, :, :], lbt[:, 0, :, :], -1.0, 1.0, ALU.mult, ALU.add))

            def modulation(l, pair):
                name = ("mod", l, pair)
                ps = await_use(dve, name)
                part = slice(16 * pair, 16 * pair + 16)
                ins = dve.tensor_tensor(modt[:, l, part, :], ps[:, 0:16 * NC_TOK].rearrange("p (a n) -> p a n", a=16),
                                        bc(par_of("ada_b", l)[:, part], 2, [P, 16, NC_TOK]), ALU.add)
                freed(ins, name)
                link(dve.memset(scratch[:, :], 0.0))

            def shift(l, part):
                return modt[:, l, part * KT:(part + 1) * KT, :]

            def modulated_norm(l, gain, sh, sc, roots):
                g = bc(gain, 2, [P, KT, NC_TOK])
                link(dve.scalar_tensor_tensor(sc1g[:, :, :], shift(l, sc), 1.0, g, ALU.add, ALU.mult))
                dve.wait_ge(s_rstd, roots)
                link(dve.reciprocal(row[:, 0, :], row[:, 0, :]))
                link(dve.tensor_tensor(h[:, :, :], x[:, :, :], bc(row[:, 0, :], 1, [P, KT, T]), ALU.mult))
                for t in range(KT):
                    dve.tensor_scalar(h[:, t, 0:TP], h[:, t, 0:TP], sc1g[:, t, 0:1], shift(l, sh)[:, t, 0:1], ALU.mult, ALU.add)
                link(dve.tensor_tensor(h[:, :, TP:T], h[:, :, TP:T], sc1g[:, :, 1:NC_TOK], ALU.mult))
                dve.tensor_tensor(h[:, :, TP:T], h[:, :, TP:T], shift(l, sh)[:, :, 1:NC_TOK], ALU.add).then_inc(s_h, 1)

            def residual(name, l, part, t, width=T):
                ps = await_use(dve, name)
                gate = shift(l, part)
                dve.scalar_tensor_tensor(x[:, t, 0:TP], ps[:, 0:TP], gate[:, t, 0:1], x[:, t, 0:TP], ALU.mult, ALU.add)
                freed(dve.tensor_tensor(small[:, t * TS:(t + 1) * TS], ps[:, TP:T], gate[:, t, 1:NC_TOK], ALU.mult), name)

            def residual_samples(signal):
                dve.wait_ge(psum_read[last_use[0] % BANKS], last_use[0] // BANKS + 1)
                dve.tensor_tensor(x[:, :, TP:T], x[:, :, TP:T], small[:, :].rearrange("p (k b) -> p k b", b=TS), ALU.add)\
                    .then_inc(signal, 1)

            last_use = [0]
            taps = [0]
            modulation(0, 0)
            for l in range(LAYERS):
                modulated_norm(l, par_of("n1", l), 0, 1, 3 * l + 1)
                for t in range(KT):
                    name = ("f", l, t)
                    dve.wait_ge(psum_read[USE[name] % BANKS], USE[name] // BANKS + 1)
                    dve.tensor_scalar(F[:, t, :], F[:, t, :], lbt[:, 1, l, t:t + 1], lbt[:, 0, l, t:t + 1], ALU.mult, ALU.add)
                    ins = dve.tensor_scalar(K[:, t, :], K[:, t, :], lbt[:, 1, l, t:t + 1], None, ALU.mult)
                link(ins)
                link(dve.tensor_scalar(F, F, 2.0 ** -63, None, ALU.max))
                dve.tensor_copy(fs[:, :, :], F[:, :, TP:T]).then_inc(s_fg, 1)
                dve.wait_ge(s_ln, l + 1)
                for hd in range(HEADS):
                    for c in range(NCH):
                        tok = slice(c * CH, (c + 1) * CH)
                        ins = dve.tensor_tensor_scan(B[:, hd, tok], ones[:, :], B[:, hd, tok], 0.0, ALU.mult, ALU.add)
                link(ins)

                def level_exponents(n):
                    m = SPANS[n - 1]
                    first, second = levels_view(B, m)
                    d1, d2 = levels_view(as_kt(DEC), m)
                    nb = TP // (2 * m)
                    ref = first[:, :, :, m - 1:m].broadcast_to([P, HEADS, nb, m])
                    dve.tensor_tensor(d1, ref, first, ALU.subtract)
                    dve.tensor_tensor(d2, second, ref, ALU.subtract).then_inc(s_dif, 1)

                def level_operands(n):
                    m = SPANS[n - 1]
                    d1, d2 = levels_view(as_kt(DEC), m)
                    k1 = levels_view(K, m)[0]
                    q2 = levels_view(Q, m)[1]
                    x1, x2 = levels_view(as_kt(Xb[n % 2]), m)
                    if n >= 3:
                        dve.wait_ge(psum_full, USE[("att", l, n - 2, 3)] + 1)
                    dve.wait_ge(s_exp, 8 * l + n)
                    dve.tensor_tensor(x1, d1, k1, ALU.mult)
                    dve.tensor_tensor(x2, d2, q2, ALU.mult).then_inc(s_xl, 1)
                    dve.wait_ge(s_xl, 7 * l + n)

                level_exponents(1)
                dve.wait_ge(s_qv, l + 1)
                level_operands(1)
                dve.wait_ge(s_att0, l + 1)
                cw = par_of("cw", l).rearrange("p (k j) -> p k j", j=CW)

                def conv_taps(l=l, cw=cw):
                    for j in range(CW):
                        for t in DVE_CONV:
                            win, acc = ubuf[:, t, j:j + TP], SBZ[:, t, 0:TP]
                            if j == 0:
                                ins = dve.tensor_scalar(acc, win, cw[:, t, 0:1], par_of("cb", l)[:, t:t + 1], ALU.mult, ALU.add)
                            else:
                                dve.wait_ge(s_conv, taps[0] - len(DVE_CONV) + 1)
                                ins = dve.scalar_tensor_tensor(acc, win, cw[:, t, j:j + 1], acc, ALU.mult, ALU.add)
                            ins.then_inc(s_conv, 1)
                            taps[0] += 1
                            yield

                conv = conv_taps()
                for r, (g, t) in enumerate(REST):
                    if g == "za":
                        name = ("za", l, t)
                        ps = await_use(dve, name)
                        dve.wait_ge(s_zb, KT * l + t + 1)
                        dve.tensor_tensor(ubuf[:, t, PAST:PAST + TP], ps[:, 0:TP], SBZ[:, t, 0:TP], ALU.mult)
                        ins = dve.tensor_tensor(us[:, t, :], ps[:, TP:T], SBZ[:, t, TP:T], ALU.mult)
                        freed(ins, name)
                        if t == KT - 1:
                            done(s_glu)
                    if r >= 2 * KT:
                        for _ in range(8):
                            next(conv, None)
                    if r in LEVEL_AFTER:
                        n = LEVEL_AFTER[r]
                        if 1 <= n < 7:
                            level_exponents(n + 1)
                            level_operands(n + 1)
                        for b in range(4):
                            name = ("att", l, n, b)
                            ps = await_use(dve, name)
                            ins = dve.copy_predicated(attb[:, 4 * b:4 * b + 4, :], bc(masks[:, n, :], 1, [P, 4, P]),
                                                      ps[:, :].rearrange("p (a n) -> p a n", a=4))
                            freed(ins, name)
                bv = B[:, :, 0:TP].rearrange("p h (c n) -> p h c n", n=CH)
                dve.tensor_tensor(as_kt(DEC)[:, :, 0:TP].rearrange("p h (c n) -> p h c n", n=CH),
                                  bv[:, :, :, CH - 1:CH].broadcast_to([P, HEADS, NCH, CH]), bv, ALU.subtract).then_inc(s_dif, 1)
                done(s_att)
                dve.wait_ge(s_exp, 8 * l + 8)
                dve.tensor_tensor(as_kt(X0)[:, :, 0:TP], as_kt(DEC)[:, :, 0:TP], K[:, :, 0:TP], ALU.mult).then_inc(s_kq, 1)
                dve.wait_ge(s_eb, l + 1)
                dve.tensor_tensor(Q[:, :, CH:TP], Q[:, :, CH:TP], B[:, :, CH:TP], ALU.mult).then_inc(s_kq, 1)
                if l == 0:
                    modulation(0, 1)
                for _ in range(40):
                    next(conv, None)
                for b in range(2):
                    name = ("s1", l, b)
                    ps = await_use(dve, name)
                    for s in range(4):
                        hd = 4 * b + s
                        ins = dve.scalar_tensor_tensor(s0b[:, hd, :], s0b[:, hd, :], ebl[:, hd, 1:2],
                                                       ps[:, s * P:(s + 1) * P], ALU.mult, ALU.add)
                    freed(ins, name)
                done(s_s1)
                for hd in range(HEADS):
                    n = HEADS * l + hd
                    st = STB[hd % 2]
                    dve.wait_ge(s_state[hd % 2], 16 * (n // 2 + 1))
                    for half in range(2):
                        name = ("kv", l, hd, half)
                        ps = await_use(dve, name)
                        for b4 in range(4):
                            b = 4 * half + b4
                            ins = dve.scalar_tensor_tensor(st[:, b * P:(b + 1) * P], st[:, b * P:(b + 1) * P],
                                                           fs[:, hd, b:b + 1], ps[:, b4 * P:(b4 + 1) * P], ALU.mult, ALU.add)
                        freed(ins, name)
                    done(s_sn)
                for _ in conv:
                    pass
                if l == 0:
                    modulation(0, 2)
                dve.wait_ge(s_cs, l + 1)
                link(dve.tensor_reduce(small[:, :], sconv[:, :, :, :].rearrange("p k b j -> p (k b) j"), AX, ALU.add))
                sm = small[:, :].rearrange("p (k b) -> p k b", b=TS)
                link(dve.tensor_tensor(us[:, :, :], us[:, :, :], cw[:, :, CW - 1:CW].broadcast_to([P, KT, TS]), ALU.mult))
                link(dve.tensor_tensor(us[:, :, :], us[:, :, :], sm, ALU.add))
                dve.tensor_tensor(SBZ[:, :, TP:T], us[:, :, :], bc(par_of("cb", l), 2, [P, KT, TS]), ALU.add)
                dve.wait_ge(s_pconv, (l + 1) * CW * len(POOL_CONV))
                done(s_cv)
                dve.wait_ge(s_mu, l + 1)
                dve.tensor_tensor(SBZ, SBZ, bc(row[:, 0, :], 1, [P, KT, T]), ALU.subtract).then_inc(s_xc, 1)
                dve.wait_ge(s_hn, l + 1)
                dve.wait_ge(s_sgr, l + 1)
                link(dve.reciprocal(X0, X0))
                link(dve.tensor_tensor(h[:, :, :], h[:, :, :], as_kt(X0), ALU.mult))
                for hd in range(HEADS):
                    ins = dve.scalar_tensor_tensor(h[:, hd, :], h[:, hd, :], par_of("hgn", l)[:, hd:hd + 1], SG[:, hd, :],
                                                   ALU.mult, ALU.mult)
                ins.then_inc(s_on, 1)
                dve.wait_ge(s_rstd, 3 * l + 2)
                link(dve.reciprocal(row[:, 1, :], row[:, 1, :]))
                dve.tensor_tensor(SBZ, SBZ, bc(row[:, 1, :], 1, [P, KT, T]), ALU.mult).then_inc(s_lnn, 1)
                for t in range(KT):
                    name = ("ya", l, t)
                    ps = await_use(dve, name)
                    freed(dve.tensor_tensor(GA[:, t, :], ps[:, 0:T], GA[:, t, :], ALU.mult), name)
                for t in range(KT):
                    name = ("yb", l, t)
                    ps = await_use(dve, name)
                    freed(dve.tensor_tensor(GB[:, t, :], ps[:, 0:T], GB[:, t, :], ALU.mult), name)
                dve.wait_ge(psum_read[USE[("yb", l, KT - 1)] % BANKS], USE[("yb", l, KT - 1)] // BANKS + 1)
                dve.tensor_tensor(GA, GA, GB, ALU.add).then_inc(s_mix, 1)
                for t in range(KT):
                    residual(("wo", l, t), l, 2, t)
                last_use[0] = USE[("wo", l, KT - 1)]
                residual_samples(s_x)
                if l == 0:
                    modulation(1, 0)
                modulated_norm(l, par_of("n2", l), 3, 4, 3 * l + 3)
                if l == 0:
                    modulation(1, 1)
                    for j in range(FT):
                        ps = await_use(dve, ("fu", j))
                        dve.wait_ge(s_gsilu, j + 1)
                        freed(dve.tensor_tensor(HID[:, j, :], ps[:, 0:T], SILU[j % 2], ALU.mult), ("fu", j))
                        dve.wait_ge(psum_read[USE[("fu", j)] % BANKS], USE[("fu", j)] // BANKS + 1)
                        dve.sem_inc(s_hid, 1)
                    for t in range(KT):
                        residual(("fd", t), 0, 5, t)
                    last_use[0] = USE[("fd", KT - 1)]
                    residual_samples(s_x)
                    modulation(1, 2)

            dve.wait_ge(s_tok, 1)
            for tt in range(3):
                link(dve.memset(rt[:, tt, :], 0.0))
            ps = await_use(dve, ("lg",))
            dve.tensor_copy(rt[:, 0:2, 0:NE], ps[:, 0:2 * NE].rearrange("p (a n) -> p a n", a=2))
            freed(dve.tensor_copy(rt[0:TS, 2, 0:NE], ps[0:TS, 2 * NE:3 * NE]), ("lg",))
            link(dve.memset(FACC, 0.0))
            for tt in range(3):
                link(dve.max(rt[:, tt, 24:32], rt[:, tt, 0:NE]))
                link(dve.max_index(rt[:, tt, 56:64].bitcast(u32), rt[:, tt, 24:32], rt[:, tt, 0:NE]))
            link(dve.tensor_copy(rt[:, :, 32:34], rt[:, :, 56:58].bitcast(u32)))
            dve.tensor_tensor(rt[:, :, 36:37], rt[:, :, 25:26], rt[:, :, 24:25], ALU.subtract).then_inc(s_lg, 1)
            dve.wait_ge(s_rex, 1)
            link(dve.tensor_scalar(rt[:, :, 34:35], rt[:, :, 36:37], 1.0, None, ALU.add))
            link(dve.reciprocal(rt[:, :, 34:35], rt[:, :, 34:35]))
            link(dve.tensor_tensor(rt[:, :, 35:36], rt[:, :, 36:37], rt[:, :, 34:35], ALU.mult))
            dve.wait_ge(s_const, 2)
            for tt in range(3):
                dve.tensor_scalar(rt[:, tt, 40:48], IOTA[:, 0:NE], rt[:, tt, 32:33], None, ALU.is_equal)
                dve.tensor_scalar(rt[:, tt, 48:56], IOTA[:, 0:NE], rt[:, tt, 33:34], None, ALU.is_equal)
                dve.tensor_scalar(rt[:, tt, 64:72], IOTA[:, 0:NE], rt[:, tt, 32:33], rt[:, tt, 34:35], ALU.is_equal, ALU.mult)
                dve.tensor_scalar(rt[:, tt, 72:80], IOTA[:, 0:NE], rt[:, tt, 33:34], rt[:, tt, 35:36], ALU.is_equal, ALU.mult)
            link(dve.memset(scratch[:, :], 0.0))
            dve.tensor_tensor(rt[:, :, 16:24], rt[:, :, 64:72], rt[:, :, 72:80], ALU.add)
            dve.tensor_tensor(rt[:, :, 8:16], rt[:, :, 40:48], rt[:, :, 48:56], ALU.add).then_inc(s_sel, 1)
            dve.wait_ge(s_sel, 1)
            ps = await_use(dve, ("pos",))
            link(dve.tensor_scalar(rt[:, :, 40:48], rt[:, :, 8:16], -4096.0, 4096.0, ALU.mult, ALU.add))
            link(dve.memset(PSEL[:, :, :, :], 0.0))
            for tt, (_, tn) in enumerate(TT):
                dve.tensor_tensor(PSEL[0:tn, 0, :, tt], rt[0:tn, tt, 40:48], ps[0:tn, tt * NE:(tt + 1) * NE], ALU.add)
                dve.tensor_copy(PSEL[0:tn, 1, :, tt], rt[0:tn, tt, 16:24])
            freed(dve.tensor_reduce(small[0:1, 0:1], ps[0:1, 3 * NE:4 * NE], AX, ALU.max), ("pos",))
            link(dve.memset(scratch[:, :], 0.0))
            link(dve.tensor_scalar(small[0:1, 2:3], small[0:1, 0:1], float(CAP), None, ALU.is_gt))
            link(dve.tensor_copy(flag[0:1, 0:1], small[0:1, 2:3]))
            dve.sem_inc(s_flag, 2)

            def expert(turn, pair, s):
                base = MOE_USE0 + s * MOE_USES
                own = [s * DVE_STEPS]

                def step(ins, wait=True):
                    own[0] += 1
                    ins.then_inc(m_dve, 1)
                    if wait:
                        dve.wait_ge(m_dve, turn * (2 * DVE_STEPS) + own[0])

                if s == 0:
                    src = PSEL[:, :, bass.ds(pair * 2, 2), :]
                    step(dve.tensor_copy(CUR[:, :, :, :], src))
                    step(dve.tensor_scalar(PSEL[:, 0, bass.ds(pair * 2, 2), :], PSEL[:, 0, bass.ds(pair * 2, 2), :],
                                           float(-CAP), None, ALU.add))
                else:
                    step(dve.memset(scratch[:, :], 0.0))
                    step(dve.memset(scratch[:, :], 0.0))
                for tt in range(3):
                    step(dve.tensor_scalar(SEL[s][:, tt, :], IOTA, CUR[:, 0, s, tt:tt + 1], None, ALU.is_equal), False)
                    step(dve.tensor_scalar(SELC[s][:, tt, :], IOTA, CUR[:, 0, s, tt:tt + 1], CUR[:, 1, s, tt:tt + 1],
                                           ALU.is_equal, ALU.mult), False)
                dve.wait_ge(m_dve, turn * (2 * DVE_STEPS) + own[0])
                dve.sem_inc(m_sel, 1)
                for j in range(FT // 2):
                    n = base + 3 + j
                    dve.wait_ge(psum_full, turn * (2 * MOE_USES) + n + 1)
                    dve.wait_ge(m_silu, (2 * turn + s) * (FT // 2) + j + 1)
                    ups = banks[n % BANKS][:, :].rearrange("p (a b n) -> p a b n", a=2, b=2)[:, :, 1, :]
                    dve.tensor_tensor(MHID[:, 2 * j:2 * j + 2, :], ups, MSILU[j % 2].rearrange("p (a n) -> p a n", a=2), ALU.mult)\
                        .then_inc(psum_read[n % BANKS], 1)
                    dve.wait_ge(psum_read[n % BANKS], turn * (2 * MOE_USES // BANKS) + n // BANKS + 1)
                    dve.sem_inc(m_hid, 1)
                for t in range(KT):
                    n = base + 5 + FT // 2 + t
                    dve.wait_ge(psum_full, turn * (2 * MOE_USES) + n + 1)
                    dve.tensor_tensor(FACC[:, t, :], FACC[:, t, :], banks[n % BANKS][:, 0:T], ALU.add)\
                        .then_inc(psum_read[n % BANKS], 1)
                assert own[0] == (s + 1) * DVE_STEPS, own[0]

            with dve.Fori(0, NE // 2) as pair:
                for s in range(2):
                    expert(pair, pair, s)
            more = dve.value_load(flag[0:1, 0:1], min_val=0, max_val=1)
            with dve.If(more > 0):
                with dve.Fori(1, 3) as rnd:
                    with dve.Fori(0, NE // 2) as pair:
                        for s in range(2):
                            expert(rnd * (NE // 2) + pair, pair, s)
            fsteps = [0]

            def flink(ins):
                fsteps[0] += 1
                ins.then_inc(f_dve, 1)
                dve.wait_ge(f_dve, fsteps[0])

            flink(dve.memset(scratch[:, :], 0.0))
            flink(dve.tensor_tensor(FACC[:, :, TP:T], FACC[:, :, TP:T], shift(1, 5)[:, :, 1:NC_TOK], ALU.mult))
            for t in range(KT):
                dve.scalar_tensor_tensor(x[:, t, 0:TP], FACC[:, t, 0:TP], shift(1, 5)[:, t, 0:1], x[:, t, 0:TP], ALU.mult, ALU.add)
            dve.tensor_tensor(x[:, :, TP:T], x[:, :, TP:T], FACC[:, :, TP:T], ALU.add).then_inc(f_x, 1)
            dve.wait_ge(f_rt, 1)
            flink(dve.reciprocal(row[:, 0, :], row[:, 0, :]))
            for t in range(KT):
                flink(dve.scalar_tensor_tensor(as_kt(X0)[:, t, :], x[:, t, :], par_of("fin")[:, t:t + 1], row[:, 0, :], ALU.mult, ALU.mult))
            dve.sem_inc(f_y, 1)


def kernel(**inputs):
    import numpy as np
    import concourse.bacc as bacc
    from concourse.bass_utils import run_bass_kernel_spmd

    f32 = np.float32
    a = {k: np.asarray(v) for k, v in inputs.items()}

    def tiles(v):
        v = v.reshape(v.shape[:-1] + (v.shape[-1] // P, P))
        return np.moveaxis(v, -1, 0)

    def fmajor(v):
        return np.ascontiguousarray(v.reshape(v.shape[0], KT, P).transpose(2, 1, 0))

    def col_tiles(w, ts=None):
        k, n = w.shape
        v = w.reshape(k // P, P, n // P, P).transpose(2, 0, 1, 3)
        return v if ts is None else v[ts]

    def slots(blocks):
        return blocks.reshape(-1, SLOT_BLOCKS, P, P).transpose(0, 2, 1, 3).reshape(-1, P, SLOT_W)

    flat = lambda v: v.reshape(-1, P, P)

    def ada(l, pair):
        return flat(col_tiles(a["ada_w"][l], slice(16 * pair, 16 * pair + 16)))

    def ffn_up(g, u):
        return flat(np.stack([col_tiles(g), col_tiles(u)], axis=1))

    seq = [ada(0, 0)]
    cols = {"q": 0, "f": 1, "i": 2, "g": 3, "za": 4, "zb": 5, "ga": 6, "gb": 7}
    for l in range(LAYERS):
        for g in ("f", "q", "i", "zb", "za", "g", "ga", "gb"):
            seq.append(flat(col_tiles(a["w_in"][l][:, cols[g] * D:(cols[g] + 1) * D])))
        if l == 0:
            seq += [ada(0, 1), ada(0, 2)]
        seq += [flat(col_tiles(a[n][l])) for n in ("w_hg_out", "w_conv_out", "w_o")]
        if l == 0:
            seq += [ada(1, 0), ada(1, 1), ffn_up(a["ffn_w_gate"][0], a["ffn_w_up"][0]),
                    flat(col_tiles(a["ffn_w_down"][0])), ada(1, 2)]
    stream = slots(np.concatenate(seq))
    moe = np.empty((NE // 2, 2 * MOE_SLOTS, P, SLOT_W), f32)
    for e in range(NE):
        down = a["moe_w_down"][0, e].reshape(FT, P, KT, P).transpose(0, 2, 1, 3)
        moe[e // 2, (e % 2) * MOE_SLOTS:(e % 2 + 1) * MOE_SLOTS] = slots(
            np.concatenate([ffn_up(a["moe_w_gate"][0, e], a["moe_w_up"][0, e]), flat(down)]))
    cw = a["conv_w"].reshape(LAYERS, CW, KT, P).transpose(3, 0, 2, 1)
    par = np.concatenate([v.reshape(P, -1) for v in (
        tiles(a["ada_b"]), tiles(a["norm1_g"]), tiles(a["norm2_g"]), tiles(a["lb_logits"]), tiles(a["hg_norm_g"]),
        tiles(a["conv_b"]), tiles(a["conv_ln_g"]), tiles(a["conv_ln_b"]), cw, tiles(a["final_norm_g"]),
        a["router_w"][0].reshape(KT, P, NE).transpose(1, 0, 2))], axis=1)
    arrays = {
        "x": fmajor(np.concatenate([a["x_prompt"][0], a["x_sample"][:, 0]])),
        "c": fmajor(np.concatenate([a["c_prompt"], a["c_sample"]])),
        "par": par, "stream": stream, "moe": moe,
        "state_h": a["state_hgrn"].transpose(0, 2, 3, 1, 4),
        "state_c": a["state_conv"].reshape(LAYERS, TS, PAST, KT, P).transpose(0, 4, 3, 1, 2),
    }
    outs = {"y": (P, KT, T), "hp": (LAYERS, P, HEADS, P), "cp": (LAYERS, P, KT, PAST),
            "hs": (LAYERS, HEADS, P, TS, P), "cs": (LAYERS, P, KT, TS, PAST)}
    nc = bacc.Bacc("TRN2", target_bir_lowering=False, num_devices=1)
    arrays = {"in_" + k: np.ascontiguousarray(v) for k, v in arrays.items()}
    ins = [nc.dram_tensor(k, v.shape, mybir.dt.from_np(v.dtype), kind="ExternalInput").ap() for k, v in arrays.items()]
    o = [nc.dram_tensor("out_" + k, v, mybir.dt.float32, kind="ExternalOutput").ap() for k, v in outs.items()]
    trunk_kernel(nc, *ins, *o)
    r = run_bass_kernel_spmd(nc, [arrays], core_ids=[0]).results[0]
    y = r["out_y"].transpose(2, 1, 0).reshape(T, D)
    hp = r["out_hp"].transpose(0, 2, 1, 3)[:, None]
    cp = r["out_cp"].transpose(0, 3, 2, 1).reshape(LAYERS, PAST, D)[:, None]
    hs = r["out_hs"].transpose(0, 3, 1, 2, 4)
    cs = r["out_cs"].transpose(0, 3, 4, 2, 1).reshape(LAYERS, TS, PAST, D)
    return (y[None, 0:TP], y[TP:T, None], hp, cp, hs, cs)
```

```python
import concourse.bass as bass
from concourse import mybir
from contextlib import ExitStack

P = 128
D = 1024
KT = D // P
TP = 256
TS = 8
T = TP + TS
NC_TOK = 1 + TS
LAYERS = 2
HEADS = 8
CH = 128
NCH = TP // CH
HC = HEADS * NCH
CW = 31
PAST = CW - 1
FF = 2816
FT = FF // P
NE = 8
SLOT_BLOCKS = 16
SLOT_W = SLOT_BLOCKS * P
RING = 6
BANKS = 8
EPS = 1e-6
SPANS = [64, 32, 16, 8, 4, 2, 1]
REST = [(g, t) for g in ("zb", "za", "g", "ga", "gb") for t in range(KT)]
STAGES = {3 * n + 2: [("att", n)] for n in range(8)}
STAGES[25] = [("vt",)]
STAGES[26] = [("kt",)]
STAGES[27] = [("s0",)]
STAGES[28] = [("o",)]
STAGES[29] = [("s1",), ("kvs",)]
for _h in range(HEADS + 1):
    STAGES[31 + _h] = ([("kv", _h)] if _h < HEADS else []) + ([("os", _h - 1)] if _h > 0 else [])
STAGE_BANKS = {"att": 4, "vt": 4, "kt": 4, "s0": 2, "o": 4, "s1": 2, "kvs": 4, "kv": 2, "os": 1}
CAP = 128
TT = [(0, P), (P, P), (TP, TS)]
POOL_CONV = (7,)
DVE_CONV = tuple(t for t in range(KT) if t not in POOL_CONV)

_at = 0
PAR = {}
for _name, _n in (("ada_b", LAYERS * 48), ("n1", LAYERS * KT), ("n2", LAYERS * KT), ("lb", LAYERS * KT),
                  ("hgn", LAYERS * KT), ("cb", LAYERS * KT), ("lng", LAYERS * KT), ("lnb", LAYERS * KT),
                  ("cw", LAYERS * KT * CW), ("fin", KT), ("rw", KT * NE)):
    PAR[_name] = (_at, _n)
    _at += _n
NPAR = _at


def psum_order():
    def mod(l, pair):
        out.append(("mod", l, pair, 0))
        for g in range(1, 4):
            out.extend([("mod", l, pair, g), ("mt", l, pair, g - 1)])
        out.append(("mt", l, pair, 3))

    out = []
    mod(0, 0)
    for l in range(LAYERS):
        out.append(("n1", l))
        if l == 1:
            mod(1, 2)
        out += [(g, l, t) for g in ("f", "q", "i") for t in range(KT)]
        for r, (g, t) in enumerate(REST):
            out.append((g, l, t))
            for stage in STAGES.get(r, ()):
                out += [(stage[0], l) + stage[1:] + (b,) for b in range(STAGE_BANKS[stage[0]])]
        out += [("hn", l, h) for h in range(HEADS)]
        if l == 0:
            mod(0, 1)
        out += [("ya", l, t) for t in range(KT)]
        out += [("mu", l), ("var", l)]
        out += [(g, l, t) for g in ("yb", "wo") for t in range(KT)]
        if l == 0:
            mod(0, 2)
        out.append(("n2", l))
        if l == 0:
            mod(1, 0)
            for j in range(FT):
                out += [("fg", j), ("fu", j)]
            out += [("fd", t) for t in range(KT)]
            mod(1, 1)
    out += [("tok", b) for b in range(6)] + [("lg",), ("pos",)]
    return out


USE = {name: n for n, name in enumerate(psum_order())}
MOE_USE0 = len(USE)
MOE_USES = 24
STREAM_SLOTS = (LAYERS * (48 + 64 + 24) * KT + 3 * FT * KT) // SLOT_BLOCKS
MOE_SLOTS = 3 * FT * KT // SLOT_BLOCKS
DVE_STEPS = 8


def trunk_kernel(nc, x_in, c_in, par_in, stream_in, moe_in, sh_in, sc_in,
                 y_out, hp_out, cp_out, hs_out, cs_out):
    fp32, u8, u32, i32 = mybir.dt.float32, mybir.dt.uint8, mybir.dt.uint32, mybir.dt.int32
    ALU = mybir.AluOpType
    ACT = mybir.ActivationFunctionType
    AX = mybir.AxisListType.X
    ctx = ExitStack()
    with ctx:
        def sb(name, shape, dt=fp32):
            return ctx.enter_context(nc.sbuf_tensor(name, shape, dt))

        def sem(name):
            return ctx.enter_context(nc.semaphore(name))

        ring = sb("ring", [P, RING, SLOT_W])
        x = sb("x", [P, KT, T])
        h = sb("h", [P, KT, T])
        qkv = sb("qkv", [P, 3, KT, T])
        big = sb("big", [P, 6, KT, T])
        tmp = sb("tmp", [P, 3, KT * T])
        attb = sb("attb", [P, HC, P])
        s0b = sb("s0b", [P, HEADS, P])
        ubuf = sb("ubuf", [P, KT, PAST + TP])
        sconv = sb("sconv", [P, KT, TS, PAST])
        par = sb("par", [P, NPAR])
        modt = sb("modt", [P, LAYERS, 48, NC_TOK])
        sc1g = sb("sc1g", [P, KT, NC_TOK])
        cT = sb("cT", [P, KT, NC_TOK])
        ident = sb("ident", [P, P])
        ones = sb("ones", [P, P])
        masks = sb("masks", [P, 8, P], u8)
        eps_col = sb("eps_col", [P, 1])
        lbt = sb("lbt", [P, 2, LAYERS, KT])
        lsm = sb("lsm", [P, 4, KT])
        fs = sb("fs", [P, HEADS, TS])
        us = sb("us", [P, KT, TS])
        ebl = sb("ebl", [P, HEADS, NCH])
        row = sb("row", [P, 2, T])
        small = sb("small", [P, KT * TS])
        rt = sb("rt", [P, 3, 80])
        scratch = sb("scratch", [P, 1])
        modrow = attb[:, 0:8, :].rearrange("p a n -> p (a n)").rearrange("p (a n) -> p a n", a=2)
        flag = sb("flag", [1, 2], i32)

        Q, K, V = (qkv[:, n] for n in range(3))
        F, SBZ, SG, GA, GB, B = (big[:, n] for n in range(6))
        DEC, X0, X1 = (tmp[:, n, :] for n in range(3))
        Xb = [X0, X1]
        KTOK, VTOK = DEC, X1
        KS, VS = X0[0:TS, 0:D], X0[0:TS, D:2 * D]
        VD = [DEC[0:TS, n * 1024:(n + 1) * 1024] for n in range(2)]
        Bf = B.rearrange("p k t -> p (k t)")
        STB = [Bf[:, 0:1024], Bf[:, 1024:2048]]
        SNEW = F.rearrange("p k t -> p (k t)")[:, 0:KT * TS * PAST]
        qkv_f = qkv[:, :, :, :].rearrange("p a k t -> p (a k t)")
        HID = qkv_f[:, 0:FT * T].rearrange("p (j t) -> p j t", t=T)
        SILU = [GA.rearrange("p k t -> p (k t)")[:, n * 512:n * 512 + T] for n in range(2)]
        MHID = qkv_f[:, 0:FT * CAP].rearrange("p (j t) -> p j t", t=CAP)
        H2G = [V.rearrange("p k t -> p (k t)")[:, n * 1024:(n + 1) * 1024] for n in range(2)]
        tmp_f = tmp[:, :, :].rearrange("p a n -> p (a n)")
        H2TOK = tmp_f[:, 0:3 * D].rearrange("p (a n) -> p a n", a=3)
        SEL = [tmp_f[:, 3 * D + n * 384:3 * D + (n + 1) * 384].rearrange("p (a n) -> p a n", a=3) for n in range(2)]
        SELC = [tmp_f[:, 4 * D + n * 384:4 * D + (n + 1) * 384].rearrange("p (a n) -> p a n", a=3) for n in range(2)]
        YE = F.rearrange("p k t -> p (k t)")[:, 0:D]
        MSILU = [SBZ.rearrange("p k t -> p (k t)")[:, n * 256:(n + 1) * 256] for n in range(2)]
        SCT = [SG.rearrange("p k t -> p (k t)")[:, n * T:(n + 1) * T] for n in range(2)]
        FACC = GA
        TRI = attb[:, 0, :]
        IOTA = attb[:, 1, :]
        PSEL = sb("psel", [P, 2, NE, 3])
        CUR = sb("cur", [P, 2, 2, 3])

        banks = [ctx.enter_context(nc.psum_tensor(f"bank{n}", [P, 512], fp32)) for n in range(BANKS)]
        psum_full = sem("psum_full")
        psum_read = [sem(f"psum_read{n}") for n in range(BANKS)]
        landed = [sem(f"weights_landed{n}") for n in range(RING)]
        started = sem("slot_started")
        s_in = sem("inputs_landed")
        s_c = sem("c_landed")
        s_state = [sem(f"state_landed{n}") for n in range(2)]
        s_sconv = sem("sconv_landed")
        s_const = sem("constants_ready")
        s_pool = sem("pool_step")
        s_dve = sem("dve_step")
        s_act = sem("act_step")
        s_sq = sem("squares_ready")
        s_rstd = sem("roots_ready")
        s_modrow = sem("modulation_rows_ready")
        s_mod = sem("modulation_ready")
        s_cact = sem("c_act_ready")
        s_lbx = sem("lb_max_ready")
        s_lbe = sem("lb_exp_ready")
        s_h = sem("h_ready")
        s_fg = sem("forget_ready")
        s_ln = sem("logf_ready")
        s_scan = sem("cumsum_ready")
        s_qv = sem("qv_ready")
        s_zb = sem("sigmoid_zb_ready")
        s_glu = sem("glu_ready")
        s_dif = sem("decay_exponent_ready")
        s_exp = sem("decay_ready")
        s_xl = sem("level_operand_ready")
        s_kq = sem("decayed_kq_ready")
        s_eb = sem("chunk_decay_ready")
        s_vt = sem("vtok_ready")
        s_kt = sem("ktok_ready")
        s_att0 = sem("att_cleared")
        s_att = sem("att_ready")
        s_s0 = sem("s0_ready")
        s_s1 = sem("s1_ready")
        s_s1out = sem("s1_stored")
        s_kvs = sem("sample_kv_ready")
        s_vd = sem("vdiag_ready")
        s_sn = sem("sample_state_ready")
        s_ssout = [sem(f"sample_state_stored{n}") for n in range(2)]
        s_o = sem("heads_out_ready")
        s_osq = sem("heads_squares_ready")
        s_hn = sem("heads_roots_ready")
        s_on = sem("gated_heads_ready")
        s_conv = sem("conv_tap")
        s_pconv = sem("pool_conv_tap")
        s_cs = sem("sample_products_ready")
        s_snew = sem("sample_conv_state_ready")
        s_csout = sem("conv_states_stored")
        s_cv = sem("conv_ready")
        s_mu = sem("mean_ready")
        s_xc = sem("centred_ready")
        s_lnn = sem("layernorm_ready")
        s_yb = sem("branch_b_ready")
        s_sgr = sem("gates_ready")
        s_mix = sem("mixed_ready")
        s_x = sem("x_ready")
        s_gsilu = sem("ffn_silu_ready")
        s_hid = sem("hidden_ready")
        s_tok = sem("h2_token_major_ready")
        s_lg = sem("logits_ready")
        s_rex = sem("router_exp_ready")
        s_sel = sem("assignment_ready")
        s_flag = sem("flag_ready")
        m_sel = sem("moe_selection_ready")
        m_h2g = sem("moe_gathered_ready")
        m_silu = sem("moe_silu_ready")
        m_hid = sem("moe_hidden_ready")
        m_sct = sem("moe_scatter_ready")
        m_y = sem("moe_y_ready")
        m_acc = sem("moe_accumulated")
        m_dve = sem("moe_dve_step")
        f_x = sem("final_x_ready")
        f_sq = sem("final_squares_ready")
        f_st = sem("final_sum_ready")
        f_rt = sem("final_root_ready")
        f_dve = sem("final_dve_step")
        f_y = sem("y_ready")
        s_done = sem("outputs_stored")

        def par_of(name, l=None):
            at, n = PAR[name]
            if l is None:
                return par[:, at:at + n]
            n //= LAYERS
            return par[:, at + l * n:at + (l + 1) * n]

        def bank(name):
            return banks[USE[name] % BANKS]

        def await_use(eng, name):
            eng.wait_ge(psum_full, USE[name] + 1)
            return bank(name)

        def freed(ins, name):
            ins.then_inc(psum_read[USE[name] % BANKS], 1)

        def levels_view(buf, m):
            v = buf[:, :, 0:TP].rearrange("p h (n a m) -> p h n a m", a=2, m=m)
            return v[:, :, :, 0, :], v[:, :, :, 1, :]

        def as_kt(flat):
            return flat.rearrange("p (k t) -> p k t", t=T)

        def bc(ap, axis, shape):
            return ap.unsqueeze(axis).broadcast_to(shape)

        block = ctx.enter_context(nc.Block())

        @block.sync
        def _(sp):
            sp.dma_start(cT[:, :, :], c_in).then_inc(s_c, 16)
            sp.dma_start(par[:, :], par_in).then_inc(s_in, 16)
            for n in range(STREAM_SLOTS):
                if n >= RING:
                    sp.wait_ge(started, n - RING + 2)
                sp.dma_start(ring[:, n % RING, :], stream_in[n]).then_inc(landed[n % RING], 16)
                if n == 0:
                    sp.dma_start(x[:, :, :], x_in).then_inc(s_in, 16)

            def expert_pair(pair, turn):
                for n in range(2 * MOE_SLOTS):
                    at = STREAM_SLOTS + n
                    sp.wait_ge(started, turn * (2 * MOE_SLOTS) + at - RING + 2)
                    sp.dma_start(ring[:, at % RING, :], moe_in[bass.ds(pair, 1), n]).then_inc(landed[at % RING], 16)

            with sp.Fori(0, NE // 2) as pair:
                expert_pair(pair, pair)
            sp.wait_ge(s_flag, 2)
            more = sp.value_load(flag[0:1, 0:1], min_val=0, max_val=1)
            with sp.If(more > 0):
                with sp.Fori(1, 3) as rnd:
                    with sp.Fori(0, NE // 2) as pair:
                        expert_pair(pair, rnd * (NE // 2) + pair)
            sp.wait_ge(f_y, 1)
            sp.dma_start(y_out, as_kt(X0)).then_inc(s_done, 16)
            sp.wait_ge(s_done, 16)
            sp.wait_ge(s_csout, 32 * LAYERS)
            sp.wait_ge(s_s1out, 16 * LAYERS)
            for n in range(2):
                sp.wait_ge(s_ssout[n], 64 * LAYERS)

        @block.tensor
        def _(pe):
            order = psum_order()
            at = {"use": 0, "block": 0}

            def mm(out, lhsT, rhs, start=True, stop=True):
                return nc.tensor.matmul(out, lhsT, rhs, start=start, stop=stop)

            def open_use(name):
                n = at["use"]
                assert order[n] == name, (order[n], name)
                at["use"] += 1
                if n >= BANKS:
                    pe.wait_ge(psum_read[n % BANKS], n // BANKS)
                return banks[n % BANKS]

            def weight_mm(out, rhs, start, stop, width=1, lhsT=None):
                n, w = divmod(at["block"], SLOT_BLOCKS)
                at["block"] += width
                if w == 0:
                    pe.wait_ge(landed[n % RING], 16 * (n // RING + 1))
                weights = ring[:, n % RING, w * P:(w + width) * P]
                ins = mm(out, weights, rhs, start, stop) if lhsT is None else mm(out, lhsT, weights, start, stop)
                if w == 0:
                    ins.then_inc(started, 1)
                return ins

            def project(name, src, tiles_ready=None):
                ps = open_use(name)
                for k in range(KT):
                    if tiles_ready is not None:
                        pe.wait_ge(s_h, tiles_ready + k)
                    ins = weight_mm(ps[:, 0:T], src[:, k, :], k == 0, k == KT - 1)
                ins.then_inc(psum_full, 1)

            mod_groups = [0]

            def modulation(l, pair):
                for g in range(5):
                    if g < 4:
                        ps = open_use(("mod", l, pair, g))
                        for k in range(KT):
                            ins = weight_mm(ps[0:NC_TOK, :], None, k == 0, k == KT - 1, 4, cT[:, k, :])
                        ins.then_inc(psum_full, 1)
                    if g >= 1:
                        mod_groups[0] += 1
                        pe.wait_ge(s_modrow, mod_groups[0])
                        ps = open_use(("mt", l, pair, g - 1))
                        for t in range(4):
                            ins = nc.tensor.transpose(ps[:, t * NC_TOK:(t + 1) * NC_TOK],
                                                      modrow[0:NC_TOK, (g - 1) % 2, t * P:(t + 1) * P],
                                                      ident[0:NC_TOK, 0:NC_TOK])
                        ins.then_inc(psum_full, 1)

            def feature_sum(name, src):
                ps = open_use(name)
                for k in range(KT):
                    ins = mm(ps[:, 0:T], ones[:, :], src[:, k, :], k == 0, k == KT - 1)
                ins.then_inc(psum_full, 1)

            def transposes(name, l, src):
                for b in range(4):
                    ps = open_use((name, l, b))
                    for s in range(4):
                        hd, c = divmod(4 * b + s, NCH)
                        ins = nc.tensor.transpose(ps[:, s * P:(s + 1) * P], src[:, hd, c * CH:(c + 1) * CH], ident[:, :])
                    ins.then_inc(psum_full, 1)

            def levels(l, n):
                if n == 0:
                    pe.wait_ge(s_fg, l + 1)
                    pe.wait_ge(s_qv, l + 1)
                else:
                    pe.wait_ge(s_xl, 7 * l + n)
                for b in range(4):
                    ps = open_use(("att", l, n, b))
                    for s in range(4):
                        hd, c = divmod(4 * b + s, NCH)
                        tok = slice(c * CH, (c + 1) * CH)
                        a, w = (K, Q) if n == 0 else (as_kt(Xb[n % 2]), as_kt(Xb[n % 2]))
                        ins = mm(ps[:, s * P:(s + 1) * P], a[:, hd, tok], w[:, hd, tok])
                    ins.then_inc(psum_full, 1)

            def decayed_keys(l):
                pe.wait_ge(s_kq, 2 * l + 1)
                transposes("kt", l, as_kt(X0))

            def chunk_states(name, l, c):
                if c == 0:
                    pe.wait_ge(s_vt, l + 1)
                    pe.wait_ge(s_kt, l + 1)
                for b in range(2):
                    ps = open_use((name, l, b))
                    for s in range(4):
                        hc = (4 * b + s) * NCH + c
                        ins = mm(ps[:, s * P:(s + 1) * P], KTOK[:, hc * P:(hc + 1) * P], VTOK[:, hc * P:(hc + 1) * P])
                    ins.then_inc(psum_full, 1)

            def heads_out(l):
                pe.wait_ge(s_att, l + 1)
                pe.wait_ge(s_s0, l + 1)
                pe.wait_ge(s_kq, 2 * l + 2)
                for b in range(4):
                    ps = open_use(("o", l, b))
                    for s in range(2):
                        hd = 2 * b + s
                        hc = hd * NCH
                        mm(ps[:, s * TP:s * TP + CH], VTOK[:, hc * P:(hc + 1) * P], attb[:, hc, :])
                        out = ps[:, s * TP + CH:(s + 1) * TP]
                        mm(out, VTOK[:, (hc + 1) * P:(hc + 2) * P], attb[:, hc + 1, :], True, False)
                        ins = mm(out, s0b[:, hd, :], Q[:, hd, CH:TP], False, True)
                    ins.then_inc(psum_full, 1)

            def sample_kv(l):
                for b in range(4):
                    ps = open_use(("kvs", l, b))
                    for s in range(4):
                        ins = mm(ps[0:TS, s * P:(s + 1) * P], (K, V)[b // 2][:, 4 * (b % 2) + s, TP:T], ident[:, :])
                    ins.then_inc(psum_full, 1)

            def sample_outer(l, hd):
                if hd == 0:
                    pe.wait_ge(s_kvs, l + 1)
                pe.wait_ge(s_vd, HEADS * l + hd + 1)
                for half in range(2):
                    ps = open_use(("kv", l, hd, half))
                    mm(ps[:, :], KS[:, hd * P:(hd + 1) * P], VD[hd % 2][:, half * 512:(half + 1) * 512])\
                        .then_inc(psum_full, 1)

            def sample_out(l, hd):
                ps = open_use(("os", l, hd, 0))
                pe.wait_ge(s_sn, HEADS * l + hd + 1)
                for b in range(TS):
                    ins = mm(ps[:, b:b + 1], STB[hd % 2][:, b * P:(b + 1) * P], Q[:, hd, TP + b:TP + b + 1])
                ins.then_inc(psum_full, 1)

            stages = {"att": levels, "vt": lambda l: transposes("vt", l, V), "kt": decayed_keys,
                      "s0": lambda l: chunk_states("s0", l, 0), "o": heads_out,
                      "s1": lambda l: chunk_states("s1", l, 1), "kvs": sample_kv, "kv": sample_outer, "os": sample_out}

            pe.wait_ge(s_const, 1)
            pe.wait_ge(s_cact, 1)
            modulation(0, 0)
            pe.wait_ge(s_const, 2)
            for l in range(LAYERS):
                pe.wait_ge(s_sq, 4 * l + 1)
                feature_sum(("n1", l), as_kt(X1))
                if l == 1:
                    modulation(1, 2)
                for g in ("f", "q", "i"):
                    for t in range(KT):
                        project((g, l, t), h, 2 * KT * l + 1 if (g, t) == ("f", 0) else None)
                for r, (g, t) in enumerate(REST):
                    project((g, l, t), h)
                    for stage in STAGES.get(r, ()):
                        stages[stage[0]](l, *stage[1:])
                pe.wait_ge(s_osq, l + 1)
                for hd in range(HEADS):
                    ps = open_use(("hn", l, hd))
                    mm(ps[:, 0:T], ones[:, :], as_kt(X1)[:, hd, :]).then_inc(psum_full, 1)
                if l == 0:
                    modulation(0, 1)
                pe.wait_ge(s_on, l + 1)
                for t in range(KT):
                    project(("ya", l, t), V)
                pe.wait_ge(s_cv, l + 1)
                feature_sum(("mu", l), SBZ)
                pe.wait_ge(s_sq, 4 * l + 2)
                feature_sum(("var", l), as_kt(DEC))
                for t in range(KT):
                    if t == 0:
                        pe.wait_ge(s_yb, l + 1)
                    project(("yb", l, t), SBZ)
                pe.wait_ge(s_mix, l + 1)
                for t in range(KT):
                    project(("wo", l, t), GA)
                if l == 0:
                    modulation(0, 2)
                pe.wait_ge(s_sq, 4 * l + 3)
                feature_sum(("n2", l), as_kt(X1))
                if l == 0:
                    modulation(1, 0)
                    for j in range(FT):
                        project(("fg", j), h, 2 * KT * l + KT + 1 if j == 0 else None)
                        project(("fu", j), h)
                    pe.wait_ge(s_hid, FT)
                    for t in range(KT):
                        ps = open_use(("fd", t))
                        for k in range(FT):
                            ins = weight_mm(ps[:, 0:T], HID[:, k, :], k == 0, k == FT - 1)
                        ins.then_inc(psum_full, 1)
                    modulation(1, 1)
            pe.wait_ge(s_h, 2 * KT * LAYERS)
            assert at["block"] == STREAM_SLOTS * SLOT_BLOCKS

            for b in range(6):
                tt, half = divmod(b, 2)
                t0, tn = TT[tt]
                ps = open_use(("tok", b))
                for s in range(4):
                    ins = mm(ps[0:tn, s * P:(s + 1) * P], h[:, 4 * half + s, t0:t0 + tn], ident[:, :])
                ins.then_inc(psum_full, 1)
            rw = par_of("rw").rearrange("p (k e) -> p k e", e=NE)
            ps = open_use(("lg",))
            for tt, (t0, tn) in enumerate(TT):
                for k in range(KT):
                    ins = mm(ps[0:tn, tt * NE:(tt + 1) * NE], h[:, k, t0:t0 + tn], rw[:, k, :], k == 0, k == KT - 1)
            ins.then_inc(psum_full, 1)
            pe.wait_ge(s_sel, 1)
            ps = open_use(("pos",))
            for tt, (_, tn) in enumerate(TT):
                for u in range(tt + 1):
                    un = TT[u][1]
                    lhsT = TRI[0:un, 0:tn] if u == tt else ones[0:un, 0:tn]
                    mm(ps[0:tn, tt * NE:(tt + 1) * NE], lhsT, rt[0:un, u, 8:16], u == 0, u == tt)
            for u, (_, un) in enumerate(TT):
                ins = mm(ps[:, 3 * NE:4 * NE], ones[0:un, :], rt[0:un, u, 8:16], u == 0, u == 2)
            ins.then_inc(psum_full, 1)
            assert at["use"] == MOE_USE0

            def expert(turn, s):
                use, blk = [s * MOE_USES], [s * MOE_SLOTS * SLOT_BLOCKS]

                def open_moe():
                    n = MOE_USE0 + use[0]
                    use[0] += 1
                    pe.wait_ge(psum_read[n % BANKS], turn * (2 * MOE_USES // BANKS) + n // BANKS)
                    return banks[n % BANKS]

                def slot_ap(width):
                    n, w = divmod(blk[0], SLOT_BLOCKS)
                    n += STREAM_SLOTS
                    if w == 0:
                        pe.wait_ge(landed[n % RING], turn * (16 * 2 * MOE_SLOTS // RING) + 16 * (n // RING + 1))
                    ap = ring[:, n % RING, w * P:(w + width) * P]
                    blk[0] += width
                    return ap, w == 0

                pe.wait_ge(m_sel, 2 * turn + s + 1)
                for half in range(2):
                    ps = open_moe()
                    for g in range(4):
                        k = 4 * half + g
                        for tt, (_, tn) in enumerate(TT):
                            ins = mm(ps[:, g * P:(g + 1) * P], H2TOK[0:tn, tt, k * P:(k + 1) * P],
                                     SEL[s][0:tn, tt, :], tt == 0, tt == 2)
                    ins.then_inc(psum_full, 1)
                ps = open_moe()
                for tt, (t0, tn) in enumerate(TT):
                    ins = mm(ps[:, t0:t0 + tn], SELC[s][0:tn, tt, :], ident[0:tn, 0:tn])
                ins.then_inc(psum_full, 1)
                pe.wait_ge(m_h2g, 2 * turn + s + 1)
                for j in range(FT // 2):
                    ps = open_moe()
                    for piece in range(4):
                        for k in range(KT):
                            w, first = slot_ap(1)
                            ins = mm(ps[:, piece * P:(piece + 1) * P], w, H2G[s][:, k * P:(k + 1) * P], k == 0, k == KT - 1)
                            if first:
                                ins.then_inc(started, 1)
                    ins.then_inc(psum_full, 1)
                halves = [open_moe(), open_moe()]
                for k in range(FT):
                    if k % 2 == 0:
                        pe.wait_ge(m_hid, (2 * turn + s) * (FT // 2) + k // 2 + 1)
                    for half in range(2):
                        w, first = slot_ap(4)
                        ins = mm(halves[half][:, :], MHID[:, k, :], w, k == 0, k == FT - 1)
                        if first:
                            ins.then_inc(started, 1)
                        if k == FT - 1:
                            ins.then_inc(psum_full, 1)
                pe.wait_ge(m_sct, 2 * turn + s + 1)
                for t in range(KT):
                    if t % 4 == 0:
                        pe.wait_ge(m_y, 2 * (2 * turn + s) + t // 4 + 1)
                    ps = open_moe()
                    mm(ps[:, 0:T], YE[:, t * P:(t + 1) * P], SCT[s]).then_inc(psum_full, 1)
                assert use[0] == (s + 1) * MOE_USES

            with pe.Fori(0, NE // 2) as pair:
                for s in range(2):
                    expert(pair, s)
            pe.wait_ge(s_flag, 2)
            more = pe.value_load(flag[0:1, 0:1], min_val=0, max_val=1)
            with pe.If(more > 0):
                with pe.Fori(1, 3) as rnd:
                    with pe.Fori(0, NE // 2) as pair:
                        for s in range(2):
                            expert(rnd * (NE // 2) + pair, s)
            pe.wait_ge(f_sq, 1)
            for k in range(KT):
                ins = mm(banks[0][:, 0:T], ones[:, :], as_kt(X1)[:, k, :], k == 0, k == KT - 1)
            ins.then_inc(f_st, 1)

        @block.scalar
        def _(act):
            steps = [0]

            def link(ins):
                steps[0] += 1
                ins.then_inc(s_act, 1)
                act.wait_ge(s_act, steps[0])

            def own_read(name):
                act.wait_ge(psum_read[USE[name] % BANKS], USE[name] // BANKS + 1)

            def log_mean(name, out, scale):
                ps = await_use(act, name)
                freed(act.activation(out, ps[:, 0:T], ACT.Ln, bias=eps_col[:, 0:1], scale=scale), name)
                own_read(name)

            def inverse_root(name, out, signal):
                log_mean(name, out, 1.0 / D)
                act.activation(out, out, ACT.Exp, scale=-0.5).then_inc(signal, 1)

            groups = [0]

            def modulation(l, pair):
                for g in range(4):
                    name = ("mod", l, pair, g)
                    ps = await_use(act, name)
                    if groups[0] >= 2:
                        act.wait_ge(s_mod, groups[0] - 1)
                    act.activation(modrow[0:NC_TOK, g % 2, :], ps[0:NC_TOK, :], ACT.Copy).then_inc(s_act, 1)
                    steps[0] += 1
                    act.wait_ge(s_act, steps[0])
                    act.sem_inc(psum_read[USE[name] % BANKS], 1)
                    act.sem_inc(s_modrow, 1)
                    groups[0] += 1

            def levels(l, n):
                if 1 <= n < 7:
                    level_exp(l, n + 1)

            def level_exp(l, n):
                act.wait_ge(s_dif, 8 * l + n)
                act.activation(as_kt(DEC)[:, :, 0:TP], as_kt(DEC)[:, :, 0:TP], ACT.Exp).then_inc(s_exp, 1)

            def values(l):
                level_exp(l, 8)
                link(act.activation(ebl[:, :, :], B[:, :, CH - 1:TP:CH], ACT.Exp))
                act.activation(B[:, :, CH:TP], B[:, :, CH:TP], ACT.Exp).then_inc(s_eb, 1)
                act.wait_ge(s_att, l + 1)
                for b in range(4):
                    ps = await_use(act, ("vt", l, b))
                    freed(act.activation(VTOK[:, b * 512:(b + 1) * 512], ps[:, :], ACT.Copy), ("vt", l, b))
                own_read(("vt", l, 3))
                act.sem_inc(s_vt, 1)

            def keys(l):
                act.wait_ge(s_kq, 2 * l + 1)
                for b in range(4):
                    ps = await_use(act, ("kt", l, b))
                    freed(act.activation(KTOK[:, b * 512:(b + 1) * 512], ps[:, :], ACT.Copy), ("kt", l, b))
                own_read(("kt", l, 3))
                act.sem_inc(s_kt, 1)

            def first_state(l):
                if l > 0:
                    act.wait_ge(s_s1out, 16 * l)
                for b in range(2):
                    ps = await_use(act, ("s0", l, b))
                    freed(act.activation(s0b[:, 4 * b:4 * b + 4, :], ps[:, :].rearrange("p (a n) -> p a n", a=4), ACT.Copy),
                          ("s0", l, b))
                own_read(("s0", l, 1))
                act.sem_inc(s_s0, 1)

            def load_state(l, hd):
                act.dma_start(STB[hd % 2], sh_in[l, hd].rearrange("p b n -> p (b n)")).then_inc(s_state[hd % 2], 16)

            def heads_out(l):
                act.wait_ge(s_kq, 2 * l + 2)
                load_state(l, 0)
                load_state(l, 1)
                for b in range(4):
                    ps = await_use(act, ("o", l, b))
                    freed(act.activation(V[:, 2 * b:2 * b + 2, 0:TP], ps[:, :].rearrange("p (a n) -> p a n", a=2), ACT.Copy),
                          ("o", l, b))

            def sample_kv(l):
                for b in range(4):
                    ps = await_use(act, ("kvs", l, b))
                    freed(act.activation((KS, VS)[b // 2][:, (b % 2) * 512:(b % 2 + 1) * 512], ps[0:TS, :], ACT.Copy),
                          ("kvs", l, b))
                own_read(("kvs", l, 3))
                act.sem_inc(s_kvs, 1)

            def next_state(l, hd):
                if hd == 0:
                    act.wait_ge(s_s1, l + 1)
                    act.dma_start(hp_out[l], s0b[:, :, :]).then_inc(s_s1out, 16)
                if hd >= 2:
                    act.wait_ge(s_ssout[hd % 2], 16 * ((HEADS * l + hd) // 2))
                    load_state(l, hd)

            def sample_out(l, hd):
                act.wait_ge(s_sn, HEADS * l + hd + 1)
                act.dma_start(hs_out[l, hd].rearrange("p b n -> p (b n)"), STB[hd % 2]).then_inc(s_ssout[hd % 2], 16)
                ps = await_use(act, ("os", l, hd, 0))
                freed(act.activation(V[:, hd, TP:T], ps[:, 0:TS], ACT.Copy), ("os", l, hd, 0))

            stages = {"att": levels, "vt": values, "kt": keys, "s0": first_state, "o": heads_out,
                      "s1": lambda l: None, "kvs": sample_kv, "kv": next_state, "os": sample_out}

            act.wait_ge(s_c, 16)
            act.activation(cT[:, :, :], cT[:, :, :], ACT.Silu).then_inc(s_cact, 1)
            act.wait_ge(s_in, 32)
            act.activation(as_kt(X1), x[:, :, :], ACT.Square).then_inc(s_sq, 1)
            act.wait_ge(s_lbx, 1)
            act.activation(lsm[:, 1:3, :], lsm[:, 1:3, :], ACT.Exp).then_inc(s_lbe, 1)
            modulation(0, 0)
            act.wait_ge(s_const, 2)
            for l in range(LAYERS):
                if l > 0:
                    act.wait_ge(s_x, 2 * l)
                    act.activation(as_kt(X1), x[:, :, :], ACT.Square).then_inc(s_sq, 1)
                    modulation(1, 1)
                inverse_root(("n1", l), row[:, 0, :], s_rstd)
                if l > 0:
                    modulation(1, 2)
                    act.wait_ge(s_csout, 32 * l)
                    for n in range(2):
                        act.wait_ge(s_ssout[n], 64 * l)
                for t in range(KT):
                    ps = await_use(act, ("f", l, t))
                    act.activation(F[:, t, :], ps[:, 0:T], ACT.Sigmoid)
                    freed(act.activation(K[:, t, :], ps[:, 0:T], ACT.Sigmoid, scale=-1.0), ("f", l, t))
                for t in range(KT):
                    ps = await_use(act, ("q", l, t))
                    freed(act.activation(Q[:, t, :], ps[:, 0:T], ACT.Silu), ("q", l, t))
                    if t == 3:
                        act.wait_ge(s_fg, l + 1)
                        act.activation(B[:, :, 0:TP], F[:, :, 0:TP], ACT.Ln).then_inc(s_ln, 1)
                for t in range(KT):
                    ps = await_use(act, ("i", l, t))
                    freed(act.activation(V[:, t, :], ps[:, 0:T], ACT.Copy), ("i", l, t))
                    if t == 0:
                        own_read(("i", l, 0))
                        act.sem_inc(s_qv, 1)
                level_exp(l, 1)
                for r, (g, t) in enumerate(REST):
                    name = (g, l, t)
                    if g != "za":
                        dst, func = {"zb": (SBZ, ACT.Sigmoid), "g": (SG, ACT.Silu), "ga": (GA, ACT.Sigmoid),
                                     "gb": (GB, ACT.Sigmoid)}[g]
                        ps = await_use(act, name)
                        if name == ("gb", l, KT - 1):
                            act.wait_ge(s_pconv, (l + 1) * CW * len(POOL_CONV))
                        freed(act.activation(dst[:, t, :], ps[:, 0:T], func), name)
                        if g == "zb":
                            own_read(name)
                            act.sem_inc(s_zb, 1)
                        if name == ("gb", l, KT - 1):
                            own_read(name)
                            act.sem_inc(s_sgr, 1)
                    for stage in STAGES.get(r, ()):
                        stages[stage[0]](l, *stage[1:])
                own_read(("os", l, HEADS - 1, 0))
                act.activation(as_kt(X1), V, ACT.Square).then_inc(s_osq, 1)
                for hd in range(HEADS):
                    log_mean(("hn", l, hd), as_kt(X0)[:, hd, :], 1.0 / P)
                act.activation(X0, X0, ACT.Exp, scale=-0.5).then_inc(s_hn, 1)
                if l == 0:
                    modulation(0, 1)
                ps = await_use(act, ("mu", l))
                freed(act.activation(row[:, 0, :], ps[:, 0:T], ACT.Copy, scale=1.0 / D), ("mu", l))
                own_read(("mu", l))
                act.sem_inc(s_mu, 1)
                act.wait_ge(s_xc, l + 1)
                act.activation(as_kt(DEC), SBZ, ACT.Square).then_inc(s_sq, 1)
                inverse_root(("var", l), row[:, 1, :], s_rstd)
                act.wait_ge(s_lnn, l + 1)
                for t in range(KT):
                    ins = act.activation(SBZ[:, t, :], SBZ[:, t, :], ACT.Silu, bias=par_of("lnb", l)[:, t:t + 1],
                                         scale=par_of("lng", l)[:, t:t + 1])
                ins.then_inc(s_yb, 1)
                act.wait_ge(s_x, 2 * l + 1)
                act.activation(as_kt(X1), x[:, :, :], ACT.Square).then_inc(s_sq, 1)
                if l == 0:
                    modulation(0, 2)
                inverse_root(("n2", l), row[:, 0, :], s_rstd)
                act.sem_inc(s_sq, 1)
                if l == 0:
                    modulation(1, 0)
                    for j in range(FT):
                        if j >= 2:
                            act.wait_ge(s_hid, j - 1)
                        ps = await_use(act, ("fg", j))
                        freed(act.activation(SILU[j % 2], ps[:, 0:T], ACT.Silu), ("fg", j))
                        own_read(("fg", j))
                        act.sem_inc(s_gsilu, 1)
            for b in range(6):
                tt, half = divmod(b, 2)
                tn = TT[tt][1]
                ps = await_use(act, ("tok", b))
                ins = act.activation(H2TOK[0:tn, tt, half * 512:(half + 1) * 512], ps[0:tn, :], ACT.Copy)
                freed(ins, ("tok", b))
            name = ("tok", 5)
            act.wait_ge(psum_read[USE[name] % BANKS], USE[name] // BANKS + 1)
            act.sem_inc(s_tok, 1)
            act.wait_ge(s_lg, 1)
            act.activation(rt[:, :, 36:37], rt[:, :, 36:37], ACT.Exp).then_inc(s_rex, 1)

            def expert(turn, s):
                base = MOE_USE0 + s * MOE_USES

                def full(n):
                    act.wait_ge(psum_full, turn * (2 * MOE_USES) + base + n + 1)
                    return banks[(base + n) % BANKS]

                for half in range(2):
                    ps = full(half)
                    act.activation(H2G[s][:, half * 512:(half + 1) * 512], ps[:, :], ACT.Copy)\
                        .then_inc(psum_read[(base + half) % BANKS], 1)
                ps = full(2)
                act.activation(SCT[s], ps[:, 0:T], ACT.Copy).then_inc(psum_read[(base + 2) % BANKS], 1)
                act.wait_ge(psum_read[(base + 2) % BANKS],
                            turn * (2 * MOE_USES // BANKS) + (base + 2) // BANKS + 1)
                act.sem_inc(m_h2g, 1)
                act.sem_inc(m_sct, 1)
                for j in range(FT // 2):
                    ps = full(3 + j)
                    if s > 0 or j >= 2:
                        act.wait_ge(m_hid, (2 * turn + s) * (FT // 2) + j - 1)
                    gates = ps[:, :].rearrange("p (a b n) -> p a b n", a=2, b=2)[:, :, 0, :]
                    act.activation(MSILU[j % 2].rearrange("p (a n) -> p a n", a=2), gates, ACT.Silu).then_inc(m_silu, 1)
                for half in range(2):
                    n = 3 + FT // 2 + half
                    ps = full(n)
                    act.activation(YE[:, half * 512:(half + 1) * 512], ps[:, :], ACT.Copy)\
                        .then_inc(psum_read[(base + n) % BANKS], 1)
                    act.wait_ge(psum_read[(base + n) % BANKS],
                                turn * (2 * MOE_USES // BANKS) + (base + n) // BANKS + 1)
                    act.sem_inc(m_y, 1)

            act.wait_ge(s_csout, 32 * LAYERS)
            with act.Fori(0, NE // 2) as pair:
                for s in range(2):
                    expert(pair, s)
            act.wait_ge(s_flag, 2)
            more = act.value_load(flag[0:1, 0:1], min_val=0, max_val=1)
            with act.If(more > 0):
                with act.Fori(1, 3) as rnd:
                    with act.Fori(0, NE // 2) as pair:
                        for s in range(2):
                            expert(rnd * (NE // 2) + pair, s)
            act.wait_ge(f_x, 1)
            act.activation(as_kt(X1), x[:, :, :], ACT.Square).then_inc(f_sq, 1)
            act.wait_ge(f_st, 1)
            act.activation(row[:, 0, :], banks[0][:, 0:T], ACT.Ln, bias=eps_col[:, 0:1], scale=1.0 / D).then_inc(f_rt, 1)
            act.wait_ge(f_rt, 1)
            act.activation(row[:, 0, :], row[:, 0, :], ACT.Exp, scale=-0.5).then_inc(f_rt, 1)

        @block.gpsimd
        def _(pool):
            steps = [0]

            def link(ins):
                steps[0] += 1
                ins.then_inc(s_pool, 1)
                pool.wait_ge(s_pool, steps[0])

            link(pool.memset(ident[:, :], 0.0))
            pool.affine_select(out=ident[:, :], in_=ident[:, :], compare_op=ALU.not_equal, fill=1.0,
                               base=0, pattern=[[-1, P]], channel_multiplier=1).then_inc(s_const, 1)
            pool.wait_ge(s_const, 1)
            pool.memset(eps_col[:, :], EPS)
            pool.memset(ones[:, :], 1.0)
            mf = as_kt(X0)[:, :, 0:P]
            link(pool.memset(mf, 0.0))
            link(pool.tensor_copy(mf[:, 0, :], ident[:, :]))
            for n, m in enumerate(SPANS):
                second = mf[:, n + 1, :].rearrange("p (n a m) -> p n a m", a=2, m=m)[:, :, 1, :]
                link(pool.memset(second, 1.0))
                blocks = P // (2 * m)
                link(pool.affine_select(out=second, in_=second, compare_op=ALU.is_ge, fill=0.0, base=0,
                                        pattern=[[-2 * m, blocks], [0, m]], channel_multiplier=1))
                link(pool.affine_select(out=second, in_=second, compare_op=ALU.is_ge, fill=0.0, base=m - 1,
                                        pattern=[[2 * m, blocks], [0, m]], channel_multiplier=-1))
            link(pool.tensor_copy(masks[:, :, :], mf))
            link(pool.memset(ubuf[:, :, 0:PAST], 0.0))
            pool.memset(ubuf[:, 0, 0:1], 0.0).then_inc(s_const, 1)
            taps = [0]
            for l in range(LAYERS):
                if l > 0:
                    pool.wait_ge(s_csout, 32 * l)
                    pool.wait_ge(s_cv, l)
                pool.dma_start(sconv[:, :, :, :], sc_in[l]).then_inc(s_sconv, 16)
                pool.wait_ge(s_fg, l + 1)
                pool.memset(attb[:, :, :], 0.0).then_inc(s_att0, 1)
                pool.wait_ge(s_glu, l + 1)
                cw = par_of("cw", l).rearrange("p (k j) -> p k j", j=CW)
                pool.dma_start(cp_out[l], ubuf[:, :, TP:TP + PAST]).then_inc(s_csout, 16)
                pool.wait_ge(s_sconv, 16 * (l + 1))
                snew = SNEW.rearrange("p (k b j) -> p k b j", b=TS, j=PAST)
                sv = sconv[:, :, :, :].rearrange("p k b j -> p (k b) j")
                snv = SNEW.rearrange("p (n j) -> p n j", j=PAST)
                pool.tensor_copy(snv[:, :, 0:PAST - 1], sv[:, :, 1:PAST])
                link(pool.tensor_copy(snew[:, :, :, PAST - 1], us[:, :, :]))
                pool.dma_start(cs_out[l], SNEW).then_inc(s_csout, 16)
                pool.tensor_tensor(sconv[:, :, :, :], sconv[:, :, :, :],
                                   bc(cw[:, :, 0:PAST], 2, [P, KT, TS, PAST]), ALU.mult).then_inc(s_cs, 1)
                for j in range(CW):
                    for n, t in enumerate(POOL_CONV):
                        win = ubuf[:, t, j:j + TP]
                        acc = SBZ[:, t, 0:TP]
                        if j == 0:
                            pool.tensor_scalar(acc, win, cw[:, t, 0:1], par_of("cb", l)[:, t:t + 1], ALU.mult, ALU.add)\
                                .then_inc(s_pconv, 1)
                            taps[0] += 1
                            continue
                        prod = GB[:, KT - 1, 0:TP]
                        pool.wait_ge(s_pconv, taps[0])
                        link(pool.tensor_scalar(prod, win, cw[:, t, j:j + 1], None, ALU.mult))
                        pool.tensor_tensor(acc, acc, prod, ALU.add).then_inc(s_pconv, 1)
                        taps[0] += 1
                diag = bc(ident[0:TS, 0:TS], 2, [TS, TS, P])
                pool.wait_ge(s_kvs, l + 1)
                pool.wait_ge(s_s1, l + 1)
                for hd in range(HEADS):
                    if hd >= 2:
                        pool.wait_ge(psum_full, USE[("kv", l, hd - 2, 1)] + 1)
                    vd = VD[hd % 2].rearrange("p (b n) -> p b n", b=TS)
                    pool.tensor_tensor(vd, diag, bc(VS[:, hd * P:(hd + 1) * P], 1, [TS, TS, P]), ALU.mult)\
                        .then_inc(s_vd, 1)
                if l == LAYERS - 1:
                    pool.wait_ge(s_on, LAYERS)
                    link(pool.memset(TRI, 1.0))
                    link(pool.affine_select(out=TRI, in_=TRI, compare_op=ALU.is_gt, fill=0.0, base=0,
                                            pattern=[[1, P]], channel_multiplier=-1))
                    pool.iota(IOTA, pattern=[[1, P]], base=0, channel_multiplier=0,
                              allow_small_or_imprecise_dtypes=True).then_inc(s_const, 1)

        @block.vector
        def _(dve):
            steps = [0]

            def link(ins):
                steps[0] += 1
                ins.then_inc(s_dve, 1)
                dve.wait_ge(s_dve, steps[0])

            def done(signal):
                link(dve.memset(scratch[:, :], 0.0))
                dve.sem_inc(signal, 1)

            def own_read(name):
                dve.wait_ge(psum_read[USE[name] % BANKS], USE[name] // BANKS + 1)

            dve.wait_ge(s_in, 32)
            lb0, lb1 = par_of("lb", 0), par_of("lb", 1)
            link(dve.tensor_tensor(lsm[:, 0, :], lb0, lb1, ALU.max))
            dve.tensor_tensor(lsm[:, 1, :], lb0, lsm[:, 0, :], ALU.subtract)
            dve.tensor_tensor(lsm[:, 2, :], lb1, lsm[:, 0, :], ALU.subtract).then_inc(s_lbx, 1)
            dve.wait_ge(s_lbe, 1)
            link(dve.tensor_tensor(lsm[:, 3, :], lsm[:, 1, :], lsm[:, 2, :], ALU.add))
            link(dve.reciprocal(lsm[:, 3, :], lsm[:, 3, :]))
            dve.tensor_tensor(lsm[:, 1, :], lsm[:, 1, :], lsm[:, 3, :], ALU.mult)
            link(dve.tensor_tensor(lsm[:, 2, :], lsm[:, 2, :], lsm[:, 3, :], ALU.mult))
            dve.tensor_tensor(lbt[:, 0, 0, :], lsm[:, 1, :], lsm[:, 1, :], ALU.subtract)
            link(dve.tensor_tensor(lsm[:, 3, :], lsm[:, 1, :], lsm[:, 2, :], ALU.add))
            link(dve.tensor_tensor(lbt[:, 0, 1, :], lsm[:, 3, :], lsm[:, 1, :], ALU.subtract))
            link(dve.tensor_scalar(lbt[:, 1, :, :], lbt[:, 0, :, :], -1.0, 1.0, ALU.mult, ALU.add))

            def modulation(l, pair):
                for g in range(4):
                    name = ("mt", l, pair, g)
                    ps = await_use(dve, name)
                    part = slice(16 * pair + 4 * g, 16 * pair + 4 * g + 4)
                    ins = dve.tensor_tensor(modt[:, l, part, :], ps[:, 0:4 * NC_TOK].rearrange("p (a n) -> p a n", a=4),
                                            bc(par_of("ada_b", l)[:, part], 2, [P, 4, NC_TOK]), ALU.add)
                    freed(ins, name)
                    own_read(name)
                    dve.sem_inc(s_mod, 1)

            def shift(l, part):
                return modt[:, l, part * KT:(part + 1) * KT, :]

            def modulated_norm(l, gain, sh, sc, roots, before_roots=None):
                g = bc(gain, 2, [P, KT, NC_TOK])
                link(dve.scalar_tensor_tensor(sc1g[:, :, :], shift(l, sc), 1.0, g, ALU.add, ALU.mult))
                for t in range(KT):
                    dve.tensor_scalar(h[:, t, 0:TP], x[:, t, 0:TP], sc1g[:, t, 0:1], None, ALU.mult)
                link(dve.tensor_tensor(h[:, :, TP:T], x[:, :, TP:T], sc1g[:, :, 1:NC_TOK], ALU.mult))
                if before_roots is not None:
                    before_roots()
                dve.wait_ge(s_rstd, roots)
                for t in range(KT):
                    link(dve.tensor_tensor(h[:, t, :], h[:, t, :], row[:, 0, :], ALU.mult))
                    dve.tensor_scalar(h[:, t, 0:TP], h[:, t, 0:TP], shift(l, sh)[:, t, 0:1], None, ALU.add)
                    dve.tensor_tensor(h[:, t, TP:T], h[:, t, TP:T], shift(l, sh)[:, t, 1:NC_TOK], ALU.add).then_inc(s_h, 1)

            def residual(name, l, part, t, width=T):
                ps = await_use(dve, name)
                gate = shift(l, part)
                dve.scalar_tensor_tensor(x[:, t, 0:TP], ps[:, 0:TP], gate[:, t, 0:1], x[:, t, 0:TP], ALU.mult, ALU.add)
                freed(dve.tensor_tensor(small[:, t * TS:(t + 1) * TS], ps[:, TP:T], gate[:, t, 1:NC_TOK], ALU.mult), name)

            def residual_samples(signal):
                dve.wait_ge(psum_read[last_use[0] % BANKS], last_use[0] // BANKS + 1)
                dve.tensor_tensor(x[:, :, TP:T], x[:, :, TP:T], small[:, :].rearrange("p (k b) -> p k b", b=TS), ALU.add)\
                    .then_inc(signal, 1)

            last_use = [0]
            taps = [0]
            modulation(0, 0)
            for l in range(LAYERS):
                modulated_norm(l, par_of("n1", l), 0, 1, 3 * l + 1, (lambda: modulation(1, 2)) if l == 1 else None)
                for t in range(KT):
                    name = ("f", l, t)
                    dve.wait_ge(psum_read[USE[name] % BANKS], USE[name] // BANKS + 1)
                    dve.tensor_scalar(F[:, t, :], F[:, t, :], lbt[:, 1, l, t:t + 1], lbt[:, 0, l, t:t + 1], ALU.mult, ALU.add)
                    ins = dve.tensor_scalar(K[:, t, :], K[:, t, :], lbt[:, 1, l, t:t + 1], None, ALU.mult)
                link(ins)
                link(dve.tensor_scalar(F, F, 2.0 ** -63, None, ALU.max))
                dve.tensor_copy(fs[:, :, :], F[:, :, TP:T]).then_inc(s_fg, 1)
                dve.wait_ge(s_ln, l + 1)
                for hd in range(HEADS):
                    for c in range(NCH):
                        tok = slice(c * CH, (c + 1) * CH)
                        ins = dve.tensor_tensor_scan(B[:, hd, tok], ones[:, :], B[:, hd, tok], 0.0, ALU.mult, ALU.add)
                link(ins)

                def level_exponents(n):
                    m = SPANS[n - 1]
                    first, second = levels_view(B, m)
                    d1, d2 = levels_view(as_kt(DEC), m)
                    nb = TP // (2 * m)
                    ref = first[:, :, :, m - 1:m].broadcast_to([P, HEADS, nb, m])
                    dve.tensor_tensor(d1, ref, first, ALU.subtract)
                    dve.tensor_tensor(d2, second, ref, ALU.subtract).then_inc(s_dif, 1)

                def level_operands(n):
                    m = SPANS[n - 1]
                    d1, d2 = levels_view(as_kt(DEC), m)
                    k1 = levels_view(K, m)[0]
                    q2 = levels_view(Q, m)[1]
                    x1, x2 = levels_view(as_kt(Xb[n % 2]), m)
                    if n >= 3:
                        dve.wait_ge(psum_full, USE[("att", l, n - 2, 3)] + 1)
                    dve.wait_ge(s_exp, 8 * l + n)
                    dve.tensor_tensor(x1, d1, k1, ALU.mult)
                    dve.tensor_tensor(x2, d2, q2, ALU.mult).then_inc(s_xl, 1)
                    dve.wait_ge(s_xl, 7 * l + n)

                level_exponents(1)
                dve.wait_ge(s_qv, l + 1)
                level_operands(1)
                dve.wait_ge(s_att0, l + 1)
                cw = par_of("cw", l).rearrange("p (k j) -> p k j", j=CW)

                def conv_taps(l=l, cw=cw):
                    for j in range(CW):
                        for t in DVE_CONV:
                            win, acc = ubuf[:, t, j:j + TP], SBZ[:, t, 0:TP]
                            if j == 0:
                                ins = dve.tensor_scalar(acc, win, cw[:, t, 0:1], par_of("cb", l)[:, t:t + 1], ALU.mult, ALU.add)
                            else:
                                dve.wait_ge(s_conv, taps[0] - len(DVE_CONV) + 1)
                                ins = dve.scalar_tensor_tensor(acc, win, cw[:, t, j:j + 1], acc, ALU.mult, ALU.add)
                            ins.then_inc(s_conv, 1)
                            taps[0] += 1
                            yield

                conv = conv_taps()

                def levels(n, l=l):
                    if 1 <= n < 7:
                        level_exponents(n + 1)
                    for b in range(4):
                        name = ("att", l, n, b)
                        ps = await_use(dve, name)
                        if n > 0:
                            own_read(("att", l, n - 1, b))
                        ins = dve.copy_predicated(attb[:, 4 * b:4 * b + 4, :], bc(masks[:, n, :], 1, [P, 4, P]),
                                                  ps[:, :].rearrange("p (a n) -> p a n", a=4))
                        freed(ins, name)
                    if 1 <= n < 7:
                        level_operands(n + 1)
                    if n == 7:
                        bv = B[:, :, 0:TP].rearrange("p h (c n) -> p h c n", n=CH)
                        dve.tensor_tensor(as_kt(DEC)[:, :, 0:TP].rearrange("p h (c n) -> p h c n", n=CH),
                                          bv[:, :, :, CH - 1:CH].broadcast_to([P, HEADS, NCH, CH]), bv, ALU.subtract)\
                            .then_inc(s_dif, 1)
                        done(s_att)

                def decayed(l=l):
                    dve.wait_ge(s_exp, 8 * l + 8)
                    dve.tensor_tensor(as_kt(X0)[:, :, 0:TP], as_kt(DEC)[:, :, 0:TP], K[:, :, 0:TP], ALU.mult).then_inc(s_kq, 1)
                    dve.wait_ge(s_eb, l + 1)
                    dve.tensor_tensor(Q[:, :, CH:TP], Q[:, :, CH:TP], B[:, :, CH:TP], ALU.mult).then_inc(s_kq, 1)

                def final_state(l=l):
                    for b in range(2):
                        name = ("s1", l, b)
                        ps = await_use(dve, name)
                        for s in range(4):
                            hd = 4 * b + s
                            ins = dve.scalar_tensor_tensor(s0b[:, hd, :], s0b[:, hd, :], ebl[:, hd, 1:2],
                                                           ps[:, s * P:(s + 1) * P], ALU.mult, ALU.add)
                        freed(ins, name)
                    done(s_s1)

                def sample_state(hd, l=l):
                    st = STB[hd % 2]
                    dve.wait_ge(s_state[hd % 2], 16 * ((HEADS * l + hd) // 2 + 1))
                    for half in range(2):
                        name = ("kv", l, hd, half)
                        ps = await_use(dve, name)
                        for b4 in range(4):
                            b = 4 * half + b4
                            ins = dve.scalar_tensor_tensor(st[:, b * P:(b + 1) * P], st[:, b * P:(b + 1) * P],
                                                           fs[:, hd, b:b + 1], ps[:, b4 * P:(b4 + 1) * P], ALU.mult, ALU.add)
                        freed(ins, name)
                    done(s_sn)

                stages = {"att": levels, "vt": decayed, "s1": final_state, "kv": sample_state}
                for r, (g, t) in enumerate(REST):
                    if g == "za":
                        name = ("za", l, t)
                        ps = await_use(dve, name)
                        dve.wait_ge(s_zb, KT * l + t + 1)
                        dve.tensor_tensor(ubuf[:, t, PAST:PAST + TP], ps[:, 0:TP], SBZ[:, t, 0:TP], ALU.mult)
                        ins = dve.tensor_tensor(us[:, t, :], ps[:, TP:T], SBZ[:, t, TP:T], ALU.mult)
                        freed(ins, name)
                        if t == KT - 1:
                            done(s_glu)
                    for stage in STAGES.get(r, ()):
                        if stage[0] in stages:
                            stages[stage[0]](*stage[1:])
                    if r >= 2 * KT:
                        for _ in range(3 if r < 24 else 7):
                            next(conv, None)
                dve.wait_ge(s_sgr, l + 1)
                for _ in range(20):
                    next(conv, None)
                dve.wait_ge(s_hn, l + 1)
                link(dve.tensor_tensor(V, V, as_kt(X0), ALU.mult))
                for hd in range(HEADS):
                    ins = dve.scalar_tensor_tensor(V[:, hd, :], V[:, hd, :], par_of("hgn", l)[:, hd:hd + 1], SG[:, hd, :],
                                                   ALU.mult, ALU.mult)
                ins.then_inc(s_on, 1)
                if l == 0:
                    for _ in conv:
                        pass
                    modulation(0, 1)
                for t in range(KT):
                    for _ in range(9):
                        next(conv, None)
                    name = ("ya", l, t)
                    ps = await_use(dve, name)
                    freed(dve.tensor_tensor(GA[:, t, :], ps[:, 0:T], GA[:, t, :], ALU.mult), name)
                    if t == 3:
                        dve.wait_ge(s_cs, l + 1)
                        link(dve.tensor_reduce(small[:, :], sconv[:, :, :, :].rearrange("p k b j -> p (k b) j"), AX, ALU.add))
                        sm = small[:, :].rearrange("p (k b) -> p k b", b=TS)
                        link(dve.tensor_tensor(us[:, :, :], us[:, :, :], cw[:, :, CW - 1:CW].broadcast_to([P, KT, TS]), ALU.mult))
                        link(dve.tensor_tensor(us[:, :, :], us[:, :, :], sm, ALU.add))
                        dve.tensor_tensor(SBZ[:, :, TP:T], us[:, :, :], bc(par_of("cb", l), 2, [P, KT, TS]), ALU.add)
                for _ in conv:
                    pass
                dve.wait_ge(s_pconv, (l + 1) * CW * len(POOL_CONV))
                done(s_cv)
                dve.wait_ge(s_mu, l + 1)
                dve.tensor_tensor(SBZ, SBZ, bc(row[:, 0, :], 1, [P, KT, T]), ALU.subtract).then_inc(s_xc, 1)
                dve.wait_ge(s_rstd, 3 * l + 2)
                dve.tensor_tensor(SBZ, SBZ, bc(row[:, 1, :], 1, [P, KT, T]), ALU.mult).then_inc(s_lnn, 1)
                for t in range(KT):
                    name = ("yb", l, t)
                    ps = await_use(dve, name)
                    freed(dve.tensor_tensor(GB[:, t, :], ps[:, 0:T], GB[:, t, :], ALU.mult), name)
                    if t % 4 == 3:
                        own_read(name)
                        ins = dve.tensor_tensor(GA[:, t - 3:t + 1, :], GA[:, t - 3:t + 1, :], GB[:, t - 3:t + 1, :], ALU.add)
                ins.then_inc(s_mix, 1)
                for t in range(KT):
                    residual(("wo", l, t), l, 2, t)
                last_use[0] = USE[("wo", l, KT - 1)]
                residual_samples(s_x)
                dve.wait_ge(s_x, 2 * l + 1)
                if l == 0:
                    modulation(0, 2)
                modulated_norm(l, par_of("n2", l), 3, 4, 3 * l + 3)
                if l == 0:
                    modulation(1, 0)
                    for j in range(FT):
                        ps = await_use(dve, ("fu", j))
                        dve.wait_ge(s_gsilu, j + 1)
                        freed(dve.tensor_tensor(HID[:, j, :], ps[:, 0:T], SILU[j % 2], ALU.mult), ("fu", j))
                        own_read(("fu", j))
                        dve.sem_inc(s_hid, 1)
                    for t in range(KT):
                        residual(("fd", t), 0, 5, t)
                    last_use[0] = USE[("fd", KT - 1)]
                    residual_samples(s_x)
                    dve.wait_ge(s_x, 2)
                    modulation(1, 1)

            dve.wait_ge(s_tok, 1)
            for tt in range(3):
                link(dve.memset(rt[:, tt, :], 0.0))
            ps = await_use(dve, ("lg",))
            dve.tensor_copy(rt[:, 0:2, 0:NE], ps[:, 0:2 * NE].rearrange("p (a n) -> p a n", a=2))
            freed(dve.tensor_copy(rt[0:TS, 2, 0:NE], ps[0:TS, 2 * NE:3 * NE]), ("lg",))
            link(dve.memset(FACC, 0.0))
            for tt in range(3):
                link(dve.max(rt[:, tt, 24:32], rt[:, tt, 0:NE]))
                link(dve.max_index(rt[:, tt, 56:64].bitcast(u32), rt[:, tt, 24:32], rt[:, tt, 0:NE]))
            link(dve.tensor_copy(rt[:, :, 32:34], rt[:, :, 56:58].bitcast(u32)))
            dve.tensor_tensor(rt[:, :, 36:37], rt[:, :, 25:26], rt[:, :, 24:25], ALU.subtract).then_inc(s_lg, 1)
            dve.wait_ge(s_rex, 1)
            link(dve.tensor_scalar(rt[:, :, 34:35], rt[:, :, 36:37], 1.0, None, ALU.add))
            link(dve.reciprocal(rt[:, :, 34:35], rt[:, :, 34:35]))
            link(dve.tensor_tensor(rt[:, :, 35:36], rt[:, :, 36:37], rt[:, :, 34:35], ALU.mult))
            dve.wait_ge(s_const, 3)
            for tt in range(3):
                dve.tensor_scalar(rt[:, tt, 40:48], IOTA[:, 0:NE], rt[:, tt, 32:33], None, ALU.is_equal)
                dve.tensor_scalar(rt[:, tt, 48:56], IOTA[:, 0:NE], rt[:, tt, 33:34], None, ALU.is_equal)
                dve.tensor_scalar(rt[:, tt, 64:72], IOTA[:, 0:NE], rt[:, tt, 32:33], rt[:, tt, 34:35], ALU.is_equal, ALU.mult)
                dve.tensor_scalar(rt[:, tt, 72:80], IOTA[:, 0:NE], rt[:, tt, 33:34], rt[:, tt, 35:36], ALU.is_equal, ALU.mult)
            link(dve.memset(scratch[:, :], 0.0))
            dve.tensor_tensor(rt[:, :, 16:24], rt[:, :, 64:72], rt[:, :, 72:80], ALU.add)
            dve.tensor_tensor(rt[:, :, 8:16], rt[:, :, 40:48], rt[:, :, 48:56], ALU.add).then_inc(s_sel, 1)
            dve.wait_ge(s_sel, 1)
            ps = await_use(dve, ("pos",))
            link(dve.tensor_scalar(rt[:, :, 40:48], rt[:, :, 8:16], -4096.0, 4096.0, ALU.mult, ALU.add))
            link(dve.memset(PSEL[:, :, :, :], 0.0))
            for tt, (_, tn) in enumerate(TT):
                dve.tensor_tensor(PSEL[0:tn, 0, :, tt], rt[0:tn, tt, 40:48], ps[0:tn, tt * NE:(tt + 1) * NE], ALU.add)
                dve.tensor_copy(PSEL[0:tn, 1, :, tt], rt[0:tn, tt, 16:24])
            freed(dve.tensor_reduce(small[0:1, 0:1], ps[0:1, 3 * NE:4 * NE], AX, ALU.max), ("pos",))
            link(dve.memset(scratch[:, :], 0.0))
            link(dve.tensor_scalar(small[0:1, 2:3], small[0:1, 0:1], float(CAP), None, ALU.is_gt))
            link(dve.tensor_copy(flag[0:1, 0:1], small[0:1, 2:3]))
            dve.sem_inc(s_flag, 2)

            def expert(turn, pair, s):
                base = MOE_USE0 + s * MOE_USES
                own = [s * DVE_STEPS]

                def step(ins, wait=True):
                    own[0] += 1
                    ins.then_inc(m_dve, 1)
                    if wait:
                        dve.wait_ge(m_dve, turn * (2 * DVE_STEPS) + own[0])

                if s == 0:
                    src = PSEL[:, :, bass.ds(pair * 2, 2), :]
                    step(dve.tensor_copy(CUR[:, :, :, :], src))
                    step(dve.tensor_scalar(PSEL[:, 0, bass.ds(pair * 2, 2), :], PSEL[:, 0, bass.ds(pair * 2, 2), :],
                                           float(-CAP), None, ALU.add))
                else:
                    step(dve.memset(scratch[:, :], 0.0))
                    step(dve.memset(scratch[:, :], 0.0))
                for tt in range(3):
                    step(dve.tensor_scalar(SEL[s][:, tt, :], IOTA, CUR[:, 0, s, tt:tt + 1], None, ALU.is_equal), False)
                    step(dve.tensor_scalar(SELC[s][:, tt, :], IOTA, CUR[:, 0, s, tt:tt + 1], CUR[:, 1, s, tt:tt + 1],
                                           ALU.is_equal, ALU.mult), False)
                dve.wait_ge(m_dve, turn * (2 * DVE_STEPS) + own[0])
                dve.sem_inc(m_sel, 1)
                for j in range(FT // 2):
                    n = base + 3 + j
                    dve.wait_ge(psum_full, turn * (2 * MOE_USES) + n + 1)
                    dve.wait_ge(m_silu, (2 * turn + s) * (FT // 2) + j + 1)
                    ups = banks[n % BANKS][:, :].rearrange("p (a b n) -> p a b n", a=2, b=2)[:, :, 1, :]
                    dve.tensor_tensor(MHID[:, 2 * j:2 * j + 2, :], ups, MSILU[j % 2].rearrange("p (a n) -> p a n", a=2), ALU.mult)\
                        .then_inc(psum_read[n % BANKS], 1)
                    dve.wait_ge(psum_read[n % BANKS], turn * (2 * MOE_USES // BANKS) + n // BANKS + 1)
                    dve.sem_inc(m_hid, 1)
                for t in range(KT):
                    n = base + 5 + FT // 2 + t
                    dve.wait_ge(psum_full, turn * (2 * MOE_USES) + n + 1)
                    dve.tensor_tensor(FACC[:, t, :], FACC[:, t, :], banks[n % BANKS][:, 0:T], ALU.add)\
                        .then_inc(psum_read[n % BANKS], 1)
                assert own[0] == (s + 1) * DVE_STEPS, own[0]

            with dve.Fori(0, NE // 2) as pair:
                for s in range(2):
                    expert(pair, pair, s)
            more = dve.value_load(flag[0:1, 0:1], min_val=0, max_val=1)
            with dve.If(more > 0):
                with dve.Fori(1, 3) as rnd:
                    with dve.Fori(0, NE // 2) as pair:
                        for s in range(2):
                            expert(rnd * (NE // 2) + pair, pair, s)
            fsteps = [0]

            def flink(ins):
                fsteps[0] += 1
                ins.then_inc(f_dve, 1)
                dve.wait_ge(f_dve, fsteps[0])

            flink(dve.memset(scratch[:, :], 0.0))
            flink(dve.tensor_tensor(FACC[:, :, TP:T], FACC[:, :, TP:T], shift(1, 5)[:, :, 1:NC_TOK], ALU.mult))
            for t in range(KT):
                dve.scalar_tensor_tensor(x[:, t, 0:TP], FACC[:, t, 0:TP], shift(1, 5)[:, t, 0:1], x[:, t, 0:TP], ALU.mult, ALU.add)
            dve.tensor_tensor(x[:, :, TP:T], x[:, :, TP:T], FACC[:, :, TP:T], ALU.add).then_inc(f_x, 1)
            dve.wait_ge(f_rt, 2)
            for t in range(KT):
                flink(dve.scalar_tensor_tensor(as_kt(X0)[:, t, :], x[:, t, :], par_of("fin")[:, t:t + 1], row[:, 0, :], ALU.mult, ALU.mult))
            dve.sem_inc(f_y, 1)


def kernel(**inputs):
    import numpy as np
    import concourse.bacc as bacc
    from concourse.bass_utils import run_bass_kernel_spmd

    f32 = np.float32
    a = {k: np.asarray(v) for k, v in inputs.items()}

    def tiles(v):
        v = v.reshape(v.shape[:-1] + (v.shape[-1] // P, P))
        return np.moveaxis(v, -1, 0)

    def fmajor(v):
        return np.ascontiguousarray(v.reshape(v.shape[0], KT, P).transpose(2, 1, 0))

    def col_tiles(w, ts=None):
        k, n = w.shape
        v = w.reshape(k // P, P, n // P, P).transpose(2, 0, 1, 3)
        return v if ts is None else v[ts]

    def slots(blocks):
        return blocks.reshape(-1, SLOT_BLOCKS, P, P).transpose(0, 2, 1, 3).reshape(-1, P, SLOT_W)

    flat = lambda v: v.reshape(-1, P, P)

    def ada(l, pair):
        w = a["ada_w"][l][:, 2048 * pair:2048 * (pair + 1)].reshape(KT, P, 4, 4, P)
        return flat(w.transpose(2, 0, 3, 1, 4))

    def ffn_up(g, u):
        return flat(np.stack([col_tiles(g), col_tiles(u)], axis=1))

    seq = [ada(0, 0)]
    cols = {"q": 0, "f": 1, "i": 2, "g": 3, "za": 4, "zb": 5, "ga": 6, "gb": 7}
    for l in range(LAYERS):
        if l == 1:
            seq.append(ada(1, 2))
        for g in ("f", "q", "i", "zb", "za", "g", "ga", "gb"):
            seq.append(flat(col_tiles(a["w_in"][l][:, cols[g] * D:(cols[g] + 1) * D])))
        if l == 0:
            seq.append(ada(0, 1))
        seq += [flat(col_tiles(a[n][l])) for n in ("w_hg_out", "w_conv_out", "w_o")]
        if l == 0:
            seq += [ada(0, 2), ada(1, 0), ffn_up(a["ffn_w_gate"][0], a["ffn_w_up"][0]),
                    flat(col_tiles(a["ffn_w_down"][0])), ada(1, 1)]
    stream = slots(np.concatenate(seq))
    moe = np.empty((NE // 2, 2 * MOE_SLOTS, P, SLOT_W), f32)
    for e in range(NE):
        down = a["moe_w_down"][0, e].reshape(FT, P, KT, P).transpose(0, 2, 1, 3)
        moe[e // 2, (e % 2) * MOE_SLOTS:(e % 2 + 1) * MOE_SLOTS] = slots(
            np.concatenate([ffn_up(a["moe_w_gate"][0, e], a["moe_w_up"][0, e]), flat(down)]))
    cw = a["conv_w"].reshape(LAYERS, CW, KT, P).transpose(3, 0, 2, 1)
    par = np.concatenate([v.reshape(P, -1) for v in (
        tiles(a["ada_b"]), tiles(a["norm1_g"]), tiles(a["norm2_g"]), tiles(a["lb_logits"]), tiles(a["hg_norm_g"]),
        tiles(a["conv_b"]), tiles(a["conv_ln_g"]), tiles(a["conv_ln_b"]), cw, tiles(a["final_norm_g"]),
        a["router_w"][0].reshape(KT, P, NE).transpose(1, 0, 2))], axis=1)
    arrays = {
        "x": fmajor(np.concatenate([a["x_prompt"][0], a["x_sample"][:, 0]])),
        "c": fmajor(np.concatenate([a["c_prompt"], a["c_sample"]])),
        "par": par, "stream": stream, "moe": moe,
        "state_h": a["state_hgrn"].transpose(0, 2, 3, 1, 4),
        "state_c": a["state_conv"].reshape(LAYERS, TS, PAST, KT, P).transpose(0, 4, 3, 1, 2),
    }
    outs = {"y": (P, KT, T), "hp": (LAYERS, P, HEADS, P), "cp": (LAYERS, P, KT, PAST),
            "hs": (LAYERS, HEADS, P, TS, P), "cs": (LAYERS, P, KT, TS, PAST)}
    nc = bacc.Bacc("TRN2", target_bir_lowering=False, num_devices=1)
    arrays = {"in_" + k: np.ascontiguousarray(v) for k, v in arrays.items()}
    ins = [nc.dram_tensor(k, v.shape, mybir.dt.from_np(v.dtype), kind="ExternalInput").ap() for k, v in arrays.items()]
    o = [nc.dram_tensor("out_" + k, v, mybir.dt.float32, kind="ExternalOutput").ap() for k, v in outs.items()]
    trunk_kernel(nc, *ins, *o)
    r = run_bass_kernel_spmd(nc, [arrays], core_ids=[0]).results[0]
    y = r["out_y"].transpose(2, 1, 0).reshape(T, D)
    hp = r["out_hp"].transpose(0, 2, 1, 3)[:, None]
    cp = r["out_cp"].transpose(0, 3, 2, 1).reshape(LAYERS, PAST, D)[:, None]
    hs = r["out_hs"].transpose(0, 3, 1, 2, 4)
    cs = r["out_cs"].transpose(0, 3, 4, 2, 1).reshape(LAYERS, TS, PAST, D)
    return (y[None, 0:TP], y[TP:T, None], hp, cp, hs, cs)
```

```python
import concourse.bass as bass
from concourse import mybir
from contextlib import ExitStack

P = 128
D = 1024
KT = D // P
TP = 256
TS = 8
T = TP + TS
NC_TOK = 1 + TS
LAYERS = 2
HEADS = 8
CH = 128
NCH = TP // CH
HC = HEADS * NCH
CW = 31
PAST = CW - 1
FF = 2816
FT = FF // P
NE = 8
SLOT_BLOCKS = 16
SLOT_W = SLOT_BLOCKS * P
RING = 6
BANKS = 8
EPS = 1e-6
SPANS = [64, 32, 16, 8, 4, 2, 1]
REST = [(g, t) for g in ("zb", "za", "g", "ga", "gb") for t in range(KT)]
STAGES = {3 * n + 2: [("att", n)] for n in range(8)}
STAGES[25] = [("vt",)]
STAGES[26] = [("kt",)]
STAGES[27] = [("s0",)]
STAGES[28] = [("o",)]
STAGES[29] = [("s1",), ("kvs",)]
for _h in range(HEADS + 1):
    STAGES[31 + _h] = ([("kv", _h)] if _h < HEADS else []) + ([("os", _h - 1)] if _h > 0 else [])
STAGE_BANKS = {"att": 4, "vt": 4, "kt": 4, "s0": 2, "o": 4, "s1": 2, "kvs": 4, "kv": 2, "os": 1}
MU_AFTER, VAR_AFTER = 3, 5
CAP = 128
TT = [(0, P), (P, P), (TP, TS)]
POOL_CONV = (7,)
DVE_CONV = tuple(t for t in range(KT) if t not in POOL_CONV)

_at = 0
PAR = {}
for _name, _n in (("ada_b", LAYERS * 48), ("n1", LAYERS * KT), ("n2", LAYERS * KT), ("lb", LAYERS * KT),
                  ("hgn", LAYERS * KT), ("cb", LAYERS * KT), ("lng", LAYERS * KT), ("lnb", LAYERS * KT),
                  ("cw", LAYERS * KT * CW), ("fin", KT), ("rw", KT * NE)):
    PAR[_name] = (_at, _n)
    _at += _n
NPAR = _at


def psum_order():
    def mod(l, pair):
        out.append(("mod", l, pair, 0))
        for g in range(1, 4):
            out.extend([("mod", l, pair, g), ("mt", l, pair, g - 1)])
        out.append(("mt", l, pair, 3))

    out = []
    mod(0, 0)
    for l in range(LAYERS):
        out.append(("n1", l))
        if l == 1:
            mod(1, 2)
        out += [(g, l, t) for g in ("f", "q", "i") for t in range(KT)]
        for r, (g, t) in enumerate(REST):
            out.append((g, l, t))
            for stage in STAGES.get(r, ()):
                out += [(stage[0], l) + stage[1:] + (b,) for b in range(STAGE_BANKS[stage[0]])]
        out += [("hn", l, h) for h in range(HEADS)]
        mod(l, 1)
        for t in range(KT):
            out.append(("ya", l, t))
            if t == MU_AFTER:
                out.append(("mu", l))
            if t == VAR_AFTER:
                out.append(("var", l))
        out += [(g, l, t) for g in ("yb", "wo") for t in range(KT)]
        if l == 0:
            mod(0, 2)
        out.append(("n2", l))
        if l == 0:
            mod(1, 0)
            for j in range(FT):
                out += [("fg", j), ("fu", j)]
            out += [("fd", t) for t in range(KT)]
    out += [("tok", b) for b in range(6)] + [("lg",), ("pos",)]
    return out


USE = {name: n for n, name in enumerate(psum_order())}
MOE_USE0 = len(USE)
CHUNKS = FT // 2
MOE_USES = 2 * CHUNKS + 2 + 4 + KT
SPLIT_RING = 4
AHEAD = 2
LOADED = RING - 1
ROUNDS = 3
GROUP = 4
GROUPS = NE // GROUP
STREAM_SLOTS = (LAYERS * (48 + 64 + 24) * KT + 3 * FT * KT) // SLOT_BLOCKS
MOE_SLOTS = 3 * FT * KT // SLOT_BLOCKS
GROUP_SLOTS = GROUP * MOE_SLOTS
MOD_SLOTS = 16 * KT // SLOT_BLOCKS
SPLIT0 = (8 * KT * KT + 3 * KT * KT) // SLOT_BLOCKS + 2 * MOD_SLOTS
SPLIT1 = SPLIT0 + 3 * MOD_SLOTS + MOE_SLOTS
SPLIT_MODS = ((0, 2), (1, 0), (1, 2))
SPLIT_AT = {(0, 2): SPLIT0, (1, 0): SPLIT0 + MOD_SLOTS, "ffn": SPLIT0 + 2 * MOD_SLOTS, "down": SPLIT0 + 2 * MOD_SLOTS + FT,
            (1, 2): SPLIT0 + 2 * MOD_SLOTS + MOE_SLOTS, ("fqi", 0): MOD_SLOTS, ("fqi", 1): SPLIT1}
FQI_SLOTS = 3 * KT * KT // SLOT_BLOCKS
SPLIT_SLOTS = [SPLIT_AT["fqi", 0] + n for n in range(FQI_SLOTS)] + list(range(SPLIT0, SPLIT1 + FQI_SLOTS))
SPLIT_INDEX = {n: i for i, n in enumerate(SPLIT_SLOTS)}
SLOT_TILES = SLOT_BLOCKS // KT
HI_RING = 5
DVE_STEPS = 3


def trunk_kernel(nc, x_in, c_in, par_in, stream_in, moe_in, sh_in, sc_in,
                 y_out, hp_out, cp_out, hs_out, cs_out):
    fp32, u8, u32, i32 = mybir.dt.float32, mybir.dt.uint8, mybir.dt.uint32, mybir.dt.int32
    ALU = mybir.AluOpType
    ACT = mybir.ActivationFunctionType
    AX = mybir.AxisListType.X
    ctx = ExitStack()
    with ctx:
        def sb(name, shape, dt=fp32):
            return ctx.enter_context(nc.sbuf_tensor(name, shape, dt))

        def sem(name):
            return ctx.enter_context(nc.semaphore(name))

        f32r = mybir.dt.float32r

        def rounded(*shapes):
            with ExitStack() as once:
                return [once.enter_context(nc.sbuf_tensor(name, shape, f32r)) for name, shape in shapes]

        ring_lo, _, h_lo = rounded(("ring_lo", [P, RING, SLOT_W]), ("x_r", [P, KT, T]), ("h_lo", [P, KT, T]))
        ring = sb("ring", [P, RING, SLOT_W])
        x = sb("x", [P, KT, T])
        h = sb("h", [P, KT, T])
        par = sb("par", [P, NPAR])
        modt = sb("modt", [P, LAYERS, 48, NC_TOK])
        sc1g = sb("sc1g", [P, KT, NC_TOK])
        cT = sb("cT", [P, KT, NC_TOK])
        c_halves = sb("c_halves", [P, KT, 2 * NC_TOK], mybir.dt.float32r)
        fold = sb("fold", [P, NC_TOK])
        ident = sb("ident", [P, P])
        ones = sb("ones", [P, P])
        masks = sb("masks", [P, 8, P], u8)
        eps_col = sb("eps_col", [P, 1])
        lbt = sb("lbt", [P, 2, LAYERS, KT])
        lsm = sb("lsm", [P, 4, KT])
        fs = sb("fs", [P, HEADS, TS])
        us = sb("us", [P, KT, TS])
        ebl = sb("ebl", [P, HEADS, NCH])
        row = sb("row", [P, 2, T])
        small = sb("small", [P, KT * TS])
        rt = sb("rt", [P, 3, 80])
        scratch = sb("scratch", [P, 1])
        flag = sb("flag", [1, 2], i32)
        PSEL = sb("psel", [P, 2, ROUNDS * NE + 2, 3])
        CUR = sb("cur", [P, 2, 2, 3])

        mix = ExitStack()

        def mix_sb(name, shape, dt=fp32):
            return mix.enter_context(nc.sbuf_tensor(name, shape, dt))

        qkv_r, big_r, tmp_r = rounded(("qkv_r", [P, 3 * KT * T]), ("big_r", [P, 6 * KT * T]), ("tmp_r", [P, 3 * KT * T]))
        qkv = mix_sb("qkv", [P, 3, KT, T])
        big = mix_sb("big", [P, 6, KT, T])
        tmp = mix_sb("tmp", [P, 3, KT * T])
        attb = mix_sb("attb", [P, HC, P])
        s0b = mix_sb("s0b", [P, HEADS, P])
        ubuf = mix_sb("ubuf", [P, KT, PAST + TP])
        sconv = mix_sb("sconv", [P, KT, TS, PAST])
        modrow = attb[:, 0:8, :].rearrange("p a n -> p (a n)").rearrange("p (a n) -> p a n", a=2)
        mix.close()
        w_hi = sb("w_hi", [P, SPLIT_RING, SLOT_W], f32r)
        w_lo = sb("w_lo", [P, SPLIT_RING, SLOT_W], f32r)
        hid_hi = sb("hid_hi", [P, FT, CAP], f32r)
        hid_lo = sb("hid_lo", [P, FT, CAP], f32r)
        tok_hi = sb("tok_hi", [P, KT, CAP], f32r)
        tok_lo = sb("tok_lo", [P, KT, CAP], f32r)
        H2TOK = sb("h2tok", [P, 3, D])
        SEL = [sb(f"sel{n}", [P, 3, CAP]) for n in range(2)]
        SELC = [sb(f"selc{n}", [P, 3, CAP]) for n in range(2)]
        SCT = [sb(f"sct{n}", [P, T]) for n in range(2)]
        YE = sb("ye", [P, D])
        MSILU = sb("msilu", [P, 2, 256])
        HTOK = sb("hid_tok", [P, 2, 256])
        FACC = h
        fin = H2TOK[:, :, :].rearrange("p a n -> p (a n)")[:, 0:KT * T].rearrange("p (k t) -> p k t", k=KT)
        TRI = sb("tri", [P, P])
        IOTA = sb("iota", [P, CAP])

        Q, K, V = (qkv[:, n] for n in range(3))
        F, SBZ, SG, GA, GB, B = (big[:, n] for n in range(6))
        DEC, X0, X1 = (tmp[:, n, :] for n in range(3))
        Xb = [X0, X1]
        KTOK, VTOK = DEC, X1
        KS, VS = X0[0:TS, 0:D], X0[0:TS, D:2 * D]
        VD = [DEC[0:TS, n * 1024:(n + 1) * 1024] for n in range(2)]
        Bf = B.rearrange("p k t -> p (k t)")
        STB = [Bf[:, 0:1024], Bf[:, 1024:2048]]
        SNEW = F.rearrange("p k t -> p (k t)")[:, 0:KT * TS * PAST]
        HI = [big_r[:, at:at + SLOT_W] for at in
              [n * SLOT_W for n in range(3)] + [4 * KT * T + n * SLOT_W for n in range(2)]]
        FQI_HI = [big_r[:, at:at + SLOT_W] for at in (KT * T + SLOT_W, 4 * KT * T, KT * T)]
        H1_LO = tmp_r[:, KT * T:2 * KT * T].rearrange("p (k t) -> p k t", t=T)
        H_HI = big_r[:, 3 * KT * T:4 * KT * T].rearrange("p (k t) -> p k t", t=T)
        HID_HI = qkv_r[:, 0:FT * T].rearrange("p (j t) -> p j t", t=T)
        HID_LO = tmp_r[:, 0:FT * T].rearrange("p (j t) -> p j t", t=T)
        att_f = attb[:, :, :].rearrange("p a n -> p (a n)")
        SILU = [att_f[:, 1024 + n * T:1024 + (n + 1) * T] for n in range(2)]
        HNEW = att_f[:, 1024 + 2 * T:1024 + 3 * T]
        banks = [ctx.enter_context(nc.psum_tensor(f"bank{n}", [P, 512], fp32)) for n in range(BANKS)]
        psum_full = sem("psum_full")
        psum_read = [sem(f"psum_read{n}") for n in range(BANKS)]
        landed = [sem(f"weights_landed{n}") for n in range(RING)]
        started = sem("slot_started")
        s_in = sem("inputs_landed")
        s_c = sem("c_landed")
        s_state = [sem(f"state_landed{n}") for n in range(2)]
        s_sconv = sem("sconv_landed")
        s_const = sem("constants_ready")
        s_pool = sem("pool_step")
        s_dve = sem("dve_step")
        s_act = sem("act_step")
        s_sq = sem("squares_ready")
        s_rstd = sem("roots_ready")
        s_modrow = sem("modulation_rows_ready")
        s_mod = sem("modulation_ready")
        s_cact = sem("c_act_ready")
        s_chalf = sem("c_halves_ready")
        s_high = sem("weights_high_ready")
        s_split = sem("weights_split")
        s_lbx = sem("lb_max_ready")
        s_lbe = sem("lb_exp_ready")
        s_h = sem("h_ready")
        s_fg = sem("forget_ready")
        s_ln = sem("logf_ready")
        s_qv = sem("qv_ready")
        s_zb = sem("sigmoid_zb_ready")
        s_glu = sem("glu_ready")
        s_dif = sem("decay_exponent_ready")
        s_exp = sem("decay_ready")
        s_xl = sem("level_operand_ready")
        s_kq = sem("decayed_kq_ready")
        s_eb = sem("chunk_decay_ready")
        s_vt = sem("vtok_ready")
        s_kt = sem("ktok_ready")
        s_att0 = sem("att_cleared")
        s_att = sem("att_ready")
        s_s0 = sem("s0_ready")
        s_s1 = sem("s1_ready")
        s_s1out = sem("s1_stored")
        s_kvs = sem("sample_kv_ready")
        s_vd = sem("vdiag_ready")
        s_sn = sem("sample_state_ready")
        s_ssout = [sem(f"sample_state_stored{n}") for n in range(2)]
        s_osq = sem("heads_squares_ready")
        s_hn = sem("heads_roots_ready")
        s_on = sem("gated_heads_ready")
        s_conv = sem("conv_tap")
        s_pconv = sem("pool_conv_tap")
        s_cs = sem("sample_products_ready")
        s_csout = sem("conv_states_stored")
        s_cv = sem("conv_ready")
        s_mu = sem("mean_ready")
        s_xc = sem("centred_ready")
        s_lnn = sem("layernorm_ready")
        s_yb = sem("branch_b_ready")
        s_sgr = sem("gates_ready")
        s_mix = sem("mixed_ready")
        s_x = sem("x_ready")
        s_gsilu = sem("ffn_silu_ready")
        s_hid = sem("hidden_ready")
        s_tok = sem("h2_token_major_ready")
        s_lg = sem("logits_ready")
        s_rex = sem("router_exp_ready")
        s_sel = sem("assignment_ready")
        s_flag = sem("flag_ready")
        m_sel = sem("moe_selection_ready")
        m_tok = sem("moe_tokens_high_ready")
        m_silu = sem("moe_silu_ready")
        m_hid = sem("moe_hidden_high_ready")
        m_hi = sem("moe_weights_high_ready")
        m_split = sem("moe_weights_split")
        m_dve = sem("moe_dve_step")
        f_x = sem("final_x_ready")
        f_sq = sem("final_squares_ready")
        f_st = sem("final_sum_ready")
        f_rt = sem("final_root_ready")
        f_dve = sem("final_dve_step")
        f_y = sem("y_ready")
        s_done = sem("outputs_stored")

        def par_of(name, l=None):
            at, n = PAR[name]
            if l is None:
                return par[:, at:at + n]
            n //= LAYERS
            return par[:, at + l * n:at + (l + 1) * n]

        def bank(name):
            return banks[USE[name] % BANKS]

        def fqi_until(l, g, t):
            return SPLIT_AT["fqi", l] + min(("fqi".index(g) * KT + t) // SLOT_TILES + 3, FQI_SLOTS)

        def high_halves(n):
            if SPLIT0 <= n < SPLIT1:
                r = n - SPLIT0
                return HI[r % HI_RING], n - HI_RING + 2 if r >= HI_RING else None
            m = n - SPLIT_AT["fqi", int(n >= SPLIT1)]
            if n < SPLIT0 and m < 3:
                return FQI_HI[m % 3], None
            return FQI_HI[m % 3], n - 3 if m < 2 else n - 1

        def await_use(eng, name):
            eng.wait_ge(psum_full, USE[name] + 1)
            return bank(name)

        def freed(ins, name):
            ins.then_inc(psum_read[USE[name] % BANKS], 1)

        def levels_view(buf, m):
            v = buf[:, :, 0:TP].rearrange("p h (n a m) -> p h n a m", a=2, m=m)
            return v[:, :, :, 0, :], v[:, :, :, 1, :]

        def as_kt(flat):
            return flat.rearrange("p (k t) -> p k t", t=T)

        def bc(ap, axis, shape):
            return ap.unsqueeze(axis).broadcast_to(shape)

        block = ctx.enter_context(nc.Block())

        @block.sync
        def _(sp):
            sp.dma_start(cT[:, :, :], c_in).then_inc(s_c, 16)
            sp.dma_start(par[:, :], par_in).then_inc(s_in, 16)
            for n in range(STREAM_SLOTS):
                if n >= RING:
                    sp.wait_ge(started, n - RING + 2)
                sp.dma_start(ring[:, n % RING, :], stream_in[n]).then_inc(landed[n % RING], 16)
                if n == 0:
                    sp.dma_start(x[:, :, :], x_in).then_inc(s_in, 16)

            def load(n, turn, source):
                at = STREAM_SLOTS + n
                sp.wait_ge(m_split, turn * GROUP_SLOTS + n + 1)
                sp.dma_start(ring[:, at % RING, :], source).then_inc(landed[at % RING], 16)

            def expert_group(turn, group):
                for n in range(LOADED, GROUP_SLOTS + LOADED):
                    load(n, turn, moe_in[bass.ds(group * GROUP_SLOTS + n, 1)])

            for n in range(LOADED):
                sp.wait_ge(started, STREAM_SLOTS + n - RING + 2)
                sp.dma_start(ring[:, (STREAM_SLOTS + n) % RING, :], moe_in[n]).then_inc(landed[(STREAM_SLOTS + n) % RING], 16)
            with sp.Fori(0, GROUPS) as group:
                expert_group(group, group)
            sp.wait_ge(s_flag, 2)
            more = sp.value_load(flag[0:1, 0:1], min_val=0, max_val=1)
            with sp.If(more > 0):
                with sp.Fori(1, ROUNDS) as rnd:
                    with sp.Fori(0, GROUPS) as group:
                        expert_group(rnd * GROUPS + group, group)
            for half in range(2):
                k = slice(half * KT // 2, (half + 1) * KT // 2)
                sp.wait_ge(f_y, k.stop)
                sp.dma_start(y_out[:, k, :], fin[:, k, :]).then_inc(s_done, 16)
            sp.wait_ge(s_done, 32)
            sp.wait_ge(s_csout, 32 * LAYERS)
            sp.wait_ge(s_s1out, 16 * LAYERS)
            for n in range(2):
                sp.wait_ge(s_ssout[n], 64 * LAYERS)

        @block.tensor
        def _(pe):
            order = psum_order()
            at = {"use": 0, "block": 0}

            def mm(out, lhsT, rhs, start=True, stop=True):
                return nc.tensor.matmul(out, lhsT, rhs, start=start, stop=stop)

            def open_use(name):
                n = at["use"]
                assert order[n] == name, (order[n], name)
                at["use"] += 1
                if n >= BANKS:
                    pe.wait_ge(psum_read[n % BANKS], n // BANKS)
                return banks[n % BANKS]

            def weight_mm(out, rhs, start, stop, width=1, lhsT=None):
                n, w = divmod(at["block"], SLOT_BLOCKS)
                at["block"] += width
                if w == 0:
                    pe.wait_ge(landed[n % RING], 16 * (n // RING + 1))
                weights = ring[:, n % RING, w * P:(w + width) * P]
                ins = mm(out, weights, rhs, start, stop) if lhsT is None else mm(out, lhsT, weights, start, stop)
                if w == 0:
                    ins.then_inc(started, 1)
                return ins

            def split_mm(out, products, start, stop, width=1):
                n, w = divmod(at["block"], SLOT_BLOCKS)
                at["block"] += width
                if w == 0:
                    pe.wait_ge(s_split, SPLIT_INDEX[n] + 1)
                cols = slice(w * P, (w + width) * P)
                halves = high_halves(n)[0][:, cols], ring_lo[:, n % RING, cols]
                for i, (half, operand) in enumerate(products):
                    pair = (operand, halves[half]) if width > 1 else (halves[half], operand)
                    ins = mm(out, *pair, start and i == 0, stop and i == len(products) - 1)
                    if w == 0 and i == 0:
                        ins.then_inc(started, 1)
                return ins

            def split_project(name, hi, lo, tiles, tiles_ready=None):
                ps = open_use(name)
                for k in range(tiles):
                    if tiles_ready is not None:
                        pe.wait_ge(s_h, tiles_ready + k)
                    ins = split_mm(ps[:, 0:T], ((0, hi[:, k, :]), (0, lo[:, k, :]), (1, hi[:, k, :])),
                                   k == 0, k == tiles - 1)
                ins.then_inc(psum_full, 1)

            def project(name, src, tiles_ready=None):
                ps = open_use(name)
                for k in range(KT):
                    if tiles_ready is not None:
                        pe.wait_ge(s_h, tiles_ready + k)
                    ins = weight_mm(ps[:, 0:T], src[:, k, :], k == 0, k == KT - 1)
                ins.then_inc(psum_full, 1)

            mod_groups = [0]

            def modulation(l, pair):
                split = (l, pair) in SPLIT_MODS
                rows = 2 * NC_TOK if split else NC_TOK
                if split:
                    pe.wait_ge(s_chalf, 1)
                for g in range(5):
                    if g < 4:
                        ps = open_use(("mod", l, pair, g))
                        for k in range(KT):
                            if split:
                                ins = split_mm(ps[0:rows, :], ((0, c_halves[:, k, :]), (1, c_halves[:, k, :])),
                                               k == 0, k == KT - 1, 4)
                            else:
                                ins = weight_mm(ps[0:rows, :], None, k == 0, k == KT - 1, 4, cT[:, k, :])
                        ins.then_inc(psum_full, 1)
                    if g >= 1:
                        mod_groups[0] += 1
                        pe.wait_ge(s_modrow, mod_groups[0])
                        ps = open_use(("mt", l, pair, g - 1))
                        for t in range(4):
                            ins = mm(ps[:, t * NC_TOK:(t + 1) * NC_TOK],
                                     modrow[0:rows, (g - 1) % 2, t * P:(t + 1) * P],
                                     (fold if split else ident)[0:rows, 0:NC_TOK])
                        ins.then_inc(psum_full, 1)

            def feature_sum(name, src):
                ps = open_use(name)
                for k in range(KT):
                    ins = mm(ps[:, 0:T], ones[:, :], src[:, k, :], k == 0, k == KT - 1)
                ins.then_inc(psum_full, 1)

            def transposes(name, l, src):
                for b in range(4):
                    ps = open_use((name, l, b))
                    for s in range(4):
                        hd, c = divmod(4 * b + s, NCH)
                        ins = nc.tensor.transpose(ps[:, s * P:(s + 1) * P], src[:, hd, c * CH:(c + 1) * CH], ident[:, :])
                    ins.then_inc(psum_full, 1)

            def levels(l, n):
                if n == 0:
                    pe.wait_ge(s_fg, l + 1)
                    pe.wait_ge(s_qv, l + 1)
                else:
                    pe.wait_ge(s_xl, 7 * l + n)
                for b in range(4):
                    ps = open_use(("att", l, n, b))
                    for s in range(4):
                        hd, c = divmod(4 * b + s, NCH)
                        tok = slice(c * CH, (c + 1) * CH)
                        a, w = (K, Q) if n == 0 else (as_kt(Xb[n % 2]), as_kt(Xb[n % 2]))
                        ins = mm(ps[:, s * P:(s + 1) * P], a[:, hd, tok], w[:, hd, tok])
                    ins.then_inc(psum_full, 1)

            def decayed_keys(l):
                pe.wait_ge(s_kq, 2 * l + 1)
                transposes("kt", l, as_kt(X0))

            def chunk_states(name, l, c):
                if c == 0:
                    pe.wait_ge(s_vt, l + 1)
                    pe.wait_ge(s_kt, l + 1)
                for b in range(2):
                    ps = open_use((name, l, b))
                    for s in range(4):
                        hc = (4 * b + s) * NCH + c
                        ins = mm(ps[:, s * P:(s + 1) * P], KTOK[:, hc * P:(hc + 1) * P], VTOK[:, hc * P:(hc + 1) * P])
                    ins.then_inc(psum_full, 1)

            def heads_out(l):
                pe.wait_ge(s_att, l + 1)
                pe.wait_ge(s_s0, l + 1)
                pe.wait_ge(s_kq, 2 * l + 2)
                for b in range(4):
                    ps = open_use(("o", l, b))
                    for s in range(2):
                        hd = 2 * b + s
                        hc = hd * NCH
                        mm(ps[:, s * TP:s * TP + CH], VTOK[:, hc * P:(hc + 1) * P], attb[:, hc, :])
                        out = ps[:, s * TP + CH:(s + 1) * TP]
                        mm(out, VTOK[:, (hc + 1) * P:(hc + 2) * P], attb[:, hc + 1, :], True, False)
                        ins = mm(out, s0b[:, hd, :], Q[:, hd, CH:TP], False, True)
                    ins.then_inc(psum_full, 1)

            def sample_kv(l):
                for b in range(4):
                    ps = open_use(("kvs", l, b))
                    for s in range(4):
                        ins = mm(ps[0:TS, s * P:(s + 1) * P], (K, V)[b // 2][:, 4 * (b % 2) + s, TP:T], ident[:, :])
                    ins.then_inc(psum_full, 1)

            def sample_outer(l, hd):
                if hd == 0:
                    pe.wait_ge(s_kvs, l + 1)
                pe.wait_ge(s_vd, HEADS * l + hd + 1)
                for half in range(2):
                    ps = open_use(("kv", l, hd, half))
                    mm(ps[:, :], KS[:, hd * P:(hd + 1) * P], VD[hd % 2][:, half * 512:(half + 1) * 512])\
                        .then_inc(psum_full, 1)

            def sample_out(l, hd):
                ps = open_use(("os", l, hd, 0))
                pe.wait_ge(s_sn, HEADS * l + hd + 1)
                for b in range(TS):
                    ins = mm(ps[:, b:b + 1], STB[hd % 2][:, b * P:(b + 1) * P], Q[:, hd, TP + b:TP + b + 1])
                ins.then_inc(psum_full, 1)

            stages = {"att": levels, "vt": lambda l: transposes("vt", l, V), "kt": decayed_keys,
                      "s0": lambda l: chunk_states("s0", l, 0), "o": heads_out,
                      "s1": lambda l: chunk_states("s1", l, 1), "kvs": sample_kv, "kv": sample_outer, "os": sample_out}

            pe.wait_ge(s_const, 1)
            pe.wait_ge(s_cact, 1)
            modulation(0, 0)
            pe.wait_ge(s_const, 2)
            for l in range(LAYERS):
                pe.wait_ge(s_sq, 4 * l + 1)
                feature_sum(("n1", l), as_kt(X1))
                if l == 1:
                    modulation(1, 2)
                for g in ("f", "q", "i"):
                    for t in range(KT):
                        split_project((g, l, t), H_HI, H1_LO, KT, 2 * KT * l + 1 if (g, t) == ("f", 0) else None)
                for r, (g, t) in enumerate(REST):
                    project((g, l, t), h)
                    for stage in STAGES.get(r, ()):
                        stages[stage[0]](l, *stage[1:])
                pe.wait_ge(s_osq, l + 1)
                for hd in range(HEADS):
                    ps = open_use(("hn", l, hd))
                    mm(ps[:, 0:T], ones[:, :], as_kt(X1)[:, hd, :]).then_inc(psum_full, 1)
                modulation(l, 1)
                pe.wait_ge(s_on, l + 1)
                for t in range(KT):
                    project(("ya", l, t), V)
                    if t == MU_AFTER:
                        pe.wait_ge(s_cv, l + 1)
                        feature_sum(("mu", l), SBZ)
                    if t == VAR_AFTER:
                        pe.wait_ge(s_sq, 4 * l + 2)
                        feature_sum(("var", l), as_kt(DEC))
                for t in range(KT):
                    if t == 0:
                        pe.wait_ge(s_yb, l + 1)
                    project(("yb", l, t), SBZ)
                pe.wait_ge(s_mix, l + 1)
                for t in range(KT):
                    project(("wo", l, t), GA)
                if l == 0:
                    modulation(0, 2)
                pe.wait_ge(s_sq, 4 * l + 3)
                feature_sum(("n2", l), as_kt(X1))
                if l == 0:
                    modulation(1, 0)
                    for j in range(FT):
                        split_project(("fg", j), H_HI, h_lo, KT, 2 * KT * l + KT + 1 if j == 0 else None)
                        split_project(("fu", j), H_HI, h_lo, KT)
                    pe.wait_ge(s_hid, FT)
                    for t in range(KT):
                        split_project(("fd", t), HID_HI, HID_LO, FT)
            assert at["block"] == STREAM_SLOTS * SLOT_BLOCKS

            for b in range(6):
                tt, half = divmod(b, 2)
                t0, tn = TT[tt]
                pe.wait_ge(s_h, 2 * KT * LAYERS - KT + 4 * (half + 1))
                ps = open_use(("tok", b))
                for s in range(4):
                    ins = mm(ps[0:tn, s * P:(s + 1) * P], h[:, 4 * half + s, t0:t0 + tn], ident[:, :])
                ins.then_inc(psum_full, 1)
            pe.wait_ge(s_h, 2 * KT * LAYERS)
            rw = par_of("rw").rearrange("p (k e) -> p k e", e=NE)
            ps = open_use(("lg",))
            for tt, (t0, tn) in enumerate(TT):
                for k in range(KT):
                    ins = mm(ps[0:tn, tt * NE:(tt + 1) * NE], h[:, k, t0:t0 + tn], rw[:, k, :], k == 0, k == KT - 1)
            ins.then_inc(psum_full, 1)
            pe.wait_ge(s_sel, 1)
            ps = open_use(("pos",))
            for tt, (_, tn) in enumerate(TT):
                for u in range(tt + 1):
                    un = TT[u][1]
                    lhsT = TRI[0:un, 0:tn] if u == tt else ones[0:un, 0:tn]
                    mm(ps[0:tn, tt * NE:(tt + 1) * NE], lhsT, rt[0:un, u, 8:16], u == 0, u == tt)
            for u, (_, un) in enumerate(TT):
                ins = mm(ps[:, 3 * NE:4 * NE], ones[0:un, :], rt[0:un, u, 8:16], u == 0, u == 2)
            ins.then_inc(psum_full, 1)
            assert at["use"] == MOE_USE0

            def moe_open(turn, n):
                n += MOE_USE0
                pe.wait_ge(psum_read[n % BANKS], turn * (GROUP * MOE_USES // BANKS) + n // BANKS)
                return banks[n % BANKS]

            def moe_read(turn, n):
                n += MOE_USE0
                pe.wait_ge(psum_read[n % BANKS], turn * (GROUP * MOE_USES // BANKS) + n // BANKS + 1)

            def gather(turn, n, e):
                for k0, kn in ((0, 3), (3, 3), (6, 2)):
                    ps = moe_open(turn, n)
                    n += 1
                    for g in range(kn):
                        for tt, (_, tn) in enumerate(TT):
                            ins = mm(ps[:, g * P:(g + 1) * P], H2TOK[0:tn, tt, (k0 + g) * P:(k0 + g + 1) * P],
                                     SEL[e][0:tn, tt, :], tt == 0, tt == 2)
                    ins.then_inc(psum_full, 1)
                ps = moe_open(turn, n)
                for tt, (t0, tn) in enumerate(TT):
                    ins = mm(ps[:, t0:t0 + tn], SELC[e][0:tn, tt, :], ident[0:tn, 0:tn])
                ins.then_inc(psum_full, 1)

            def expert(turn, s):
                use = 4 + s * MOE_USES
                blk = [s * MOE_SLOTS * SLOT_BLOCKS]

                def next_weights():
                    n, w = divmod(blk[0], SLOT_BLOCKS)
                    if w == 0:
                        pe.wait_ge(m_split, turn * GROUP_SLOTS + RING + n + 1)
                    cols = slice(w * P, (w + 4) * P)
                    blk[0] += 4
                    return w_hi[:, n % SPLIT_RING, cols], w_lo[:, n % SPLIT_RING, cols], w == 0

                def three(ps, hi, lo, k, last):
                    whi, wlo, first = next_weights()
                    ins = mm(ps, hi, whi, k == 0, False)
                    if first:
                        ins.then_inc(started, 1)
                    mm(ps, lo, whi, False, False)
                    return mm(ps, hi, wlo, False, k == last)

                def gate_up(c):
                    ps = moe_open(turn, use + (0 if c == 0 else 2 * c - 1))
                    for k in range(KT):
                        ins = three(ps[:, :], tok_hi[:, k, :], tok_lo[:, k, :], k, KT - 1)
                    ins.then_inc(psum_full, 1)

                def hidden_transposes(c):
                    moe_read(turn, use + (0 if c == 0 else 2 * c - 1))
                    ps = moe_open(turn, use + 2 * c + (2 if c < CHUNKS - 1 else 1))
                    for t in range(2):
                        ins = nc.tensor.transpose(ps[:, t * P:(t + 1) * P], HTOK[:, c % 2, t * P:(t + 1) * P], ident[:, :])
                    ins.then_inc(psum_full, 1)

                for c in range(CHUNKS):
                    gate_up(c)
                    if c >= 1:
                        hidden_transposes(c - 1)
                down = use + 2 * CHUNKS
                halves = [moe_open(turn, down), moe_open(turn, down + 1)]
                for k in range(FT):
                    if k == 2:
                        hidden_transposes(CHUNKS - 1)
                    if k % 2 == 0:
                        c = k // 2
                        moe_read(turn, use + 2 * c + (2 if c < CHUNKS - 1 else 1))
                    for half in range(2):
                        ins = three(halves[half][:, :], hid_hi[:, k, :], hid_lo[:, k, :], k, FT - 1)
                        if k == FT - 1:
                            ins.then_inc(psum_full, 1)
                pe.wait_ge(m_sel, GROUP * turn + s + 2)
                gather(turn, down + 2, (s + 1) % 2)
                for t in range(KT):
                    if t % 4 == 0:
                        moe_read(turn, down + t // 4)
                    ps = moe_open(turn, down + 6 + t)
                    mm(ps[:, 0:T], YE[:, t * P:(t + 1) * P], SCT[s % 2][:, :]).then_inc(psum_full, 1)
                for n in range(4):
                    moe_read(turn, down + 2 + n)

            pe.wait_ge(m_sel, 1)
            gather(0, 0, 0)
            for n in range(4):
                moe_read(0, n)
            with pe.Fori(0, GROUPS) as group:
                for s in range(GROUP):
                    expert(group, s)
            pe.wait_ge(s_flag, 2)
            more = pe.value_load(flag[0:1, 0:1], min_val=0, max_val=1)
            with pe.If(more > 0):
                with pe.Fori(1, ROUNDS) as rnd:
                    with pe.Fori(0, GROUPS) as group:
                        for s in range(GROUP):
                            expert(rnd * GROUPS + group, s)
            for k in range(KT):
                pe.wait_ge(f_sq, k + 1)
                ins = mm(banks[0][:, 0:T], ones[:, :], fin[:, k, :], k == 0, k == KT - 1)
            ins.then_inc(f_st, 1)

        @block.scalar
        def _(act):
            steps = [0]

            def link(ins):
                steps[0] += 1
                ins.then_inc(s_act, 1)
                act.wait_ge(s_act, steps[0])

            def own_read(name):
                act.wait_ge(psum_read[USE[name] % BANKS], USE[name] // BANKS + 1)

            def log_mean(name, out, scale):
                ps = await_use(act, name)
                freed(act.activation(out, ps[:, 0:T], ACT.Ln, bias=eps_col[:, 0:1], scale=scale), name)
                own_read(name)

            def inverse_root(name, out, signal):
                log_mean(name, out, 1.0 / D)
                act.activation(out, out, ACT.Exp, scale=-0.5).then_inc(signal, 1)

            def expert_high(turn, n):
                at = STREAM_SLOTS + n
                act.wait_ge(landed[at % RING], turn * (16 * GROUP_SLOTS // RING) + 16 * (at // RING + 1))
                act.wait_ge(started, turn * GROUP_SLOTS + at - SPLIT_RING + 2)
                act.activation(w_hi[:, n % SPLIT_RING, :], ring[:, at % RING, :], ACT.Copy).then_inc(m_hi, 1)

            groups, high = [0], [0]

            def split_high(until):
                while high[0] < len(SPLIT_SLOTS) and SPLIT_SLOTS[high[0]] < until:
                    n = SPLIT_SLOTS[high[0]]
                    buf, free = high_halves(n)
                    act.wait_ge(landed[n % RING], 16 * (n // RING + 1))
                    if free is not None:
                        act.wait_ge(started, free)
                    act.activation(buf, ring[:, n % RING, :], ACT.Copy).then_inc(s_high, 1)
                    high[0] += 1

            def modulation(l, pair):
                split = (l, pair) in SPLIT_MODS
                rows = 2 * NC_TOK if split else NC_TOK
                for g in range(4):
                    if split:
                        split_high(min(SPLIT_AT[l, pair] + 2 * g + HI_RING, SPLIT1 + 2))
                    name = ("mod", l, pair, g)
                    ps = await_use(act, name)
                    if groups[0] >= 2:
                        act.wait_ge(s_mod, groups[0] - 1)
                    act.activation(modrow[0:rows, g % 2, :], ps[0:rows, :], ACT.Copy).then_inc(s_act, 1)
                    steps[0] += 1
                    act.wait_ge(s_act, steps[0])
                    act.sem_inc(psum_read[USE[name] % BANKS], 1)
                    act.sem_inc(s_modrow, 1)
                    groups[0] += 1

            def levels(l, n):
                if 1 <= n < 7:
                    level_exp(l, n + 1)

            def level_exp(l, n):
                act.wait_ge(s_dif, 8 * l + n)
                act.activation(as_kt(DEC)[:, :, 0:TP], as_kt(DEC)[:, :, 0:TP], ACT.Exp).then_inc(s_exp, 1)

            def values(l):
                level_exp(l, 8)
                link(act.activation(ebl[:, :, :], B[:, :, CH - 1:TP:CH], ACT.Exp))
                act.activation(B[:, :, CH:TP], B[:, :, CH:TP], ACT.Exp).then_inc(s_eb, 1)
                act.wait_ge(s_att, l + 1)
                for b in range(4):
                    ps = await_use(act, ("vt", l, b))
                    freed(act.activation(VTOK[:, b * 512:(b + 1) * 512], ps[:, :], ACT.Copy), ("vt", l, b))
                own_read(("vt", l, 3))
                act.sem_inc(s_vt, 1)

            def keys(l):
                act.wait_ge(s_kq, 2 * l + 1)
                for b in range(4):
                    ps = await_use(act, ("kt", l, b))
                    freed(act.activation(KTOK[:, b * 512:(b + 1) * 512], ps[:, :], ACT.Copy), ("kt", l, b))
                own_read(("kt", l, 3))
                act.sem_inc(s_kt, 1)

            def first_state(l):
                if l > 0:
                    act.wait_ge(s_s1out, 16 * l)
                for b in range(2):
                    ps = await_use(act, ("s0", l, b))
                    freed(act.activation(s0b[:, 4 * b:4 * b + 4, :], ps[:, :].rearrange("p (a n) -> p a n", a=4), ACT.Copy),
                          ("s0", l, b))
                own_read(("s0", l, 1))
                act.sem_inc(s_s0, 1)

            def load_state(l, hd):
                act.dma_start(STB[hd % 2], sh_in[l, hd].rearrange("p b n -> p (b n)")).then_inc(s_state[hd % 2], 16)

            def heads_out(l):
                act.wait_ge(s_kq, 2 * l + 2)
                load_state(l, 0)
                load_state(l, 1)
                for b in range(4):
                    ps = await_use(act, ("o", l, b))
                    freed(act.activation(V[:, 2 * b:2 * b + 2, 0:TP], ps[:, :].rearrange("p (a n) -> p a n", a=2), ACT.Copy),
                          ("o", l, b))

            def sample_kv(l):
                for b in range(4):
                    ps = await_use(act, ("kvs", l, b))
                    freed(act.activation((KS, VS)[b // 2][:, (b % 2) * 512:(b % 2 + 1) * 512], ps[0:TS, :], ACT.Copy),
                          ("kvs", l, b))
                own_read(("kvs", l, 3))
                act.sem_inc(s_kvs, 1)

            def next_state(l, hd):
                if hd == 0:
                    act.wait_ge(s_s1, l + 1)
                    act.dma_start(hp_out[l], s0b[:, :, :]).then_inc(s_s1out, 16)
                if hd >= 2:
                    act.wait_ge(s_ssout[hd % 2], 16 * ((HEADS * l + hd) // 2))
                    load_state(l, hd)

            def sample_out(l, hd):
                act.wait_ge(s_sn, HEADS * l + hd + 1)
                act.dma_start(hs_out[l, hd].rearrange("p b n -> p (b n)"), STB[hd % 2]).then_inc(s_ssout[hd % 2], 16)
                ps = await_use(act, ("os", l, hd, 0))
                freed(act.activation(V[:, hd, TP:T], ps[:, 0:TS], ACT.Copy), ("os", l, hd, 0))

            stages = {"att": levels, "vt": values, "kt": keys, "s0": first_state, "o": heads_out,
                      "s1": lambda l: None, "kvs": sample_kv, "kv": next_state, "os": sample_out}

            act.wait_ge(s_c, 16)
            act.activation(cT[:, :, :], cT[:, :, :], ACT.Silu).then_inc(s_cact, 1)
            act.wait_ge(s_in, 32)
            act.activation(as_kt(X1), x[:, :, :], ACT.Square).then_inc(s_sq, 1)
            act.wait_ge(s_lbx, 1)
            act.activation(lsm[:, 1:3, :], lsm[:, 1:3, :], ACT.Exp).then_inc(s_lbe, 1)
            modulation(0, 0)
            act.wait_ge(s_const, 2)
            for l in range(LAYERS):
                if l > 0:
                    act.wait_ge(s_x, 2 * l)
                    act.activation(as_kt(X1), x[:, :, :], ACT.Square).then_inc(s_sq, 1)
                if l == 0:
                    split_high(SPLIT_AT["fqi", 0] + 1)
                inverse_root(("n1", l), row[:, 0, :], s_rstd)
                if l > 0:
                    modulation(1, 2)
                    act.wait_ge(s_csout, 32 * l)
                    for n in range(2):
                        act.wait_ge(s_ssout[n], 64 * l)
                for t in range(KT):
                    split_high(fqi_until(l, "f", t))
                    ps = await_use(act, ("f", l, t))
                    act.activation(F[:, t, :], ps[:, 0:T], ACT.Sigmoid)
                    freed(act.activation(K[:, t, :], ps[:, 0:T], ACT.Sigmoid, scale=-1.0), ("f", l, t))
                for t in range(KT):
                    split_high(fqi_until(l, "q", t))
                    ps = await_use(act, ("q", l, t))
                    freed(act.activation(Q[:, t, :], ps[:, 0:T], ACT.Silu), ("q", l, t))
                    if t == 3:
                        act.wait_ge(s_fg, l + 1)
                        act.activation(B[:, :, 0:TP], F[:, :, 0:TP], ACT.Ln).then_inc(s_ln, 1)
                for t in range(KT):
                    split_high(fqi_until(l, "i", t))
                    ps = await_use(act, ("i", l, t))
                    freed(act.activation(V[:, t, :], ps[:, 0:T], ACT.Copy), ("i", l, t))
                    if t == 0:
                        own_read(("i", l, 0))
                        act.sem_inc(s_qv, 1)
                level_exp(l, 1)
                for r, (g, t) in enumerate(REST):
                    name = (g, l, t)
                    if g != "za":
                        dst, func = {"zb": (SBZ, ACT.Sigmoid), "g": (SG, ACT.Silu), "ga": (GA, ACT.Sigmoid),
                                     "gb": (GB, ACT.Sigmoid)}[g]
                        ps = await_use(act, name)
                        if name == ("gb", l, KT - 1):
                            act.wait_ge(s_pconv, (l + 1) * CW * len(POOL_CONV))
                        freed(act.activation(dst[:, t, :], ps[:, 0:T], func), name)
                        if g == "zb":
                            own_read(name)
                            act.sem_inc(s_zb, 1)
                        if name == ("gb", l, KT - 1):
                            own_read(name)
                            act.sem_inc(s_sgr, 1)
                    for stage in STAGES.get(r, ()):
                        stages[stage[0]](l, *stage[1:])
                own_read(("os", l, HEADS - 1, 0))
                act.activation(as_kt(X1), V, ACT.Square).then_inc(s_osq, 1)
                for hd in range(HEADS):
                    log_mean(("hn", l, hd), as_kt(X0)[:, hd, :], 1.0 / P)
                act.activation(X0, X0, ACT.Exp, scale=-0.5).then_inc(s_hn, 1)
                modulation(l, 1)
                ps = await_use(act, ("mu", l))
                freed(act.activation(row[:, 0, :], ps[:, 0:T], ACT.Copy, scale=1.0 / D), ("mu", l))
                own_read(("mu", l))
                act.sem_inc(s_mu, 1)
                act.wait_ge(s_xc, l + 1)
                act.activation(as_kt(DEC), SBZ, ACT.Square).then_inc(s_sq, 1)
                inverse_root(("var", l), row[:, 1, :], s_rstd)
                act.wait_ge(s_lnn, l + 1)
                for t in range(KT):
                    ins = act.activation(SBZ[:, t, :], SBZ[:, t, :], ACT.Silu, bias=par_of("lnb", l)[:, t:t + 1],
                                         scale=par_of("lng", l)[:, t:t + 1])
                ins.then_inc(s_yb, 1)
                if l == 0:
                    act.wait_ge(s_csout, 32)
                    for n in range(2):
                        act.wait_ge(s_ssout[n], 64)
                    await_use(act, ("wo", l, 0))
                    split_high(SPLIT0 + 3)
                act.wait_ge(s_x, 2 * l + 1)
                act.activation(as_kt(X1), x[:, :, :], ACT.Square).then_inc(s_sq, 1)
                if l == 0:
                    modulation(0, 2)
                inverse_root(("n2", l), row[:, 0, :], s_rstd)
                act.sem_inc(s_sq, 1)
                if l == 0:
                    modulation(1, 0)
                    for j in range(FT):
                        split_high(SPLIT_AT["ffn"] + j + HI_RING - 1)
                        if j >= 2:
                            act.wait_ge(s_hid, j - 1)
                        ps = await_use(act, ("fg", j))
                        freed(act.activation(SILU[j % 2], ps[:, 0:T], ACT.Silu), ("fg", j))
                        own_read(("fg", j))
                        act.sem_inc(s_gsilu, 1)
                    split_high(SPLIT_AT[1, 2] + HI_RING - 2)
            act.wait_ge(s_csout, 32 * LAYERS)
            act.wait_ge(s_s1out, 16 * LAYERS)
            for n in range(2):
                act.wait_ge(s_ssout[n], 64 * LAYERS)
            for n in range(AHEAD):
                expert_high(0, n)
            for b in range(6):
                tt, half = divmod(b, 2)
                tn = TT[tt][1]
                ps = await_use(act, ("tok", b))
                ins = act.activation(H2TOK[0:tn, tt, half * 512:(half + 1) * 512], ps[0:tn, :], ACT.Copy)
                freed(ins, ("tok", b))
            name = ("tok", 5)
            act.wait_ge(psum_read[USE[name] % BANKS], USE[name] // BANKS + 1)
            act.sem_inc(s_tok, 1)
            act.wait_ge(s_lg, 1)
            act.activation(rt[:, :, 36:37], rt[:, :, 36:37], ACT.Exp).then_inc(s_rex, 1)

            def moe_full(turn, n):
                act.wait_ge(psum_full, turn * (GROUP * MOE_USES) + MOE_USE0 + n + 1)
                return banks[(MOE_USE0 + n) % BANKS]

            def gathered(turn, n, e):
                for k0, kn in ((0, 3), (3, 3), (6, 2)):
                    ps = moe_full(turn, n)
                    n += 1
                    act.activation(tok_hi[:, k0:k0 + kn, :], ps[:, 0:kn * P].rearrange("p (a n) -> p a n", a=kn), ACT.Copy)\
                        .then_inc(m_tok, 1)
                ps = moe_full(turn, n)
                act.activation(SCT[e][:, :], ps[:, 0:T], ACT.Copy).then_inc(psum_read[(MOE_USE0 + n) % BANKS], 1)

            def expert(turn, s):
                use = 4 + s * MOE_USES
                slot = s * MOE_SLOTS + AHEAD

                def silu(c):
                    n = use + (0 if c == 0 else 2 * c - 1)
                    ps = moe_full(turn, n)
                    if c >= 2:
                        m = MOE_USE0 + use + (0 if c == 2 else 2 * c - 5)
                        act.wait_ge(psum_read[m % BANKS], turn * (GROUP * MOE_USES // BANKS) + m // BANKS + 1)
                    act.activation(MSILU[:, c % 2, :], ps[:, 0:256], ACT.Silu).then_inc(m_silu, 1)

                def hidden_high(c):
                    ps = moe_full(turn, use + 2 * c + (2 if c < CHUNKS - 1 else 1))
                    act.activation(hid_hi[:, 2 * c:2 * c + 2, :], ps[:, 0:256].rearrange("p (a n) -> p a n", a=2), ACT.Copy)\
                        .then_inc(m_hid, 1)

                for c in range(CHUNKS):
                    expert_high(turn, slot + 2 * c)
                    expert_high(turn, slot + 2 * c + 1)
                    silu(c)
                    if c >= 1:
                        hidden_high(c - 1)
                expert_high(turn, slot + 2 * CHUNKS)
                hidden_high(CHUNKS - 1)
                for n in range(2 * CHUNKS + 1, MOE_SLOTS):
                    expert_high(turn, slot + n)
                down = use + 2 * CHUNKS
                for half in range(2):
                    ps = moe_full(turn, down + half)
                    act.activation(YE[:, half * 512:(half + 1) * 512], ps[:, :], ACT.Copy)\
                        .then_inc(psum_read[(MOE_USE0 + down + half) % BANKS], 1)
                gathered(turn, down + 2, (s + 1) % 2)

            act.wait_ge(m_sel, 1)
            gathered(0, 0, 0)
            with act.Fori(0, GROUPS) as group:
                for s in range(GROUP):
                    expert(group, s)
            act.wait_ge(s_flag, 2)
            more = act.value_load(flag[0:1, 0:1], min_val=0, max_val=1)
            with act.If(more > 0):
                with act.Fori(1, ROUNDS) as rnd:
                    with act.Fori(0, GROUPS) as group:
                        for s in range(GROUP):
                            expert(rnd * GROUPS + group, s)
            for t in range(KT):
                act.wait_ge(f_x, t + 1)
                act.activation(fin[:, t, :], x[:, t, :], ACT.Square).then_inc(f_sq, 1)
            act.wait_ge(f_st, 1)
            act.activation(row[:, 0, :], banks[0][:, 0:T], ACT.Ln, bias=eps_col[:, 0:1], scale=1.0 / D).then_inc(f_rt, 1)
            act.wait_ge(f_rt, 1)
            act.activation(row[:, 0, :], row[:, 0, :], ACT.Exp, scale=-0.5).then_inc(f_rt, 1)

        @block.gpsimd
        def _(pool):
            steps = [0]

            def link(ins):
                steps[0] += 1
                ins.then_inc(s_pool, 1)
                pool.wait_ge(s_pool, steps[0])

            link(pool.memset(ident[:, :], 0.0))
            pool.affine_select(out=ident[:, :], in_=ident[:, :], compare_op=ALU.not_equal, fill=1.0,
                               base=0, pattern=[[-1, P]], channel_multiplier=1).then_inc(s_const, 1)
            pool.wait_ge(s_const, 1)
            pool.memset(eps_col[:, :], EPS)
            pool.memset(ones[:, :], 1.0)
            mf = as_kt(X0)[:, :, 0:P]
            link(pool.memset(mf, 0.0))
            link(pool.tensor_copy(mf[:, 0, :], ident[:, :]))
            for n, m in enumerate(SPANS):
                second = mf[:, n + 1, :].rearrange("p (n a m) -> p n a m", a=2, m=m)[:, :, 1, :]
                link(pool.memset(second, 1.0))
                blocks = P // (2 * m)
                link(pool.affine_select(out=second, in_=second, compare_op=ALU.is_ge, fill=0.0, base=0,
                                        pattern=[[-2 * m, blocks], [0, m]], channel_multiplier=1))
                link(pool.affine_select(out=second, in_=second, compare_op=ALU.is_ge, fill=0.0, base=m - 1,
                                        pattern=[[2 * m, blocks], [0, m]], channel_multiplier=-1))
            link(pool.tensor_copy(masks[:, :, :], mf))
            link(pool.memset(ubuf[:, :, 0:PAST], 0.0))
            pool.memset(ubuf[:, 0, 0:1], 0.0).then_inc(s_const, 1)
            taps = [0]
            for l in range(LAYERS):
                if l > 0:
                    pool.wait_ge(s_csout, 32 * l)
                    pool.wait_ge(s_cv, l)
                pool.dma_start(sconv[:, :, :, :], sc_in[l]).then_inc(s_sconv, 16)
                pool.wait_ge(s_fg, l + 1)
                pool.memset(attb[:, :, :], 0.0).then_inc(s_att0, 1)
                pool.wait_ge(s_glu, l + 1)
                cw = par_of("cw", l).rearrange("p (k j) -> p k j", j=CW)
                pool.dma_start(cp_out[l], ubuf[:, :, TP:TP + PAST]).then_inc(s_csout, 16)
                pool.wait_ge(s_sconv, 16 * (l + 1))
                snew = SNEW.rearrange("p (k b j) -> p k b j", b=TS, j=PAST)
                sv = sconv[:, :, :, :].rearrange("p k b j -> p (k b) j")
                snv = SNEW.rearrange("p (n j) -> p n j", j=PAST)
                pool.tensor_copy(snv[:, :, 0:PAST - 1], sv[:, :, 1:PAST])
                link(pool.tensor_copy(snew[:, :, :, PAST - 1], us[:, :, :]))
                pool.dma_start(cs_out[l], SNEW).then_inc(s_csout, 16)
                pool.tensor_tensor(sconv[:, :, :, :], sconv[:, :, :, :],
                                   bc(cw[:, :, 0:PAST], 2, [P, KT, TS, PAST]), ALU.mult).then_inc(s_cs, 1)
                for j in range(CW):
                    for n, t in enumerate(POOL_CONV):
                        win = ubuf[:, t, j:j + TP]
                        acc = SBZ[:, t, 0:TP]
                        if j == 0:
                            pool.tensor_scalar(acc, win, cw[:, t, 0:1], par_of("cb", l)[:, t:t + 1], ALU.mult, ALU.add)\
                                .then_inc(s_pconv, 1)
                            taps[0] += 1
                            continue
                        prod = GB[:, KT - 1, 0:TP]
                        pool.wait_ge(s_pconv, taps[0])
                        link(pool.tensor_scalar(prod, win, cw[:, t, j:j + 1], None, ALU.mult))
                        pool.tensor_tensor(acc, acc, prod, ALU.add).then_inc(s_pconv, 1)
                        taps[0] += 1
                diag = bc(ident[0:TS, 0:TS], 2, [TS, TS, P])
                pool.wait_ge(s_kvs, l + 1)
                pool.wait_ge(s_s1, l + 1)
                for hd in range(HEADS):
                    if hd >= 2:
                        pool.wait_ge(psum_full, USE[("kv", l, hd - 2, 1)] + 1)
                    vd = VD[hd % 2].rearrange("p (b n) -> p b n", b=TS)
                    pool.tensor_tensor(vd, diag, bc(VS[:, hd * P:(hd + 1) * P], 1, [TS, TS, P]), ALU.mult)\
                        .then_inc(s_vd, 1)
                if l == LAYERS - 1:
                    pool.wait_ge(s_x, 2 * LAYERS - 1)
                    pool.wait_ge(s_csout, 32 * LAYERS)
                    pool.wait_ge(s_s1out, 16 * LAYERS)
                    for n in range(2):
                        pool.wait_ge(s_ssout[n], 64 * LAYERS)
                    link(pool.memset(TRI[:, :], 1.0))
                    link(pool.affine_select(out=TRI[:, :], in_=TRI[:, :], compare_op=ALU.is_gt, fill=0.0, base=0,
                                            pattern=[[1, P]], channel_multiplier=-1))
                    pool.iota(IOTA[:, :], pattern=[[1, P]], base=0, channel_multiplier=0,
                              allow_small_or_imprecise_dtypes=True).then_inc(s_const, 1)

        @block.vector
        def _(dve):
            steps = [0]

            def link(ins):
                steps[0] += 1
                ins.then_inc(s_dve, 1)
                dve.wait_ge(s_dve, steps[0])

            def done(signal):
                link(dve.memset(scratch[:, :], 0.0))
                dve.sem_inc(signal, 1)

            def own_read(name):
                dve.wait_ge(psum_read[USE[name] % BANKS], USE[name] // BANKS + 1)

            dve.wait_ge(s_in, 32)
            lb0, lb1 = par_of("lb", 0), par_of("lb", 1)
            link(dve.tensor_tensor(lsm[:, 0, :], lb0, lb1, ALU.max))
            dve.tensor_tensor(lsm[:, 1, :], lb0, lsm[:, 0, :], ALU.subtract)
            dve.tensor_tensor(lsm[:, 2, :], lb1, lsm[:, 0, :], ALU.subtract).then_inc(s_lbx, 1)
            dve.wait_ge(s_lbe, 1)
            link(dve.tensor_tensor(lsm[:, 3, :], lsm[:, 1, :], lsm[:, 2, :], ALU.add))
            link(dve.reciprocal(lsm[:, 3, :], lsm[:, 3, :]))
            dve.tensor_tensor(lsm[:, 1, :], lsm[:, 1, :], lsm[:, 3, :], ALU.mult)
            link(dve.tensor_tensor(lsm[:, 2, :], lsm[:, 2, :], lsm[:, 3, :], ALU.mult))
            dve.tensor_tensor(lbt[:, 0, 0, :], lsm[:, 1, :], lsm[:, 1, :], ALU.subtract)
            link(dve.tensor_tensor(lsm[:, 3, :], lsm[:, 1, :], lsm[:, 2, :], ALU.add))
            link(dve.tensor_tensor(lbt[:, 0, 1, :], lsm[:, 3, :], lsm[:, 1, :], ALU.subtract))
            link(dve.tensor_scalar(lbt[:, 1, :, :], lbt[:, 0, :, :], -1.0, 1.0, ALU.mult, ALU.add))

            def expert_low(turn, n):
                at = STREAM_SLOTS + n
                dve.wait_ge(m_hi, turn * GROUP_SLOTS + n + 1)
                dve.tensor_tensor(w_lo[:, n % SPLIT_RING, :], ring[:, at % RING, :],
                                  w_hi[:, n % SPLIT_RING, :].bitcast(fp32), ALU.subtract).then_inc(m_split, 1)

            low = [0]

            def split_low(until):
                while low[0] < len(SPLIT_SLOTS) and SPLIT_SLOTS[low[0]] < until:
                    n = SPLIT_SLOTS[low[0]]
                    dve.wait_ge(s_high, low[0] + 1)
                    dve.tensor_tensor(ring_lo[:, n % RING, :], ring[:, n % RING, :], high_halves(n)[0].bitcast(fp32),
                                      ALU.subtract).then_inc(s_split, 1)
                    low[0] += 1

            def modulation(l, pair, between=None):
                for g in range(4):
                    if between is not None:
                        between()
                    if (l, pair) in SPLIT_MODS:
                        split_low(min(SPLIT_AT[l, pair] + 2 * g + 2 + HI_RING, SPLIT1 + 2))
                    name = ("mt", l, pair, g)
                    ps = await_use(dve, name)
                    part = slice(16 * pair + 4 * g, 16 * pair + 4 * g + 4)
                    ins = dve.tensor_tensor(modt[:, l, part, :], ps[:, 0:4 * NC_TOK].rearrange("p (a n) -> p a n", a=4),
                                            bc(par_of("ada_b", l)[:, part], 2, [P, 4, NC_TOK]), ALU.add)
                    freed(ins, name)
                    own_read(name)
                    dve.sem_inc(s_mod, 1)

            def shift(l, part):
                return modt[:, l, part * KT:(part + 1) * KT, :]

            def modulated_norm(l, gain, sh, sc, roots, halves=None, parts=1):
                g = bc(gain, 2, [P, KT, NC_TOK])
                link(dve.scalar_tensor_tensor(sc1g[:, :, :], shift(l, sc), 1.0, g, ALU.add, ALU.mult))
                for t in range(KT):
                    dve.tensor_scalar(h[:, t, 0:TP], x[:, t, 0:TP], sc1g[:, t, 0:1], None, ALU.mult)
                link(dve.tensor_tensor(h[:, :, TP:T], x[:, :, TP:T], sc1g[:, :, 1:NC_TOK], ALU.mult))
                dve.wait_ge(s_rstd, roots)
                if halves is None:
                    for t in range(KT):
                        link(dve.tensor_tensor(h[:, t, :], h[:, t, :], row[:, 0, :], ALU.mult))
                        dve.tensor_scalar(h[:, t, 0:TP], h[:, t, 0:TP], shift(l, sh)[:, t, 0:1], None, ALU.add)
                        dve.tensor_tensor(h[:, t, TP:T], h[:, t, TP:T], shift(l, sh)[:, t, 1:NC_TOK], ALU.add).then_inc(s_h, 1)
                    return
                hi, lo = halves
                kn = KT // parts
                for k0 in range(0, KT, kn):
                    k = slice(k0, k0 + kn)
                    link(dve.tensor_tensor(h[:, k, :], h[:, k, :], bc(row[:, 0, :], 1, [P, kn, T]), ALU.mult))
                    between(parts)
                    for t in range(k0, k0 + kn):
                        dve.tensor_scalar(h[:, t, 0:TP], h[:, t, 0:TP], shift(l, sh)[:, t, 0:1], None, ALU.add)
                    link(dve.tensor_tensor(h[:, k, TP:T], h[:, k, TP:T], shift(l, sh)[:, k, 1:NC_TOK], ALU.add))
                    between(parts)
                    link(dve.tensor_copy(hi[:, k, :], h[:, k, :]))
                    between(parts)
                    dve.tensor_tensor(lo[:, k, :], h[:, k, :], hi[:, k, :].bitcast(fp32), ALU.subtract).then_inc(s_h, kn)
                    if parts > 1 and k0 + kn in (KT // 2, KT):
                        split_low(SPLIT_SLOTS[low[0]] + 1)

            def between(parts):
                if parts == 1:
                    split_low(SPLIT_SLOTS[low[0]] + 1)

            def residual(name, l, part, t):
                ps = await_use(dve, name)
                gate = shift(l, part)
                dve.scalar_tensor_tensor(x[:, t, 0:TP], ps[:, 0:TP], gate[:, t, 0:1], x[:, t, 0:TP], ALU.mult, ALU.add)
                freed(dve.tensor_tensor(small[:, t * TS:(t + 1) * TS], ps[:, TP:T], gate[:, t, 1:NC_TOK], ALU.mult), name)

            def residual_samples(signal):
                dve.wait_ge(psum_read[last_use[0] % BANKS], last_use[0] // BANKS + 1)
                dve.tensor_tensor(x[:, :, TP:T], x[:, :, TP:T], small[:, :].rearrange("p (k b) -> p k b", b=TS), ALU.add)\
                    .then_inc(signal, 1)

            last_use = [0]
            taps = [0]
            dve.wait_ge(s_cact, 1)
            dve.wait_ge(s_const, 1)
            link(dve.tensor_copy(c_halves[:, :, 0:NC_TOK], cT[:, :, :]))
            dve.tensor_tensor(c_halves[:, :, NC_TOK:2 * NC_TOK], cT[:, :, :], c_halves[:, :, 0:NC_TOK].bitcast(fp32), ALU.subtract)
            dve.tensor_tensor(fold[:, :], ident[:, 0:NC_TOK], ident[:, NC_TOK:2 * NC_TOK], ALU.add)
            done(s_chalf)
            modulation(0, 0)
            for l in range(LAYERS):
                if l == 0:
                    split_low(SPLIT_AT["fqi", 0] + 1)
                    dve.wait_ge(s_const, 2)
                modulated_norm(l, par_of("n1", l), 0, 1, 3 * l + 1, (H_HI, H1_LO), 4 if l == 0 else 1)
                if l == 1:
                    modulation(1, 2)
                for t in range(KT):
                    name = ("f", l, t)
                    split_low(fqi_until(l, "f", t))
                    dve.wait_ge(psum_read[USE[name] % BANKS], USE[name] // BANKS + 1)
                    dve.tensor_scalar(F[:, t, :], F[:, t, :], lbt[:, 1, l, t:t + 1], lbt[:, 0, l, t:t + 1], ALU.mult, ALU.add)
                    ins = dve.tensor_scalar(K[:, t, :], K[:, t, :], lbt[:, 1, l, t:t + 1], None, ALU.mult)
                link(ins)
                link(dve.tensor_scalar(F, F, 2.0 ** -63, None, ALU.max))
                dve.tensor_copy(fs[:, :, :], F[:, :, TP:T]).then_inc(s_fg, 1)
                split_low(fqi_until(l, "q", 3))
                dve.wait_ge(s_ln, l + 1)
                for hd in range(HEADS):
                    if hd == HEADS // 2:
                        split_low(fqi_until(l, "q", 4))
                    for c in range(NCH):
                        tok = slice(c * CH, (c + 1) * CH)
                        ins = dve.tensor_tensor_scan(B[:, hd, tok], ones[:, :], B[:, hd, tok], 0.0, ALU.mult, ALU.add)
                link(ins)

                def level_exponents(n):
                    m = SPANS[n - 1]
                    first, second = levels_view(B, m)
                    d1, d2 = levels_view(as_kt(DEC), m)
                    nb = TP // (2 * m)
                    ref = first[:, :, :, m - 1:m].broadcast_to([P, HEADS, nb, m])
                    dve.tensor_tensor(d1, ref, first, ALU.subtract)
                    dve.tensor_tensor(d2, second, ref, ALU.subtract).then_inc(s_dif, 1)

                def level_operands(n):
                    m = SPANS[n - 1]
                    d1, d2 = levels_view(as_kt(DEC), m)
                    k1 = levels_view(K, m)[0]
                    q2 = levels_view(Q, m)[1]
                    x1, x2 = levels_view(as_kt(Xb[n % 2]), m)
                    if n >= 3:
                        dve.wait_ge(psum_full, USE[("att", l, n - 2, 3)] + 1)
                    dve.wait_ge(s_exp, 8 * l + n)
                    dve.tensor_tensor(x1, d1, k1, ALU.mult)
                    dve.tensor_tensor(x2, d2, q2, ALU.mult).then_inc(s_xl, 1)
                    dve.wait_ge(s_xl, 7 * l + n)

                split_low(fqi_until(l, "q", 6))
                level_exponents(1)
                split_low(fqi_until(l, "i", 0))
                dve.wait_ge(s_qv, l + 1)
                split_low(fqi_until(l, "i", KT - 1))
                level_operands(1)
                dve.wait_ge(s_att0, l + 1)
                cw = par_of("cw", l).rearrange("p (k j) -> p k j", j=CW)

                def conv_taps(l=l, cw=cw):
                    for j in range(CW):
                        for t in DVE_CONV:
                            win, acc = ubuf[:, t, j:j + TP], SBZ[:, t, 0:TP]
                            if j == 0:
                                ins = dve.tensor_scalar(acc, win, cw[:, t, 0:1], par_of("cb", l)[:, t:t + 1], ALU.mult, ALU.add)
                            else:
                                dve.wait_ge(s_conv, taps[0] - len(DVE_CONV) + 1)
                                ins = dve.scalar_tensor_tensor(acc, win, cw[:, t, j:j + 1], acc, ALU.mult, ALU.add)
                            ins.then_inc(s_conv, 1)
                            taps[0] += 1
                            yield

                conv = conv_taps()

                def levels(n, l=l):
                    if 1 <= n < 7:
                        level_exponents(n + 1)
                    for b in range(4):
                        name = ("att", l, n, b)
                        ps = await_use(dve, name)
                        if n > 0:
                            own_read(("att", l, n - 1, b))
                        ins = dve.copy_predicated(attb[:, 4 * b:4 * b + 4, :], bc(masks[:, n, :], 1, [P, 4, P]),
                                                  ps[:, :].rearrange("p (a n) -> p a n", a=4))
                        freed(ins, name)
                    if 1 <= n < 7:
                        level_operands(n + 1)
                    if n == 7:
                        bv = B[:, :, 0:TP].rearrange("p h (c n) -> p h c n", n=CH)
                        dve.tensor_tensor(as_kt(DEC)[:, :, 0:TP].rearrange("p h (c n) -> p h c n", n=CH),
                                          bv[:, :, :, CH - 1:CH].broadcast_to([P, HEADS, NCH, CH]), bv, ALU.subtract)\
                            .then_inc(s_dif, 1)
                        done(s_att)

                def decayed(l=l):
                    dve.wait_ge(s_exp, 8 * l + 8)
                    dve.tensor_tensor(as_kt(X0)[:, :, 0:TP], as_kt(DEC)[:, :, 0:TP], K[:, :, 0:TP], ALU.mult).then_inc(s_kq, 1)
                    dve.wait_ge(s_eb, l + 1)
                    dve.tensor_tensor(Q[:, :, CH:TP], Q[:, :, CH:TP], B[:, :, CH:TP], ALU.mult).then_inc(s_kq, 1)

                def final_state(l=l):
                    for b in range(2):
                        name = ("s1", l, b)
                        ps = await_use(dve, name)
                        for s in range(4):
                            hd = 4 * b + s
                            ins = dve.scalar_tensor_tensor(s0b[:, hd, :], s0b[:, hd, :], ebl[:, hd, 1:2],
                                                           ps[:, s * P:(s + 1) * P], ALU.mult, ALU.add)
                        freed(ins, name)
                    done(s_s1)

                def sample_state(hd, l=l):
                    st = STB[hd % 2]
                    dve.wait_ge(s_state[hd % 2], 16 * ((HEADS * l + hd) // 2 + 1))
                    for half in range(2):
                        name = ("kv", l, hd, half)
                        ps = await_use(dve, name)
                        for b4 in range(4):
                            b = 4 * half + b4
                            ins = dve.scalar_tensor_tensor(st[:, b * P:(b + 1) * P], st[:, b * P:(b + 1) * P],
                                                           fs[:, hd, b:b + 1], ps[:, b4 * P:(b4 + 1) * P], ALU.mult, ALU.add)
                        freed(ins, name)
                    done(s_sn)

                stages = {"att": levels, "vt": decayed, "s1": final_state, "kv": sample_state}
                for r, (g, t) in enumerate(REST):
                    if g == "za":
                        name = ("za", l, t)
                        ps = await_use(dve, name)
                        dve.wait_ge(s_zb, KT * l + t + 1)
                        dve.tensor_tensor(ubuf[:, t, PAST:PAST + TP], ps[:, 0:TP], SBZ[:, t, 0:TP], ALU.mult)
                        ins = dve.tensor_tensor(us[:, t, :], ps[:, TP:T], SBZ[:, t, TP:T], ALU.mult)
                        freed(ins, name)
                        if t == KT - 1:
                            done(s_glu)
                    for stage in STAGES.get(r, ()):
                        if stage[0] in stages:
                            stages[stage[0]](*stage[1:])
                    if r >= 2 * KT:
                        for _ in range(3 if r < 24 else 7):
                            next(conv, None)
                dve.wait_ge(s_sgr, l + 1)
                for _ in range(20):
                    next(conv, None)
                dve.wait_ge(s_hn, l + 1)
                link(dve.tensor_tensor(V, V, as_kt(X0), ALU.mult))
                for hd in range(HEADS):
                    ins = dve.scalar_tensor_tensor(V[:, hd, :], V[:, hd, :], par_of("hgn", l)[:, hd:hd + 1], SG[:, hd, :],
                                                   ALU.mult, ALU.mult)
                ins.then_inc(s_on, 1)
                modulation(l, 1, lambda: [next(conv, None) for _ in range(16)])
                for t in range(KT):
                    if t == 1:
                        dve.wait_ge(s_cs, l + 1)
                        link(dve.tensor_reduce(small[:, :], sconv[:, :, :, :].rearrange("p k b j -> p (k b) j"), AX, ALU.add))
                        sm = small[:, :].rearrange("p (k b) -> p k b", b=TS)
                        link(dve.tensor_tensor(us[:, :, :], us[:, :, :], cw[:, :, CW - 1:CW].broadcast_to([P, KT, TS]), ALU.mult))
                        link(dve.tensor_tensor(us[:, :, :], us[:, :, :], sm, ALU.add))
                        dve.tensor_tensor(SBZ[:, :, TP:T], us[:, :, :], bc(par_of("cb", l), 2, [P, KT, TS]), ALU.add)
                    if t == MU_AFTER:
                        for _ in conv:
                            pass
                        dve.wait_ge(s_pconv, (l + 1) * CW * len(POOL_CONV))
                        done(s_cv)
                    for _ in range(9):
                        next(conv, None)
                    name = ("ya", l, t)
                    ps = await_use(dve, name)
                    freed(dve.tensor_tensor(GA[:, t, :], ps[:, 0:T], GA[:, t, :], ALU.mult), name)
                    if t == MU_AFTER:
                        dve.wait_ge(s_mu, l + 1)
                        dve.tensor_tensor(SBZ, SBZ, bc(row[:, 0, :], 1, [P, KT, T]), ALU.subtract).then_inc(s_xc, 1)
                    if t == VAR_AFTER:
                        dve.wait_ge(s_rstd, 3 * l + 2)
                        dve.tensor_tensor(SBZ, SBZ, bc(row[:, 1, :], 1, [P, KT, T]), ALU.mult).then_inc(s_lnn, 1)
                for t in range(KT):
                    name = ("yb", l, t)
                    ps = await_use(dve, name)
                    freed(dve.tensor_tensor(GB[:, t, :], ps[:, 0:T], GB[:, t, :], ALU.mult), name)
                    if t % 4 == 3:
                        own_read(name)
                        ins = dve.tensor_tensor(GA[:, t - 3:t + 1, :], GA[:, t - 3:t + 1, :], GB[:, t - 3:t + 1, :], ALU.add)
                ins.then_inc(s_mix, 1)
                for t in range(KT):
                    if l == 0 and t % 2 == 1:
                        split_low(SPLIT0 + t // 2)
                    residual(("wo", l, t), l, 2, t)
                last_use[0] = USE[("wo", l, KT - 1)]
                residual_samples(s_x)
                dve.wait_ge(s_x, 2 * l + 1)
                if l == LAYERS - 1:
                    dve.sem_inc(m_split, RING)
                if l == 0:
                    modulation(0, 2)
                modulated_norm(l, par_of("n2", l), 3, 4, 3 * l + 3, (H_HI, h_lo) if l == 0 else None)
                if l == 0:
                    modulation(1, 0)
                    for j in range(FT):
                        split_low(SPLIT_AT["ffn"] + j + HI_RING - 1)
                        ps = await_use(dve, ("fu", j))
                        dve.wait_ge(s_gsilu, j + 1)
                        freed(dve.tensor_tensor(HNEW, ps[:, 0:T], SILU[j % 2], ALU.mult), ("fu", j))
                        own_read(("fu", j))
                        link(dve.tensor_copy(HID_HI[:, j, :], HNEW))
                        dve.tensor_tensor(HID_LO[:, j, :], HNEW, HID_HI[:, j, :].bitcast(fp32), ALU.subtract).then_inc(s_hid, 1)
                        dve.wait_ge(s_hid, j + 1)
                    for t in range(KT):
                        split_low(SPLIT_AT["down"] + ((t + 1) * FT - 1) // SLOT_BLOCKS + HI_RING - 1)
                        residual(("fd", t), 0, 5, t)
                    last_use[0] = USE[("fd", KT - 1)]
                    residual_samples(s_x)
                    dve.wait_ge(s_x, 2)

            for n in range(AHEAD):
                expert_low(0, n)

            dve.wait_ge(s_tok, 1)
            for tt in range(3):
                link(dve.memset(rt[:, tt, :], 0.0))
            ps = await_use(dve, ("lg",))
            dve.tensor_copy(rt[:, 0:2, 0:NE], ps[:, 0:2 * NE].rearrange("p (a n) -> p a n", a=2))
            freed(dve.tensor_copy(rt[0:TS, 2, 0:NE], ps[0:TS, 2 * NE:3 * NE]), ("lg",))
            link(dve.memset(FACC[:, :, :], 0.0))
            for tt in range(3):
                link(dve.max(rt[:, tt, 24:32], rt[:, tt, 0:NE]))
                link(dve.max_index(rt[:, tt, 56:64].bitcast(u32), rt[:, tt, 24:32], rt[:, tt, 0:NE]))
            link(dve.tensor_copy(rt[:, :, 32:34], rt[:, :, 56:58].bitcast(u32)))
            dve.tensor_tensor(rt[:, :, 36:37], rt[:, :, 25:26], rt[:, :, 24:25], ALU.subtract).then_inc(s_lg, 1)
            dve.wait_ge(s_rex, 1)
            link(dve.tensor_scalar(rt[:, :, 34:35], rt[:, :, 36:37], 1.0, None, ALU.add))
            link(dve.reciprocal(rt[:, :, 34:35], rt[:, :, 34:35]))
            link(dve.tensor_tensor(rt[:, :, 35:36], rt[:, :, 36:37], rt[:, :, 34:35], ALU.mult))
            dve.wait_ge(s_const, 3)
            for tt in range(3):
                dve.tensor_scalar(rt[:, tt, 40:48], IOTA[:, 0:NE], rt[:, tt, 32:33], None, ALU.is_equal)
                dve.tensor_scalar(rt[:, tt, 48:56], IOTA[:, 0:NE], rt[:, tt, 33:34], None, ALU.is_equal)
                dve.tensor_scalar(rt[:, tt, 64:72], IOTA[:, 0:NE], rt[:, tt, 32:33], rt[:, tt, 34:35], ALU.is_equal, ALU.mult)
                dve.tensor_scalar(rt[:, tt, 72:80], IOTA[:, 0:NE], rt[:, tt, 33:34], rt[:, tt, 35:36], ALU.is_equal, ALU.mult)
            link(dve.memset(scratch[:, :], 0.0))
            dve.tensor_tensor(rt[:, :, 16:24], rt[:, :, 64:72], rt[:, :, 72:80], ALU.add)
            dve.tensor_tensor(rt[:, :, 8:16], rt[:, :, 40:48], rt[:, :, 48:56], ALU.add).then_inc(s_sel, 1)
            dve.wait_ge(s_sel, 1)
            ps = await_use(dve, ("pos",))
            link(dve.tensor_scalar(rt[:, :, 40:48], rt[:, :, 8:16], -4096.0, 4096.0, ALU.mult, ALU.add))
            link(dve.memset(PSEL[:, :, :, :], 0.0))
            for tt, (_, tn) in enumerate(TT):
                dve.tensor_tensor(PSEL[0:tn, 0, 0:NE, tt], rt[0:tn, tt, 40:48], ps[0:tn, tt * NE:(tt + 1) * NE], ALU.add)
                for rnd in range(ROUNDS):
                    dve.tensor_copy(PSEL[0:tn, 1, rnd * NE:(rnd + 1) * NE, tt], rt[0:tn, tt, 16:24])
            freed(dve.tensor_reduce(small[0:1, 0:1], ps[0:1, 3 * NE:4 * NE], AX, ALU.max), ("pos",))
            link(dve.memset(scratch[:, :], 0.0))
            for rnd in range(1, ROUNDS):
                dve.tensor_scalar(PSEL[:, 0, rnd * NE:(rnd + 1) * NE, :], PSEL[:, 0, 0:NE, :], float(-CAP * rnd), None, ALU.add)
            link(dve.tensor_scalar(small[0:1, 2:3], small[0:1, 0:1], float(CAP), None, ALU.is_gt))
            link(dve.tensor_copy(flag[0:1, 0:1], small[0:1, 2:3]))
            dve.sem_inc(s_flag, 2)

            def select(e, at, wait):
                wait(dve.tensor_copy(CUR[:, :, e, :], PSEL[:, :, at, :]))
                for tt in range(3):
                    dve.tensor_scalar(SEL[e][:, tt, :], IOTA[:, :], CUR[:, 0, e, tt:tt + 1], None, ALU.is_equal)
                    dve.tensor_scalar(SELC[e][:, tt, :], IOTA[:, :], CUR[:, 0, e, tt:tt + 1], CUR[:, 1, e, tt:tt + 1],
                                      ALU.is_equal, ALU.mult)
                wait(dve.memset(scratch[:, :], 0.0))
                dve.sem_inc(m_sel, 1)

            def moe_full(turn, n):
                dve.wait_ge(psum_full, turn * (GROUP * MOE_USES) + MOE_USE0 + n + 1)
                return banks[(MOE_USE0 + n) % BANKS]

            def moe_freed(ins, n):
                ins.then_inc(psum_read[(MOE_USE0 + n) % BANKS], 1)

            def gathered(turn, n, count):
                for g, (k0, kn) in enumerate(((0, 3), (3, 3), (6, 2))):
                    ps = moe_full(turn, n + g)
                    dve.wait_ge(m_tok, count + g + 1)
                    moe_freed(dve.tensor_tensor(tok_lo[:, k0:k0 + kn, :], ps[:, 0:kn * P].rearrange("p (a n) -> p a n", a=kn),
                                                tok_hi[:, k0:k0 + kn, :].bitcast(fp32), ALU.subtract), n + g)

            def expert(turn, s):
                use = 4 + s * MOE_USES
                slot = s * MOE_SLOTS + AHEAD
                own = [s * DVE_STEPS]

                def wait(ins):
                    own[0] += 1
                    ins.then_inc(m_dve, 1)
                    dve.wait_ge(m_dve, turn * (GROUP * DVE_STEPS) + 2 + own[0])

                def hidden(c):
                    n = use + (0 if c == 0 else 2 * c - 1)
                    ps = moe_full(turn, n)
                    dve.wait_ge(m_silu, (GROUP * turn + s) * CHUNKS + c + 1)
                    moe_freed(dve.tensor_tensor(HTOK[:, c % 2, :], ps[:, 256:512], MSILU[:, c % 2, :], ALU.mult), n)

                def hidden_low(c):
                    n = use + 2 * c + (2 if c < CHUNKS - 1 else 1)
                    ps = moe_full(turn, n)
                    dve.wait_ge(m_hid, (GROUP * turn + s) * CHUNKS + c + 1)
                    moe_freed(dve.tensor_tensor(hid_lo[:, 2 * c:2 * c + 2, :], ps[:, 0:256].rearrange("p (a n) -> p a n", a=2),
                                                hid_hi[:, 2 * c:2 * c + 2, :].bitcast(fp32), ALU.subtract), n)

                for c in range(CHUNKS):
                    expert_low(turn, slot + 2 * c)
                    expert_low(turn, slot + 2 * c + 1)
                    hidden(c)
                    if c >= 1:
                        hidden_low(c - 1)
                expert_low(turn, slot + 2 * CHUNKS)
                hidden_low(CHUNKS - 1)
                for n in range(2 * CHUNKS + 1, MOE_SLOTS):
                    expert_low(turn, slot + n)
                    if n == 2 * CHUNKS + 4:
                        select((s + 1) % 2, bass.ds(turn * GROUP + s + 1, 1), wait)
                down = use + 2 * CHUNKS
                gathered(turn, down + 2, (GROUP * turn + s + 1) * 3)
                for t in range(KT):
                    n = down + 6 + t
                    ps = moe_full(turn, n)
                    moe_freed(dve.tensor_tensor(FACC[:, t, :], FACC[:, t, :], ps[:, 0:T], ALU.add), n)
                own[0] = (s + 1) * DVE_STEPS - 1
                wait(dve.memset(scratch[:, :], 0.0))

            def first(ins):
                steps_first[0] += 1
                ins.then_inc(m_dve, 1)
                dve.wait_ge(m_dve, steps_first[0])

            steps_first = [0]
            select(0, slice(0, 1), first)
            gathered(0, 0, 0)
            with dve.Fori(0, GROUPS) as group:
                for s in range(GROUP):
                    expert(group, s)
            more = dve.value_load(flag[0:1, 0:1], min_val=0, max_val=1)
            with dve.If(more > 0):
                with dve.Fori(1, ROUNDS) as rnd:
                    with dve.Fori(0, GROUPS) as group:
                        for s in range(GROUP):
                            expert(rnd * GROUPS + group, s)
            fsteps = [0]

            def flink(ins):
                fsteps[0] += 1
                ins.then_inc(f_dve, 1)
                dve.wait_ge(f_dve, fsteps[0])

            flink(dve.memset(scratch[:, :], 0.0))
            flink(dve.tensor_tensor(FACC[:, :, TP:T], FACC[:, :, TP:T], shift(1, 5)[:, :, 1:NC_TOK], ALU.mult))
            dve.tensor_tensor(x[:, :, TP:T], x[:, :, TP:T], FACC[:, :, TP:T], ALU.add)
            for t in range(KT):
                dve.scalar_tensor_tensor(x[:, t, 0:TP], FACC[:, t, 0:TP], shift(1, 5)[:, t, 0:1], x[:, t, 0:TP], ALU.mult, ALU.add)\
                    .then_inc(f_x, 1)
            dve.wait_ge(f_rt, 2)
            for t in range(KT):
                dve.scalar_tensor_tensor(fin[:, t, :], x[:, t, :], par_of("fin")[:, t:t + 1], row[:, 0, :], ALU.mult, ALU.mult)\
                    .then_inc(f_y, 1)


def kernel(**inputs):
    import numpy as np
    import concourse.bacc as bacc
    from concourse.bass_utils import run_bass_kernel_spmd

    f32 = np.float32
    a = {k: np.asarray(v) for k, v in inputs.items()}

    def tiles(v):
        v = v.reshape(v.shape[:-1] + (v.shape[-1] // P, P))
        return np.moveaxis(v, -1, 0)

    def fmajor(v):
        return np.ascontiguousarray(v.reshape(v.shape[0], KT, P).transpose(2, 1, 0))

    def col_tiles(w, ts=None):
        k, n = w.shape
        v = w.reshape(k // P, P, n // P, P).transpose(2, 0, 1, 3)
        return v if ts is None else v[ts]

    def slots(blocks):
        return blocks.reshape(-1, SLOT_BLOCKS, P, P).transpose(0, 2, 1, 3).reshape(-1, P, SLOT_W)

    flat = lambda v: v.reshape(-1, P, P)

    def ada(l, pair):
        w = a["ada_w"][l][:, 2048 * pair:2048 * (pair + 1)].reshape(KT, P, 4, 4, P)
        return flat(w.transpose(2, 0, 3, 1, 4))

    def ffn_up(g, u):
        return flat(np.stack([col_tiles(g), col_tiles(u)], axis=1))

    seq = [ada(0, 0)]
    cols = {"q": 0, "f": 1, "i": 2, "g": 3, "za": 4, "zb": 5, "ga": 6, "gb": 7}
    for l in range(LAYERS):
        if l == 1:
            seq.append(ada(1, 2))
        for g in ("f", "q", "i", "zb", "za", "g", "ga", "gb"):
            seq.append(flat(col_tiles(a["w_in"][l][:, cols[g] * D:(cols[g] + 1) * D])))
        seq.append(ada(l, 1))
        seq += [flat(col_tiles(a[n][l])) for n in ("w_hg_out", "w_conv_out", "w_o")]
        if l == 0:
            seq += [ada(0, 2), ada(1, 0), ffn_up(a["ffn_w_gate"][0], a["ffn_w_up"][0]),
                    flat(col_tiles(a["ffn_w_down"][0]))]
    stream = slots(np.concatenate(seq))
    moe = []
    for e in range(NE):
        gate, up = (a[n][0, e].reshape(KT, P, CHUNKS, 2, P) for n in ("moe_w_gate", "moe_w_up"))
        chunks = np.concatenate([gate, up], axis=3).transpose(2, 0, 3, 1, 4)
        down = a["moe_w_down"][0, e].reshape(FT, P, KT, P).transpose(0, 2, 1, 3)
        moe.append(slots(np.concatenate([flat(chunks), flat(down)])))
    moe = np.concatenate(moe + [moe[0][0:LOADED]])
    cw = a["conv_w"].reshape(LAYERS, CW, KT, P).transpose(3, 0, 2, 1)
    par = np.concatenate([v.reshape(P, -1) for v in (
        tiles(a["ada_b"]), tiles(a["norm1_g"]), tiles(a["norm2_g"]), tiles(a["lb_logits"]), tiles(a["hg_norm_g"]),
        tiles(a["conv_b"]), tiles(a["conv_ln_g"]), tiles(a["conv_ln_b"]), cw, tiles(a["final_norm_g"]),
        a["router_w"][0].reshape(KT, P, NE).transpose(1, 0, 2))], axis=1)
    arrays = {
        "x": fmajor(np.concatenate([a["x_prompt"][0], a["x_sample"][:, 0]])),
        "c": fmajor(np.concatenate([a["c_prompt"], a["c_sample"]])),
        "par": par, "stream": stream, "moe": moe,
        "state_h": a["state_hgrn"].transpose(0, 2, 3, 1, 4),
        "state_c": a["state_conv"].reshape(LAYERS, TS, PAST, KT, P).transpose(0, 4, 3, 1, 2),
    }
    outs = {"y": (P, KT, T), "hp": (LAYERS, P, HEADS, P), "cp": (LAYERS, P, KT, PAST),
            "hs": (LAYERS, HEADS, P, TS, P), "cs": (LAYERS, P, KT, TS, PAST)}
    nc = bacc.Bacc("TRN2", target_bir_lowering=False, num_devices=1)
    arrays = {"in_" + k: np.ascontiguousarray(v) for k, v in arrays.items()}
    ins = [nc.dram_tensor(k, v.shape, mybir.dt.from_np(v.dtype), kind="ExternalInput").ap() for k, v in arrays.items()]
    o = [nc.dram_tensor("out_" + k, v, mybir.dt.float32, kind="ExternalOutput").ap() for k, v in outs.items()]
    trunk_kernel(nc, *ins, *o)
    r = run_bass_kernel_spmd(nc, [arrays], core_ids=[0]).results[0]
    y = r["out_y"].transpose(2, 1, 0).reshape(T, D)
    hp = r["out_hp"].transpose(0, 2, 1, 3)[:, None]
    cp = r["out_cp"].transpose(0, 3, 2, 1).reshape(LAYERS, PAST, D)[:, None]
    hs = r["out_hs"].transpose(0, 3, 1, 2, 4)
    cs = r["out_cs"].transpose(0, 3, 4, 2, 1).reshape(LAYERS, TS, PAST, D)
    return (y[None, 0:TP], y[TP:T, None], hp, cp, hs, cs)
```
